# Optimizing a Trainium2 kernel written in Bass

```python
import jax, jax.numpy as jnp
from jax import lax
import numpy as np

D_MODEL = 1024
BATCH = 1
SEQ = 1024
DEPTH = 2
DEC_BATCH = 8
DEC_SEQ = 8
PAST_LEN = 1024
PAGE_SIZE = 128

H_A = 4
DH_A = D_MODEL // 8
W_A = H_A * DH_A
CHUNK_A = 64
DH = 64
ROT_DIM = DH // 4
ROPE_THETA = 500000.0
BLK = 128
DIL_WINDOWS = (128, 512, 2048)
DIL_RATES = (1, 4, 16)
N_DIL = 3
H_B = D_MODEL // (2 * DH)
W_B = H_B * DH
H_C = D_MODEL // DH
KV_C = 2
WIN_C = 128
D_FF = 4 * D_MODEL
N_AB = (DEPTH + 1) // 2
N_C = DEPTH // 2
ALPHA = (2.0 * DEPTH) ** 0.25
BETA = (8.0 * DEPTH) ** -0.25
LN_EPS = 1e-5
IN_AB = 4 * W_A + 2 * H_A + 3 * N_DIL * W_B
OUT_AB = W_A + W_B
IN_C = (H_C + 2 * KV_C) * DH
OUT_C = H_C * DH

kernel_name = 'hybrid_mlstm_dilated_swa_decoder_step'

def layer_norm(x, g, b):
    xf = x.astype(jnp.float32)
    mu = jnp.mean(xf, axis=-1, keepdims=True)
    var = jnp.mean(jnp.square(xf - mu), axis=-1, keepdims=True)
    y = (xf - mu) * lax.rsqrt(var + LN_EPS) * g.astype(jnp.float32) + b.astype(jnp.float32)
    return y.astype(x.dtype)

def sq_relu_mlp(x, w_up, w_down):
    return jnp.square(jax.nn.relu(x @ w_up)) @ w_down

def rope(x, pos):
    half = ROT_DIM // 2
    inv = ROPE_THETA ** (-jnp.arange(half, dtype=jnp.float32) / half)
    ang = pos.astype(jnp.float32)[:, None] * inv[None, :]
    cos = jnp.cos(ang)[:, None, :]
    sin = jnp.sin(ang)[:, None, :]
    x1 = x[..., :half].astype(jnp.float32)
    x2 = x[..., half:ROT_DIM].astype(jnp.float32)
    rot = jnp.concatenate([x1 * cos - x2 * sin, x2 * cos + x1 * sin], axis=-1).astype(x.dtype)
    return jnp.concatenate([rot, x[..., ROT_DIM:]], axis=-1)

def banded_attention(q, k, v, max_dist, sinks=None):
    n, length, hq, dh = q.shape
    hk = k.shape[2]
    grp = hq // hk
    lp = -(-length // BLK) * BLK
    pad = ((0, 0), (0, lp - length), (0, 0), (0, 0))
    q, k, v = jnp.pad(q, pad), jnp.pad(k, pad), jnp.pad(v, pad)
    nb = lp // BLK
    qb = q.reshape(n, nb, BLK, hk, grp, dh)
    kb = k.reshape(n, nb, BLK, hk, dh)
    vb = v.reshape(n, nb, BLK, hk, dh)
    shift = ((0, 0), (1, 0), (0, 0), (0, 0), (0, 0))
    kk = jnp.concatenate([jnp.pad(kb, shift)[:, :-1], kb], axis=2)
    vv = jnp.concatenate([jnp.pad(vb, shift)[:, :-1], vb], axis=2)
    s = jnp.einsum('nbqhgd,nbkhd->nbhgqk', qb, kk, preferred_element_type=jnp.float32) * (dh ** -0.5)
    qi = jnp.arange(BLK)[:, None] + BLK
    ki = jnp.arange(2 * BLK)[None, :]
    dist = qi - ki
    band = (dist >= 0) & (dist <= max_dist)
    mask = band[None] & ((jnp.arange(nb)[:, None, None] > 0) | (ki[None] >= BLK))
    s = jnp.where(mask[None, :, None, None], s, -jnp.inf)
    m = jnp.max(s, axis=-1)
    if sinks is not None:
        sk = sinks.astype(jnp.float32).reshape(hk, grp)[None, None, :, :, None]
        m = jnp.maximum(m, sk)
    p = jnp.exp(s - m[..., None])
    den = jnp.sum(p, axis=-1)
    if sinks is not None:
        den = den + jnp.exp(sk - m)
    o = jnp.einsum('nbhgqk,nbkhd->nbqhgd', p, vv.astype(jnp.float32))
    o = o / jnp.transpose(den, (0, 1, 4, 2, 3))[..., None]
    o = o.reshape(n, lp, hq, dh)[:, :length].astype(q.dtype)
    lse = jnp.transpose(m + jnp.log(den), (0, 1, 4, 2, 3)).reshape(n, lp, hq)[:, :length]
    return o, lse

def dilated_prompt(q, k, v, rate, span):
    bn, s_len, h, dh = q.shape
    sp = -(-s_len // rate) * rate
    length = sp // rate

    def to_strided(t):
        t = jnp.pad(t, ((0, 0), (0, sp - s_len), (0, 0), (0, 0)))
        return jnp.transpose(t.reshape(bn, length, rate, h, dh), (0, 2, 1, 3, 4)).reshape(bn * rate, length, h, dh)

    o, lse = banded_attention(to_strided(q), to_strided(k), to_strided(v), span)
    o = jnp.transpose(o.reshape(bn, rate, length, h, dh), (0, 2, 1, 3, 4)).reshape(bn, sp, h, dh)[:, :s_len]
    lse = jnp.transpose(lse.reshape(bn, rate, length, h), (0, 2, 1, 3)).reshape(bn, sp, h)[:, :s_len]
    return o, lse

def dilated_sample(q, k_all, v_all, rate, span, n_past):
    t_len = q.shape[1]
    idx = n_past + jnp.arange(t_len)[:, None] - rate * jnp.arange(span + 1)[None, :]
    valid = idx >= 0
    idx = jnp.maximum(idx, 0)
    kg = k_all[:, idx]
    vg = v_all[:, idx]
    s = jnp.einsum('bthd,btmhd->bthm', q, kg, preferred_element_type=jnp.float32) * (q.shape[-1] ** -0.5)
    s = jnp.where(valid[None, :, None, :], s, -jnp.inf)
    m = jnp.max(s, axis=-1)
    p = jnp.exp(s - m[..., None])
    den = jnp.sum(p, axis=-1)
    o = jnp.einsum('bthm,btmhd->bthd', p, vg.astype(jnp.float32)) / den[..., None]
    return o.astype(q.dtype), m + jnp.log(den)

def swa_sample(q, k_all, v_all, sinks, n_past):
    bd, t_len, hq, dh = q.shape
    hk = k_all.shape[2]
    grp = hq // hk
    qg = q.reshape(bd, t_len, hk, grp, dh)
    s = jnp.einsum('bthgd,bshd->bhgts', qg, k_all, preferred_element_type=jnp.float32) * (dh ** -0.5)
    dist = (n_past + jnp.arange(t_len))[:, None] - jnp.arange(n_past + t_len)[None, :]
    mask = (dist >= 0) & (dist < WIN_C)
    s = jnp.where(mask, s, -jnp.inf)
    sk = sinks.astype(jnp.float32).reshape(hk, grp)[None, :, :, None]
    m = jnp.maximum(jnp.max(s, axis=-1), sk)
    p = jnp.exp(s - m[..., None])
    den = jnp.sum(p, axis=-1) + jnp.exp(sk - m)
    o = jnp.einsum('bhgts,bshd->bthgd', p, v_all.astype(jnp.float32))
    o = o / jnp.transpose(den, (0, 3, 1, 2))[..., None]
    return o.reshape(bd, t_len, hq, dh).astype(q.dtype)

def mlstm_chunk(carry, xs):
    c_prev, n_prev, m_prev = carry
    q, k, v, logi, logf = xs
    q = q.astype(jnp.float32)
    k = k.astype(jnp.float32)
    v = v.astype(jnp.float32)
    length = q.shape[2]
    b = jnp.cumsum(logf, axis=-1)
    a = b + m_prev[..., None]
    causal = jnp.tril(jnp.ones((length, length), dtype=bool))
    dmat = jnp.where(causal, b[..., :, None] - b[..., None, :] + logi[..., None, :], -jnp.inf)
    mt = jnp.maximum(a, jnp.max(dmat, axis=-1))
    wts = jnp.exp(dmat - mt[..., None])
    inter = jnp.exp(a - mt)
    sqk = jnp.einsum('bhtd,bhsd->bhts', q, k) * wts
    num = inter[..., None] * jnp.einsum('bhtd,bhde->bhte', q, c_prev) + jnp.einsum('bhts,bhse->bhte', sqk, v)
    nq = inter * jnp.einsum('bhtd,bhd->bht', q, n_prev) + jnp.sum(sqk, axis=-1)
    h = num / jnp.maximum(jnp.abs(nq), jnp.exp(-mt))[..., None]
    w_last = wts[..., -1, :]
    c_new = inter[..., -1, None, None] * c_prev + jnp.einsum('bhs,bhsd,bhse->bhde', w_last, k, v)
    n_new = inter[..., -1, None] * n_prev + jnp.einsum('bhs,bhsd->bhd', w_last, k)
    return (c_new, n_new, mt[..., -1]), h

def mlstm_prompt(q, k, v, logi, logf):
    bn, s_len, h, d = q.shape
    nc = s_len // CHUNK_A

    def split_chunks(t):
        t = t.reshape((bn, nc, CHUNK_A) + t.shape[2:])
        return jnp.moveaxis(jnp.moveaxis(t, 1, 0), 3, 2)

    init = (jnp.zeros((bn, h, d, d), jnp.float32), jnp.zeros((bn, h, d), jnp.float32), jnp.zeros((bn, h), jnp.float32))
    xs = (split_chunks(q), split_chunks(k), split_chunks(v), split_chunks(logi), split_chunks(logf))
    final, hs = lax.scan(mlstm_chunk, init, xs)
    hs = jnp.transpose(hs, (1, 0, 3, 2, 4)).reshape(bn, s_len, h, d)
    return hs, final

def mlstm_sample(q, k, v, logi, logf, carry):
    xs = (jnp.transpose(q, (0, 2, 1, 3)), jnp.transpose(k, (0, 2, 1, 3)), jnp.transpose(v, (0, 2, 1, 3)),
          jnp.transpose(logi, (0, 2, 1)), jnp.transpose(logf, (0, 2, 1)))
    final, hs = mlstm_chunk(carry, xs)
    return jnp.transpose(hs, (0, 2, 1, 3)), final

def ab_project(x, w_in, b_gate, pos):
    bn, s_len, _ = x.shape
    z = x @ w_in
    cuts = [W_A, 2 * W_A, 3 * W_A, 4 * W_A, 4 * W_A + 2 * H_A,
            4 * W_A + 2 * H_A + N_DIL * W_B, 4 * W_A + 2 * H_A + 2 * N_DIL * W_B]
    qa, ka, va, oa, gates, qb, kb, vb = jnp.split(z, cuts, axis=-1)
    qa = qa.reshape(bn, s_len, H_A, DH_A)
    ka = ka.reshape(bn, s_len, H_A, DH_A) * (DH_A ** -0.5)
    va = va.reshape(bn, s_len, H_A, DH_A)
    gates = (gates + b_gate).astype(jnp.float32)
    logi = gates[..., :H_A]
    logf = jax.nn.log_sigmoid(gates[..., H_A:])
    qb = rope(qb.reshape(bn, s_len, N_DIL * H_B, DH), pos).reshape(bn, s_len, N_DIL, H_B, DH)
    kb = rope(kb.reshape(bn, s_len, N_DIL * H_B, DH), pos).reshape(bn, s_len, N_DIL, H_B, DH)
    vb = vb.reshape(bn, s_len, N_DIL, H_B, DH)
    return qa, ka, va, oa, logi, logf, qb, kb, vb

def ab_output(h_a, oa, outs, lses, w_out):
    bn, s_len = oa.shape[:2]
    ga = h_a.astype(oa.dtype).reshape(bn, s_len, W_A) * jax.nn.sigmoid(oa)
    wts = jax.nn.softmax(jnp.stack(lses, axis=0), axis=0)
    ob = jnp.sum(wts[..., None].astype(oa.dtype) * jnp.stack(outs, axis=0), axis=0)
    return jnp.concatenate([ga, ob.reshape(bn, s_len, W_B)], axis=-1) @ w_out

def c_project(x, w_in, pos):
    bn, s_len, _ = x.shape
    z = x @ w_in
    q, k, v = jnp.split(z, [H_C * DH, (H_C + KV_C) * DH], axis=-1)
    q = rope(q.reshape(bn, s_len, H_C, DH), pos)
    k = rope(k.reshape(bn, s_len, KV_C, DH), pos)
    v = v.reshape(bn, s_len, KV_C, DH)
    return q, k, v

def setup_inputs(seed: int = 0) -> dict:
    key = jax.random.key(seed)
    ks = jax.random.split(key, 24)

    def nrm(k, shape, scale):
        return jax.random.normal(k, shape, jnp.float32) * scale

    b_gate = jnp.concatenate([nrm(ks[10], (N_AB, H_A), 0.1),
                              jnp.linspace(3.0, 6.0, H_A, dtype=jnp.float32)[None, :] + nrm(ks[11], (N_AB, H_A), 0.1)], axis=-1)
    return {
        'x_prompt': nrm(ks[0], (BATCH, SEQ, D_MODEL), 1.0),
        'x_sample': nrm(ks[1], (DEC_BATCH, DEC_SEQ, D_MODEL), 1.0),
        'state_mlstm_C': nrm(ks[2], (N_AB, DEC_BATCH, H_A, DH_A, DH_A), DH_A ** -0.5),
        'state_mlstm_n': nrm(ks[3], (N_AB, DEC_BATCH, H_A, DH_A), 0.5),
        'state_mlstm_m': nrm(ks[4], (N_AB, DEC_BATCH, H_A), 1.0),
        'cache_dil1_kv': nrm(ks[5], (N_AB, DEC_BATCH, min(DIL_WINDOWS[0], PAST_LEN), 2, H_B, DH), 1.0),
        'cache_dil2_kv': nrm(ks[6], (N_AB, DEC_BATCH, min(DIL_WINDOWS[1], PAST_LEN), 2, H_B, DH), 1.0),
        'cache_dil3_kv': nrm(ks[7], (N_AB, DEC_BATCH, min(DIL_WINDOWS[2], PAST_LEN), 2, H_B, DH), 1.0),
        'cache_swa_kv': nrm(ks[8], (N_C, DEC_BATCH, min(WIN_C, PAST_LEN), 2, KV_C, DH), 1.0),
        'w_in_ab': nrm(ks[9], (N_AB, D_MODEL, IN_AB), D_MODEL ** -0.5),
        'b_gate_ab': b_gate,
        'w_out_ab': nrm(ks[12], (N_AB, OUT_AB, D_MODEL), BETA * OUT_AB ** -0.5),
        'w_in_c': nrm(ks[13], (N_C, D_MODEL, IN_C), D_MODEL ** -0.5),
        'sinks_c': nrm(ks[14], (N_C, H_C), 0.5),
        'w_out_c': nrm(ks[15], (N_C, OUT_C, D_MODEL), BETA * OUT_C ** -0.5),
        'ln1_g': 1.0 + nrm(ks[16], (DEPTH, D_MODEL), 0.05),
        'ln1_b': nrm(ks[17], (DEPTH, D_MODEL), 0.02),
        'ln2_g': 1.0 + nrm(ks[18], (DEPTH, D_MODEL), 0.05),
        'ln2_b': nrm(ks[19], (DEPTH, D_MODEL), 0.02),
        'w_up': nrm(ks[20], (DEPTH, D_MODEL, D_FF), D_MODEL ** -0.5),
        'w_down': nrm(ks[21], (DEPTH, D_FF, D_MODEL), BETA * D_FF ** -0.5),
    }

def reference(x_prompt, x_sample, state_mlstm_C, state_mlstm_n, state_mlstm_m, cache_dil1_kv, cache_dil2_kv,
              cache_dil3_kv, cache_swa_kv, w_in_ab, b_gate_ab, w_out_ab, w_in_c, sinks_c, w_out_c,
              ln1_g, ln1_b, ln2_g, ln2_b, w_up, w_down):
    s_len = x_prompt.shape[1]
    t_len = x_sample.shape[1]
    pos_p = jnp.arange(s_len, dtype=jnp.int32)
    pos_s = PAST_LEN + jnp.arange(t_len, dtype=jnp.int32)
    dil_caches = (cache_dil1_kv, cache_dil2_kv, cache_dil3_kv)
    mc_p, mc_s, mn_p, mn_s, mm_p, mm_s = [], [], [], [], [], []
    dil_p = [[] for _ in range(N_DIL)]
    dil_s = [[] for _ in range(N_DIL)]
    swa_p, swa_s = [], []
    xp, xs = x_prompt, x_sample
    for layer in range(DEPTH):
        j = layer // 2
        if layer % 2 == 0:
            qa, ka, va, oa, logi, logf, qb, kb, vb = ab_project(xp, w_in_ab[j], b_gate_ab[j], pos_p)
            h_a, (c_new, n_new, m_new) = mlstm_prompt(qa, ka, va, logi, logf)
            mc_p.append(c_new)
            mn_p.append(n_new)
            mm_p.append(m_new)
            outs, lses = [], []
            for g in range(N_DIL):
                o, l = dilated_prompt(qb[:, :, g], kb[:, :, g], vb[:, :, g], DIL_RATES[g], DIL_WINDOWS[g] // DIL_RATES[g])
                outs.append(o)
                lses.append(l)
                keep = min(DIL_WINDOWS[g], s_len)
                dil_p[g].append(jnp.stack([kb[:, s_len - keep:, g], vb[:, s_len - keep:, g]], axis=2))
            mix_p = ab_output(h_a, oa, outs, lses, w_out_ab[j])
            qa, ka, va, oa, logi, logf, qb, kb, vb = ab_project(xs, w_in_ab[j], b_gate_ab[j], pos_s)
            carry = (state_mlstm_C[j].astype(jnp.float32), state_mlstm_n[j].astype(jnp.float32),
                     state_mlstm_m[j].astype(jnp.float32))
            h_a, (c_new, n_new, m_new) = mlstm_sample(qa, ka, va, logi, logf, carry)
            mc_s.append(c_new)
            mn_s.append(n_new)
            mm_s.append(m_new)
            outs, lses = [], []
            for g in range(N_DIL):
                buf = dil_caches[g][j].astype(kb.dtype)
                n_past = buf.shape[1]
                k_all = jnp.concatenate([buf[:, :, 0], kb[:, :, g]], axis=1)
                v_all = jnp.concatenate([buf[:, :, 1], vb[:, :, g]], axis=1)
                o, l = dilated_sample(qb[:, :, g], k_all, v_all, DIL_RATES[g], DIL_WINDOWS[g] // DIL_RATES[g], n_past)
                outs.append(o)
                lses.append(l)
                keep = min(DIL_WINDOWS[g], n_past + t_len)
                dil_s[g].append(jnp.stack([k_all[:, n_past + t_len - keep:], v_all[:, n_past + t_len - keep:]], axis=2))
            mix_s = ab_output(h_a, oa, outs, lses, w_out_ab[j])
        else:
            q, k, v = c_project(xp, w_in_c[j], pos_p)
            o, _ = banded_attention(q, k, v, WIN_C - 1, sinks_c[j])
            keep = min(WIN_C, s_len)
            swa_p.append(jnp.stack([k[:, s_len - keep:], v[:, s_len - keep:]], axis=2))
            mix_p = o.reshape(xp.shape[0], s_len, OUT_C) @ w_out_c[j]
            q, k, v = c_project(xs, w_in_c[j], pos_s)
            buf = cache_swa_kv[j].astype(k.dtype)
            n_past = buf.shape[1]
            k_all = jnp.concatenate([buf[:, :, 0], k], axis=1)
            v_all = jnp.concatenate([buf[:, :, 1], v], axis=1)
            o = swa_sample(q, k_all, v_all, sinks_c[j], n_past)
            keep = min(WIN_C, n_past + t_len)
            swa_s.append(jnp.stack([k_all[:, n_past + t_len - keep:], v_all[:, n_past + t_len - keep:]], axis=2))
            mix_s = o.reshape(xs.shape[0], t_len, OUT_C) @ w_out_c[j]
        xp = layer_norm(ALPHA * xp + mix_p, ln1_g[layer], ln1_b[layer])
        xp = layer_norm(ALPHA * xp + sq_relu_mlp(xp, w_up[layer], w_down[layer]), ln2_g[layer], ln2_b[layer])
        xs = layer_norm(ALPHA * xs + mix_s, ln1_g[layer], ln1_b[layer])
        xs = layer_norm(ALPHA * xs + sq_relu_mlp(xs, w_up[layer], w_down[layer]), ln2_g[layer], ln2_b[layer])
    mlstm_C_p = jnp.stack(mc_p)
    mlstm_C_s = jnp.stack(mc_s)
    mlstm_n_p = jnp.stack(mn_p)
    mlstm_n_s = jnp.stack(mn_s)
    mlstm_m_p = jnp.stack(mm_p)
    mlstm_m_s = jnp.stack(mm_s)
    dil1_kv_p = jnp.stack(dil_p[0])
    dil1_kv_s = jnp.stack(dil_s[0])
    dil2_kv_p = jnp.stack(dil_p[1])
    dil2_kv_s = jnp.stack(dil_s[1])
    dil3_kv_p = jnp.stack(dil_p[2])
    dil3_kv_s = jnp.stack(dil_s[2])
    swa_kv_p = jnp.stack(swa_p)
    swa_kv_s = jnp.stack(swa_s)
    return (xp, xs, mlstm_C_p, mlstm_C_s, mlstm_n_p, mlstm_n_s, mlstm_m_p, mlstm_m_s,
            dil1_kv_p, dil1_kv_s, dil2_kv_p, dil2_kv_s, dil3_kv_p, dil3_kv_s, swa_kv_p, swa_kv_s)


_drawn_inputs = setup_inputs


def setup_inputs(seed=0):
    import zlib

    import numpy as np

    out = dict(_drawn_inputs(seed))
    spreads = {}
    factors = {'sinks_c': 8.0}
    for name, (base, spread) in spreads.items():
        noise = np.random.default_rng([zlib.crc32(name.encode()), seed]).standard_normal(out[name].shape)
        drawn = base * np.exp(spread * noise) if base else spread * noise
        out[name] = __import__('jax').numpy.asarray(drawn.astype(out[name].dtype))
    for name, factor in factors.items():
        out[name] = (out[name] * factor).astype(out[name].dtype)
    return out
```

```python
from contextlib import ExitStack

import numpy as np

import concourse.bass as bass
from concourse import mybir

F32 = mybir.dt.float32
F32R = mybir.dt.float32r
ALU = mybir.AluOpType
ACT = mybir.ActivationFunctionType
AX = mybir.AxisListType

P = 128
D = 1024
KT = D // P
SEQ = 1024
NT = SEQ // P
BD, TD = 8, 8
NS = BD * TD
PAST = 1024
HA, DA = 4, 128
WA = HA * DA
HB, DH = 8, 64
WB = HB * DH
NG = 3
RATES = (1, 4, 16)
KEEP_P = (128, 512, 1024)
CACHE = (128, 512, 1024)
KEEP_S = (128, 512, 1032)
HC, KVC = 16, 2
FF = 4096
ALPHA = 4.0 ** 0.25
EPS = 1e-5
SCALE = DH ** -0.5
NEG = -1e30
SROW = WB + 2 * HB
IN_AB = 4 * WA + 2 * HA + 3 * NG * WB
QB0 = 4 * WA + 2 * HA


def constants():
    c = {}
    q, k = np.arange(P)[:, None], np.arange(P)[None, :]
    off = np.full((P, P), NEG)
    cur = np.where(k <= q, 0.0, NEG)
    c["ident"] = np.eye(P)
    c["m_dil"] = np.concatenate([np.where(k >= q, 0.0, NEG), cur], 1)
    c["m_swa"] = np.concatenate([np.where(k > q, 0.0, NEG), cur], 1)
    c["m_first"] = np.concatenate([off, cur], 1)
    c["m_pair"] = np.concatenate([off, np.where((k <= q) & (k // 64 == q // 64), 0.0, NEG)], 1)
    c["m_causalT"] = cur.T
    c["m_sampleT"] = np.full((P, NS), NEG)
    s = np.arange(NS)
    c["m_sampleT"][:NS] = np.where((s[:, None] <= s[None, :]) & (s[:, None] // TD == s[None, :] // TD), 0.0, NEG)
    inv = 500000.0 ** (-np.arange(8, dtype=np.float32) / np.float32(8))

    def rope(pos):
        ang = pos.astype(np.float32)[..., None] * inv.astype(np.float32)
        co, si = np.cos(ang), np.sin(ang)
        return np.concatenate([co, co, -si, si], -1)

    n, p = np.arange(NT)[:, None], np.arange(P)[None, :]
    tok = [n * P + p, n // 2 + 4 * (P * (n % 2) + p), 2 * n + p // 64 + 16 * (p % 64)]
    rp = np.stack([rope(t) for t in tok])
    rs = np.zeros((P, 32))
    rs[:NS] = rope(PAST + s % TD)
    c["rope_s"] = rs
    sel = np.zeros((P, HA * P))
    for h in range(HA):
        sel[h, h * P:(h + 1) * P] = 1
    c["sel"] = sel
    c["ones"] = np.ones((P, P))
    blk = np.zeros((P, BD))
    blk[s, s // TD] = 1
    c["blk"] = blk
    r = np.arange(NS)
    h, t = (r // TD)[:, None], (r % TD)[:, None]
    kk = np.arange(P)[None, :]
    ms = [np.where(kk >= t, 0.0, NEG)]
    for j in range(4):
        ms.append(np.where((t % 4 == j) & ((t < 4) | (kk > 0)), 0.0, NEG))
    for j in range(4):
        ms.append(np.where((t % 4 == j) & (t // 4 == kk // 64), 0.0, NEG))
    u = np.arange(TD)[None, :]
    ms += [np.where(u <= t, 0.0, NEG), np.where((u <= t) & ((t - u) % 4 == 0), 0.0, NEG), np.where(u == t, 0.0, NEG)]
    m = np.zeros((P, 9 * P + 3 * TD))
    m[:NS] = np.concatenate(ms, 1)
    c["m_samp"] = m
    dg = np.zeros((P, HB))
    dg[r, r // TD] = 1
    c["diag"] = dg
    hm = np.zeros((P, 4, HB, TD))
    for uu in range(4):
        hm[:64, uu, 2 * uu] = 1
        hm[64:, uu, 2 * uu + 1] = 1
    c["headsel"] = hm.reshape(P, -1)
    t = (np.arange(P) % TD)[:, None]
    c["m_swas"] = np.concatenate([np.where(kk >= t + 1, 0.0, NEG), np.where(u <= t, 0.0, NEG)], 1)
    at, cols = {}, 0
    for name, a in c.items():
        at[name] = (cols, a.shape[1])
        cols += a.shape[1]
    table = np.concatenate([a for a in c.values()], 1).astype(np.float32)
    return table, at, rp.astype(np.float32)


CONST, CONST_AT, ROPE = constants()


class Count:

    def __init__(self, sem, per=1, credit=0, pre=0):
        self.sem, self.per, self.credit, self.pre = sem, per, credit, pre

    def done(self, n, c=0, back=0):
        return n * self.per + (self.credit + self.pre + c + 1 - back)


def hold(eng):
    eng.nop(nofuse=True)


class Phase:

    def __init__(self, nc, env):
        self.nc, self.env, self.stack, self.given = nc, env, ExitStack(), []

    def enter_context(self, manager):
        self.given.append(self.stack.enter_context(manager))
        return self.given[-1]

    def __enter__(self):
        self.env["sems"] = self
        return self

    def __exit__(self, *error):
        if not error[0]:
            with self.nc.Block() as block:
                @block.sync
                def _(sp):
                    for s in self.given:
                        sp.sem_clear(s)
        self.stack.close()
        return False


def own_semaphores(phase):
    def run(nc, env, *more):
        with Phase(nc, env):
            phase(nc, env, *more)
    return run


def row_tiles(t, rate, n_half, par):
    if rate == 1:
        return [t.rearrange("(n two p) c -> two n p c", two=2, p=P)[par, n_half]]
    if rate == 4:
        return [t.rearrange("(b p j) c -> b j p c", j=4, b=2)[par, n_half]]
    v = t.rearrange("(p j four) c -> four j p c", j=4, four=4)
    return [v[2 * par, n_half], v[2 * par + 1, n_half]]


def halves(tile, parts):
    return [tile] if len(parts) == 1 else [tile[0:64], tile[64:128]]


@own_semaphores
def attention(nc, env, name, cfg):
    H, widths, prev, rate = cfg["heads"], cfg["widths"], cfg["prev"], cfg["rate"]
    swa = cfg["sinks"] is not None
    QW, KW = cfg["qw"], cfg["kw"]
    ZW = sum(widths)
    NCH = len(widths)
    QT = QW // P
    UT = 2 if swa else KW // P
    NROPE = (QW + KW) // DH
    NK = 2 * P if prev else P
    K0 = 0 if prev else P
    PAIRS = H // 2
    jobs = [[(0, t) for t in range(a, a + 4)] for a in range(0, QT, 4)] + [[(1, u) for u in range(UT)]]
    NQK = len(jobs)
    U = NQK + 2 + PAIRS
    NX = 2 if rate == 16 else 1
    XAMT = 16 * (NX + 1)
    W, w_sems = cfg["w"], cfg["w_sems"]
    cst = env["cst"]
    ident = cst("ident")

    with ExitStack() as ctx:
        def sb(nm, shape):
            return ctx.enter_context(nc.sbuf_tensor(f"{name}_{nm}", shape, F32))

        def ps(nm):
            return ctx.enter_context(nc.psum_tensor(f"{name}_{nm}", [P, 512], F32))

        def sem(nm):
            return env["sems"].enter_context(nc.semaphore(f"{name}_{nm}"))

        xn = [sb(f"xn{i}", [P, D]) for i in range(2)]
        rt = [sb(f"rt{i}", [P, 32]) for i in range(2)]
        xT = [sb(f"xT{i}", [P, KT, P]) for i in range(2)]
        z = [sb(f"z{i}", [P, ZW + (P if swa else 0)]) for i in range(2)]
        qT = sb("qT", [P, QT, P])
        kT = [sb(f"kT{i}", [P, UT, P]) for i in range(2)]
        VW = ZW - QW - KW
        vb = [sb(f"vb{i}", [P, VW]) for i in range(2)]
        prob = sb("prob", [P, H, NK])
        pT = sb("pT", [P, PAIRS, 4 if prev else 2, P])
        osb = [sb(f"o{i}", [P, H * DH + 2 * H]) for i in range(2)]
        nmx = sb("nmx", [P, H])
        rot = sb("rot", [P, 2 * NROPE * 16])
        mask_even = sb("mask_even", [P, 2 * P])
        if swa:
            sinkb = sb("sinkb", [P, H])
            sink8 = sb("sink8", [P, H])
            sk = sb("sk", [P, H])
            rden = sb("rden", [P, H])
        mask_odd = cst(cfg["mask"])
        ps_z = [ps(f"ps_z{i}") for i in range(2)]
        ps_t = [ps(f"ps_t{i}") for i in range(2)]
        ps_s = [ps(f"ps_s{i}") for i in range(2)]
        ps_o = [ps(f"ps_o{i}") for i in range(H * DH // 512)]

        x_loaded = [sem(f"x_loaded{i}") for i in range(2)]
        o_stored = [sem(f"o_stored{i}") for i in range(2)]
        kv_stored = [sem(f"kv_stored{i}") for i in range(2)]
        s_stored = sem("s_stored")
        sink_loaded = sem("sink_loaded")
        t_full = Count(sem("t_full"), U, pre=2)
        t_free = Count(sem("t_free"), U, pre=2, credit=2)
        z_full = Count(sem("z_full"), NCH)
        z_free = Count(sem("z_free"), NCH, credit=2)
        s_full = Count(sem("s_full"), PAIRS)
        s_free = Count(sem("s_free"), PAIRS, credit=2)
        max_ready = Count(sem("max_ready"), H // 4)
        exp_done = Count(sem("exp_done"), PAIRS)
        sk_ready = Count(sem("sk_ready"), 1)
        sink_done = Count(sem("sink_done"), 1)
        roped = Count(sem("roped"), 1)
        v_ready = Count(sem("v_ready"), 1, credit=1)
        o_full = Count(sem("o_full"), 1, credit=1)
        o_free = Count(sem("o_free"), 1, credit=1)
        cleared = sem("cleared")
        dve_step = sem("dve_step")
        KVAMT = 32 * NX if cfg["kv_tiles"] != "last" else 0

        block = ctx.enter_context(nc.Block())

        @block.sync
        def _(sp):
            def load(i, par):
                parts = row_tiles(cfg["x"], rate, i, par)
                for dst, src in zip(halves(xn[par][:, :], parts), parts):
                    sp.dma_start(dst, src).then_inc(x_loaded[par], 16)
                sp.dma_start(rt[par][:, :], cfg["rope"].rearrange("(n two) p c -> two n p c", two=2)[par, i])\
                    .then_inc(x_loaded[par], 16)

            def load_sample():
                for a in range(NX):
                    rows = NS // NX
                    sp.dma_start(xn[0][a * rows:(a + 1) * rows, :], cfg["xs"][a * rows:(a + 1) * rows, :])\
                        .then_inc(x_loaded[0], 16)
                sp.dma_start(rt[0][0:NS, :], cst("rope_s", DRAM=True)[0:NS, :]).then_inc(x_loaded[0], 16)

            def store_kv(i, par):
                for which, col in ((0, QW), (1, QW + KW)):
                    parts = cfg["kv_rows"](i, par, which)
                    for src, dst in zip(halves(z[par][:, col:col + KW], parts), parts):
                        sp.dma_start(dst, src).then_inc(kv_stored[par], 16)

            def store_o(i, par, n):
                sp.wait_ge(o_free.sem, o_free.done(n))
                if cfg["out_norm"]:
                    parts, width = row_tiles(cfg["out"], rate, i, par), H * DH
                else:
                    parts, width = row_tiles(cfg["out"], rate, i, par), SROW
                for src, dst in zip(halves(osb[par][:, 0:width], parts), parts):
                    sp.dma_start(dst, src).then_inc(o_stored[par], 16)

            if swa:
                sp.dma_start(sinkb[:, :], cfg["sinks"].to_broadcast([P, H])).then_inc(sink_loaded, 16)
            load(0, 0)
            load(0, 1)
            cfg["prefetch"](sp)

            def step(i, par, n, more):
                sp.wait_ge(roped.sem, roped.done(n))
                if KVAMT and (cfg["kv_tiles"] == "all" or par == 1):
                    store_kv(i, par)
                if par == 1 and not more and cfg["kv_tiles"] == "last":
                    store_kv(i, par)
                if more:
                    load(i + 1, par)
                elif par == 0:
                    load_sample()
                store_o(i, par, n)

            with sp.Fori(0, NT // 2 - 1) as i:
                for par in range(2):
                    cfg["spread"](sp, i, par)
                    step(i, par, 2 * i + par, True)
            for par in range(2):
                cfg["spread"](sp, NT // 2 - 1, par)
                step(NT // 2 - 1, par, NT - 2 + par, False)
            sp.wait_ge(roped.sem, roped.done(NT))
            n_s = cfg["store_sample"](sp, z[0], s_stored)
            sp.wait_ge(s_stored, 16 * n_s)
            for par in range(2):
                sp.wait_ge(o_stored[par], 16 * NX * (NT // 2 + 1))
            if KVAMT:
                sp.wait_ge(kv_stored[1], KVAMT * (NT // 2 + 1))
                if cfg["kv_tiles"] == "all":
                    sp.wait_ge(kv_stored[0], KVAMT * (NT // 2 + 1))
            else:
                sp.wait_ge(kv_stored[1], 32 * NX)

        @block.tensor
        def _(pe):
            def transposes(n, c, bank, ins):
                pe.wait_ge(t_free.sem, t_free.done(n, c, back=2))
                for j, a in enumerate(ins):
                    last = pe.transpose(ps_t[bank][:, j * P:(j + 1) * P], a, ident)
                last.then_inc(t_full.sem, 1)

            def x_transposes(n, c, i_next, par):
                pe.wait_ge(x_loaded[par], XAMT * (i_next + 1))
                for half in range(2):
                    transposes(n, c + half, (bank_of(par ^ 1, c + half) if c >= 0 else half),
                               [xn[par][:, (4 * half + j) * P:(4 * half + j + 1) * P] for j in range(4)])

            def bank_of(par, c):
                return (par * U + c) % 2

            def project(n, par, xT_count):
                pe.wait_ge(t_free.sem, xT_count)
                col = 0
                for c, width in enumerate(widths):
                    pe.wait_ge(z_free.sem, z_free.done(n, c, back=2))
                    if isinstance(n, int) and n == 0:
                        pe.wait_ge(w_sems[c], 16)
                    for k in range(KT):
                        last = pe.matmul(ps_z[(par * NCH + c) % 2][:, 0:width], xT[par][:, k, :],
                                         W[:, k, col:col + width], start=(k == 0), stop=(k == KT - 1))
                    last.then_inc(z_full.sem, 1)
                    col += width

            def step(i, par, n):
                pe.wait_ge(roped.sem, roped.done(n))
                for j, job in enumerate(jobs):
                    cols = [t * P if kind == 0 else QW + t * P for kind, t in job]
                    if swa and job[0][0] == 1:
                        cols = [QW, ZW]
                    transposes(n, j, bank_of(par, j), [z[par][:, a:a + P] for a in cols])
                x_transposes(n, NQK, i + par, par ^ 1)
                pe.wait_ge(t_free.sem, t_free.done(n, NQK - 1))
                for s in range(PAIRS):
                    r, a = s // 2, s % 2
                    pe.wait_ge(s_free.sem, s_free.done(n, s, back=2))
                    for j in range(2):
                        h = 4 * r + 2 * j + a
                        u = (0 if h // 8 == a else 1) if swa else h // 2
                        rows = slice(64 * a, 64 * a + 64)
                        out = ps_s[a][:, j * NK:(j + 1) * NK]
                        if prev:
                            pe.matmul(out[:, 0:P], qT[rows, h // 2, :], kT[par ^ 1][rows, u, :], start=True, stop=True)
                        last = pe.matmul(out[:, NK - P:NK], qT[rows, h // 2, :], kT[par][rows, u, :], start=True, stop=True)
                    last.then_inc(s_full.sem, 1)
                project(n + 1, par ^ 1, t_free.done(n, NQK + 1))
                pe.wait_ge(o_free.sem, o_free.done(n, back=1))
                pe.wait_ge(v_ready.sem, v_ready.done(n))
                nb = 4 if prev else 2
                for pr in range(PAIRS + 1):
                    if pr < PAIRS:
                        pe.wait_ge(exp_done.sem, exp_done.done(n, pr))
                        transposes(n, NQK + 2 + pr, bank_of(par, NQK + 2 + pr),
                                   [prob[:, 2 * pr + m // (nb // 2), (m % (nb // 2)) * P:(m % (nb // 2) + 1) * P]
                                    for m in range(nb)])
                    if pr >= 1:
                        pe.wait_ge(t_free.sem, t_free.done(n, NQK + 2 + pr - 1))
                        for hh in range(2):
                            h = 2 * (pr - 1) + hh
                            v0 = (h // 8 if swa else h) * DH
                            out = ps_o[h // 8][:, (h % 8) * DH:(h % 8 + 1) * DH]
                            if prev:
                                pe.matmul(out, pT[:, pr - 1, 2 * hh, :], vb[par ^ 1][:, v0:v0 + DH], start=True, stop=False)
                            last = pe.matmul(out, pT[:, pr - 1, (nb // 2) * hh + nb // 2 - 1, :], vb[par][:, v0:v0 + DH],
                                             start=not prev, stop=True)
                last.then_inc(o_full.sem, 1)

            x_transposes(0, -2, 0, 0)
            project(0, 0, t_free.done(0, -1))
            pe.wait_ge(cleared, 1)
            with pe.Fori(0, NT // 2) as i:
                for par in range(2):
                    step(i, par, 2 * i + par)

        @block.scalar
        def _(act):
            def evacuate(n, c, bank, dst, src=None):
                act.wait_ge(t_full.sem, t_full.done(n, c))
                nc.scalar.copy(dst, ps_t[bank][:, 0:512] if src is None else ps_t[bank][:, 0:src])\
                    .then_inc(t_free.sem, 1)

            def x_out(n, c, par):
                for half in range(2):
                    evacuate(n, c + half, ((par ^ 1) * U + c + half) % 2 if c >= 0 else half,
                             xT[par][:, 4 * half:4 * half + 4, :].rearrange("p k t -> p (k t)"))

            x_out(0, -2, 0)
            with act.Fori(0, NT // 2) as i:
                for par in range(2):
                    n = 2 * i + par
                    for j, job in enumerate(jobs):
                        kind, t0 = job[0]
                        dst = qT[:, t0:t0 + 4, :] if kind == 0 else kT[par][:, :, :]
                        evacuate(n, j, (par * U + j) % 2, dst.rearrange("p k t -> p (k t)"), len(job) * P)
                    x_out(n, NQK, par ^ 1)
                    for h in range(H):
                        if h % 4 == 0:
                            act.wait_ge(max_ready.sem, max_ready.done(n, h // 4))
                        e = nc.scalar.activation(prob[:, h, :], prob[:, h, :], ACT.Exp, bias=nmx[:, h:h + 1], scale=SCALE,
                                                 accum_out=osb[par][:, H * DH + H + h:H * DH + H + h + 1])
                        if h % 2:
                            e.then_inc(exp_done.sem, 1)
                    if swa:
                        act.wait_ge(sk_ready.sem, sk_ready.done(n))
                        nc.scalar.activation(sk[:, :], sk[:, :], ACT.Exp).then_inc(sink_done.sem, 1)
                    for pr in range(PAIRS):
                        evacuate(n, NQK + 2 + pr, (par * U + NQK + 2 + pr) % 2,
                                 pT[:, pr, :, :].rearrange("p k t -> p (k t)"), (4 if prev else 2) * P)

        @block.gpsimd
        def _(pool):
            pool.memset(kT[1][:, :, :], 0.0)
            pool.memset(vb[1][:, :], 0.0).then_inc(cleared, 1)
            for c, k in ((t_free, 2), (z_free, 2), (s_free, 2), (v_ready, 1), (o_full, 1), (o_free, 1)):
                pool.sem_inc(c.sem, k)
            for par in range(2):
                pool.sem_inc(o_stored[par], 16 * NX)
                if KVAMT and (par == 1 or cfg["kv_tiles"] == "all"):
                    pool.sem_inc(kv_stored[par], KVAMT)
            with pool.Fori(0, NT // 2) as i:
                for par in range(2):
                    n = 2 * i + par
                    pool.wait_ge(cleared, 1)
                    pool.wait_ge(roped.sem, roped.done(n))
                    pool.wait_ge(o_full.sem, o_full.done(n, back=1))
                    hold(pool)
                    pool.tensor_copy(vb[par][:, :], z[par][:, QW + KW:ZW]).then_inc(v_ready.sem, 1)

        @block.vector
        def _(dve):
            steps = [0]
            base = [0]

            def link(ins):
                steps[0] += 1
                ins.then_inc(dve_step, 1)
                dve.wait_ge(dve_step, base[0] + steps[0])

            def z_out(n, par, i_next):
                col = 0
                if KVAMT and (cfg["kv_tiles"] == "all" or par == 1):
                    dve.wait_ge(kv_stored[par], KVAMT * (i_next + 1))
                dve.wait_ge(v_ready.sem, v_ready.done(n, back=2) if not isinstance(n, int) else 1)
                for c, width in enumerate(widths):
                    dve.wait_ge(z_full.sem, z_full.done(n, c))
                    last = dve.tensor_copy(z[par][:, col:col + width], ps_z[(par * NCH + c) % 2][:, 0:width])
                    last.then_inc(z_free.sem, 1)
                    col += width
                dve.wait_ge(z_free.sem, z_free.done(n, NCH - 1))
                dve.wait_ge(x_loaded[par], XAMT * (i_next + 1))
                zr = z[par][:, 0:NROPE * DH].rearrange("p (h d) -> p h d", d=DH)
                ra = rot[:, 0:NROPE * 16].rearrange("p (h d) -> p h d", d=16)
                rb = rot[:, NROPE * 16:2 * NROPE * 16].rearrange("p (h d) -> p h d", d=16)

                def tab(a, b):
                    return rt[par][:, a:b].rearrange("p (o d) -> p o d", o=1).broadcast_to([P, NROPE, b - a])

                dve.tensor_tensor(ra, zr[:, :, 0:16], tab(0, 16), ALU.mult)
                dve.tensor_tensor(rb[:, :, 0:8], zr[:, :, 8:16], tab(16, 24), ALU.mult)
                link(dve.tensor_tensor(rb[:, :, 8:16], zr[:, :, 0:8], tab(24, 32), ALU.mult))
                if not swa:
                    dve.tensor_tensor(zr[:, :, 0:16], ra, rb, ALU.add).then_inc(roped.sem, 1)
                    return
                link(dve.tensor_tensor(zr[:, :, 0:16], ra, rb, ALU.add))
                dve.tensor_copy(z[par][:, ZW:ZW + DH], z[par][:, QW + DH:QW + 2 * DH])
                dve.tensor_copy(z[par][:, ZW + DH:ZW + 2 * DH], z[par][:, QW:QW + DH]).then_inc(roped.sem, 1)

            if swa:
                dve.wait_ge(sink_loaded, 16)
                dve.tensor_scalar(sink8[:, :], sinkb[:, :], 1.0 / SCALE, None, ALU.mult)
            if prev:
                link(dve.tensor_copy(mask_even[:, :], cst("m_first")))
            z_out(0, 0, 0)
            before, per_pair = steps[0], 2 * (H // 4 + 4 if swa else 1) + (prev and cfg["mask_even_after"])
            with dve.Fori(0, NT // 2) as i:
                for par in range(2):
                    n = 2 * i + par
                    if par == 0:
                        base[0], steps[0] = i * per_pair + before, 0
                    mask = mask_odd if (par == 1 or not prev) else mask_even[:, :]
                    dve.wait_ge(t_full.sem, t_full.done(n, 0))
                    dve.wait_ge(o_stored[par], 16 * NX * (i + 1))
                    for s in range(PAIRS):
                        r, a = s // 2, s % 2
                        dve.wait_ge(s_full.sem, s_full.done(n, s))
                        hold(dve)
                        for j in range(2):
                            h = 4 * r + 2 * j + a
                            last = dve.tensor_tensor_reduce(
                                out=prob[:, h, :], in0=ps_s[a][:, j * NK:(j + 1) * NK], in1=mask[:, K0:2 * P],
                                scale=1.0, scalar=NEG, op0=ALU.add, op1=ALU.max,
                                accum_out=osb[par][:, H * DH + h:H * DH + h + 1])
                        last.then_inc(s_free.sem, 1)
                        if a == 1:
                            hs = slice(4 * r, 4 * r + 4)
                            mx = osb[par][:, H * DH + 4 * r:H * DH + 4 * r + 4]
                            dve.wait_ge(s_free.sem, s_free.done(n, s))
                            if swa:
                                link(dve.tensor_tensor(mx, mx, sink8[:, hs], ALU.max))
                            dve.tensor_scalar(nmx[:, hs], mx, -SCALE, None, ALU.mult).then_inc(max_ready.sem, 1)
                    if swa:
                        dve.wait_ge(max_ready.sem, max_ready.done(n, H // 4 - 1))
                        dve.tensor_tensor(sk[:, :], sinkb[:, :], nmx[:, :], ALU.add).then_inc(sk_ready.sem, 1)
                    if prev and par == 0 and cfg["mask_even_after"]:
                        link(dve.tensor_copy(mask_even[:, :], mask_odd))
                    z_out(n + 1, par ^ 1, i + par)
                    dve.wait_ge(o_full.sem, o_full.done(n))
                    if not swa:
                        dve.tensor_copy(osb[par][:, 0:512], ps_o[0][:, :]).then_inc(o_free.sem, 1)
                    else:
                        dve.wait_ge(sink_done.sem, sink_done.done(n))
                        den = osb[par][:, H * DH + H:H * DH + 2 * H]
                        link(dve.tensor_tensor(rden[:, :], den, sk[:, :], ALU.add))
                        link(dve.reciprocal(rden[:, :], rden[:, :]))
                        for b in range(2):
                            last = dve.tensor_tensor(
                                osb[par][:, b * 512:(b + 1) * 512].rearrange("p (h d) -> p h d", d=DH),
                                ps_o[b][:, :].rearrange("p (h d) -> p h d", d=DH),
                                rden[:, 8 * b:8 * b + 8].rearrange("p (h o) -> p h o", o=1).broadcast_to([P, 8, DH]),
                                ALU.mult)
                        last.then_inc(o_free.sem, 1)
            assert steps[0] == per_pair


@own_semaphores
def mlstm(nc, env, cfg):
    widths = [WA, WA, WA, WA, 2 * HA]
    NCH, U = len(widths), 6
    Q_T, K_T, G_T, X_T, C_T = 0, 1, 2, 3, 5
    W, w_sems, cst = cfg["w"], cfg["w_sems"], env["cst"]
    ident, sel, ones = cst("ident"), cst("sel"), cst("ones")
    KSCALE = DA ** -0.5

    with ExitStack() as ctx:
        def sb(nm, shape):
            return ctx.enter_context(nc.sbuf_tensor(f"m_{nm}", shape, F32))

        def sem(nm):
            return env["sems"].enter_context(nc.semaphore(f"m_{nm}"))

        xn = [sb(f"xn{i}", [P, D]) for i in range(2)]
        xT = [sb(f"xT{i}", [P, KT, P]) for i in range(2)]
        z = [sb(f"z{i}", [P, 4 * WA]) for i in range(2)]
        gate = sb("gate", [P, 2 * HA])
        absf = sb("absf", [P, HA])
        logs = [sb(f"logs{i}", [P, P]) for i in range(2)]
        biasb = sb("biasb", [P, 2 * HA])
        qT = sb("qT", [P, HA, P])
        kT = sb("kT", [P, HA, P])
        lrow, frow, brow, rrow = (sb(nm, [HA, P]) for nm in ("lrow", "frow", "brow", "rrow"))
        mrow = [sb(f"mrow{i}", [HA, P]) for i in range(2)]
        zero4 = sb("zero4", [HA, P])
        rows = sb("rows", [P, P])
        ial = sb("ial", [HA, 1])
        ild = sb("ild", [HA, HA * BD])
        cols = sb("cols", [P, P])
        ecol = sb("ecol", [P, 3 * HA])
        il = sb("il", [P, HA * BD])
        wt = sb("wt", [P, HA, P])
        kw = sb("kw", [P, HA, P])
        sig = sb("sig", [P, WA])
        num_in = sb("num_in", [P, HA, P])
        num = sb("num", [P, HA, P])
        nq = sb("nq", [P, 3 * HA])
        ga = [sb(f"ga{i}", [P, WA]) for i in range(2)]
        C = sb("C", [P, HA, DA])
        nst = sb("nst", [P, HA])

        x_loaded = [sem(f"x_loaded{i}") for i in range(2)]
        ga_stored = [sem(f"ga_stored{i}") for i in range(2)]
        bias_loaded, cleared, out_stored = sem("bias_loaded"), sem("cleared"), sem("out_stored")
        t_full, t_free = Count(sem("t_full"), U, pre=2), Count(sem("t_free"), U, pre=2, credit=2)
        z_full, z_free = Count(sem("z_full"), NCH), Count(sem("z_free"), NCH, credit=2)
        abs_ready, log_ready, z_ready = (Count(sem(s)) for s in ("abs_ready", "log_ready", "z_ready"))
        rows_ready, d_full, s_full = (Count(sem(s)) for s in ("rows_ready", "d_full", "s_full"))
        cols_ready, masked, w_ready, sw_ready = (Count(sem(s)) for s in ("cols_ready", "masked", "w_ready", "sw_ready"))
        kw_ready, sig_ready, all_full, num_copied = (Count(sem(s)) for s in ("kw_ready", "sig_ready", "all_full", "num_copied"))
        ga_ready = Count(sem("ga_ready"))
        state_ready = Count(sem("state_ready"), 1, credit=1)
        exp_gate = Count(sem("exp_gate"))
        dve_step = sem("dve_step")

        bank_stack = ctx.enter_context(ExitStack())

        def ps(nm):
            return bank_stack.enter_context(nc.psum_tensor(f"m_{nm}", [P, 512], F32))

        ps_z = [ps(f"ps_z{i}") for i in range(2)]
        ps_t = [ps(f"ps_t{i}") for i in range(2)]
        ps_s, ps_d, ps_o, ps_m = ps("ps_s"), ps("ps_d"), ps("ps_o"), ps("ps_m")

        def head(t, h, w=P):
            return t[:, h * w:(h + 1) * w]

        def tbank(par, c):
            return ps_t[(par * U + c) % 2] if c >= 0 else ps_t[c % 2]

        with nc.Block() as block:
            @block.sync
            def _(sp):
                def load(i, par):
                    sp.dma_start(xn[par][:, :], row_tiles(cfg["x"], 1, i, par)[0]).then_inc(x_loaded[par], 16)

                sp.dma_start(biasb[:, :], cfg["bias"].to_broadcast([P, 2 * HA])).then_inc(bias_loaded, 16)
                load(0, 0)
                load(0, 1)
                cfg["prefetch"](sp)

                def step(i, par, n, more):
                    sp.wait_ge(z_ready.sem, z_ready.done(n))
                    if more:
                        load(i + 1, par)
                    elif par == 0:
                        sp.dma_start(xn[0][0:NS, :], cfg["xs"]).then_inc(x_loaded[0], 16)
                    sp.wait_ge(ga_ready.sem, ga_ready.done(n))
                    sp.dma_start(row_tiles(cfg["out"][0:SEQ, 0:WA], 1, i, par)[0], ga[par][:, :]).then_inc(ga_stored[par], 16)

                with sp.Fori(0, NT // 2 - 1) as i:
                    for par in range(2):
                        step(i, par, 2 * i + par, True)
                for par in range(2):
                    step(NT // 2 - 1, par, NT - 2 + par, False)
                sp.wait_ge(state_ready.sem, state_ready.done(NT - 1))
                with nc.allow_non_contiguous_dma(reason="a few numbers"):
                    sp.dma_start(cfg["C_p"].rearrange("h d e -> d h e"), C[:, :, :]).then_inc(out_stored, 16)
                    sp.dma_start(cfg["n_p"].rearrange("h d -> d h"), nst[:, :]).then_inc(out_stored, 16)
                    sp.dma_start(cfg["m_p"].rearrange("(h o) -> h o", o=1), mrow[1][:, P - 1:P]).then_inc(out_stored, 16)
                sp.wait_ge(out_stored, 48)
                for par in range(2):
                    sp.wait_ge(ga_stored[par], 16 * (NT // 2 + 1))

            @block.tensor
            def _(pe):
                def x_transposes(n, c, i_next, par):
                    pe.wait_ge(x_loaded[par], 16 * (i_next + 1))
                    for half in range(2):
                        bank = tbank(par ^ 1, c + half) if c >= 0 else ps_t[half]
                        pe.wait_ge(t_free.sem, t_free.done(n, c + half, back=2))
                        for j in range(4):
                            last = pe.transpose(head(bank, j), head(xn[par], 4 * half + j), ident)
                        last.then_inc(t_full.sem, 1)

                def project(n, par, chunks):
                    for c in chunks:
                        pe.wait_ge(z_free.sem, z_free.done(n, c, back=2))
                        if isinstance(n, int) and n == 0:
                            pe.wait_ge(w_sems[c], 16)
                        for k in range(KT):
                            last = pe.matmul(ps_z[(par * NCH + c) % 2][:, 0:widths[c]], xT[par][:, k, :],
                                             W[:, k, c * WA:c * WA + widths[c]], start=(k == 0), stop=(k == KT - 1))
                        last.then_inc(z_full.sem, 1)

                def step(i, par, n):
                    zt = z[par]
                    pe.wait_ge(z_ready.sem, z_ready.done(n))
                    for c, col in ((Q_T, 0), (K_T, WA)):
                        pe.wait_ge(t_free.sem, t_free.done(n, c, back=2))
                        for h in range(HA):
                            last = pe.transpose(head(tbank(par, c), h), zt[:, col + h * P:col + (h + 1) * P], ident)
                        last.then_inc(t_full.sem, 1)
                    pe.wait_ge(t_free.sem, t_free.done(n, G_T, back=2))
                    pe.transpose(tbank(par, G_T)[:, 0:P], logs[par][:, :], ident).then_inc(t_full.sem, 1)
                    x_transposes(n, X_T, i + par, par ^ 1)
                    pe.wait_ge(t_free.sem, t_free.done(n, K_T))
                    pe.wait_ge(state_ready.sem, state_ready.done(n, back=1))
                    for h in range(HA):
                        last = pe.matmul(head(ps_s, h), kT[:, h, :], qT[:, h, :], start=True, stop=True)
                    last.then_inc(s_full.sem, 1)
                    pe.wait_ge(t_free.sem, t_free.done(n, X_T + 1))
                    project(n + 1, par ^ 1, (0, 1))
                    pe.wait_ge(rows_ready.sem, rows_ready.done(n))
                    for h in range(HA):
                        pe.matmul(head(ps_d, h), sel[0:HA, h * P:(h + 1) * P], rrow[:, :], start=True, stop=True)
                    pe.matmul(ps_m[:, 12:16], ones[0:HA, :], ild[:, 0:HA], start=True, stop=True).then_inc(d_full.sem, 1)
                    pe.wait_ge(t_free.sem, t_free.done(n, C_T, back=2))
                    pe.transpose(tbank(par, C_T)[:, 0:P], rows[:, :], ident).then_inc(t_full.sem, 1)
                    project(n + 1, par ^ 1, (2, 3, 4))
                    pe.wait_ge(cols_ready.sem, cols_ready.done(n))
                    pe.wait_ge(sw_ready.sem, sw_ready.done(n))
                    for h in range(HA):
                        pe.matmul(head(ps_o, h), wt[:, h, :], zt[:, 2 * WA + h * P:2 * WA + (h + 1) * P], start=True, stop=True)
                        pe.matmul(ps_m[:, h:h + 1], wt[:, h, :], ones[:, 0:1], start=True, stop=True)
                    for h in range(HA):
                        pe.matmul(head(ps_s, h), qT[:, h, :], C[:, h, :], start=True, stop=True)
                        pe.matmul(ps_m[:, HA + h:HA + h + 1], qT[:, h, :], nst[:, h:h + 1], start=True, stop=True)
                    pe.wait_ge(kw_ready.sem, kw_ready.done(n))
                    for h in range(HA):
                        pe.matmul(head(ps_d, h), kw[:, h, :], zt[:, 2 * WA + h * P:2 * WA + (h + 1) * P], start=True, stop=True)
                        last = pe.matmul(ps_m[:, 2 * HA + h:2 * HA + h + 1], kw[:, h, :], ones[:, 0:1], start=True, stop=True)
                    last.then_inc(all_full.sem, 1)

                x_transposes(0, -2, 0, 0)
                pe.wait_ge(t_free.sem, t_free.done(0, -1))
                project(0, 0, range(NCH))
                pe.wait_ge(cleared, 3)
                with pe.Fori(0, NT // 2) as i:
                    for par in range(2):
                        step(i, par, 2 * i + par)

            @block.scalar
            def _(act):
                def evacuate(n, c, bank, dst, w=512):
                    act.wait_ge(t_full.sem, t_full.done(n, c))
                    nc.scalar.copy(dst, bank[:, 0:w]).then_inc(t_free.sem, 1)

                def x_out(n, c, par):
                    for half in range(2):
                        bank = tbank(par ^ 1, c + half) if c >= 0 else ps_t[half]
                        evacuate(n, c + half, bank, xT[par][:, 4 * half:4 * half + 4, :].rearrange("p k t -> p (k t)"))

                def log_gate(n):
                    act.wait_ge(abs_ready.sem, abs_ready.done(n))
                    nc.scalar.activation(absf[:, :], absf[:, :], ACT.Exp, scale=-1.0).then_inc(exp_gate.sem, 1)
                    act.wait_ge(exp_gate.sem, exp_gate.done(n))
                    nc.scalar.activation(absf[:, :], absf[:, :], ACT.Ln, bias=1.0).then_inc(log_ready.sem, 1)

                x_out(0, -2, 0)
                log_gate(0)
                with act.Fori(0, NT // 2) as i:
                    for par in range(2):
                        n = 2 * i + par
                        evacuate(n, Q_T, tbank(par, Q_T), qT[:, :, :].rearrange("p h t -> p (h t)"))
                        evacuate(n, K_T, tbank(par, K_T), kT[:, :, :].rearrange("p h t -> p (h t)"))
                        act.wait_ge(t_full.sem, t_full.done(n, G_T))
                        nc.scalar.copy(lrow[:, :], tbank(par, G_T)[0:HA, 0:P])
                        nc.scalar.copy(frow[:, :], tbank(par, G_T)[32:32 + HA, 0:P]).then_inc(t_free.sem, 1)
                        x_out(n, X_T, par ^ 1)
                        evacuate(n, C_T, tbank(par, C_T), cols[:, :], P)
                        act.wait_ge(t_free.sem, t_free.done(n, C_T))
                        nc.scalar.activation(ecol[:, 0:HA], cols[:, 32:32 + HA], ACT.Exp)
                        nc.scalar.activation(ecol[:, HA:2 * HA], cols[:, 64:64 + HA], ACT.Exp, scale=-1.0)
                        nc.scalar.activation(ecol[:, 2 * HA:3 * HA], cols[:, 96:96 + HA], ACT.Exp)
                        nc.scalar.activation(il[:, 0:HA], ps_m[:, 12:16], ACT.Exp).then_inc(cols_ready.sem, 1)
                        act.wait_ge(masked.sem, masked.done(n))
                        for h in range(HA):
                            last = nc.scalar.activation(wt[:, h, :], wt[:, h, :], ACT.Exp, bias=cols[:, h:h + 1])
                        last.then_inc(w_ready.sem, 1)
                        nc.scalar.activation(sig[:, :], z[par][:, 3 * WA:4 * WA], ACT.Exp, scale=-1.0).then_inc(sig_ready.sem, 1)
                        log_gate(n + 1)
                        act.wait_ge(all_full.sem, all_full.done(n))
                        nc.scalar.copy(num_in[:, :, :].rearrange("p h t -> p (h t)"), ps_o[:, :]).then_inc(num_copied.sem, 1)

            @block.gpsimd
            def _(pool):
                for c, k in ((t_free, 2), (z_free, 2), (state_ready, 1)):
                    pool.sem_inc(c.sem, k)
                for par in range(2):
                    pool.sem_inc(ga_stored[par], 16)
                    pool.memset(mrow[par][:, :], 0.0)
                    pool.memset(logs[par][:, :], 0.0)
                pool.memset(C[:, :, :], 0.0)
                pool.memset(nst[:, :], 0.0)
                pool.memset(zero4[:, :], 0.0)
                pool.memset(rows[:, :], 0.0).then_inc(cleared, 3)
                with pool.Fori(0, NT // 2) as i:
                    for par in range(2):
                        n = 2 * i + par
                        pool.wait_ge(state_ready.sem, state_ready.done(n, back=1))
                        pool.wait_ge(cols_ready.sem, cols_ready.done(n))
                        pool.tensor_tensor(kw[:, :, :], z[par][:, WA:2 * WA].rearrange("p (h d) -> p h d", d=P),
                                           ecol[:, 0:HA].rearrange("p (h o) -> p h o", o=1).broadcast_to([P, HA, P]),
                                           ALU.mult).then_inc(kw_ready.sem, 1)

            @block.vector
            def _(dve):
                steps, base = [0], [0]

                def link(ins):
                    steps[0] += 1
                    ins.then_inc(dve_step, 1)
                    dve.wait_ge(dve_step, base[0] + steps[0])

                def z_out(n, par):
                    for c in range(NCH):
                        dve.wait_ge(z_full.sem, z_full.done(n, c))
                        src = ps_z[(par * NCH + c) % 2][:, 0:widths[c]]
                        dst = z[par][:, c * WA:(c + 1) * WA] if c < 4 else None
                        if c == 1:
                            last = dve.tensor_scalar(dst, src, KSCALE, None, ALU.mult)
                        elif c == 4:
                            last = dve.tensor_tensor(gate[:, :], src, biasb[:, :], ALU.add)
                        else:
                            last = dve.tensor_copy(dst, src)
                        last.then_inc(z_free.sem, 1)
                    dve.wait_ge(z_free.sem, z_free.done(n, NCH - 1))
                    dve.tensor_copy(logs[par][:, 0:HA], gate[:, 0:HA])
                    dve.scalar_tensor_tensor(out=absf[:, :], in0=gate[:, HA:2 * HA], scalar=-1.0, in1=gate[:, HA:2 * HA],
                                             op0=ALU.mult, op1=ALU.max).then_inc(abs_ready.sem, 1)
                    dve.wait_ge(log_ready.sem, log_ready.done(n))
                    dve.scalar_tensor_tensor(out=logs[par][:, 32:32 + HA], in0=gate[:, HA:2 * HA], scalar=0.0,
                                             in1=absf[:, :], op0=ALU.min, op1=ALU.subtract).then_inc(z_ready.sem, 1)

                dve.wait_ge(bias_loaded, 16)
                dve.wait_ge(cleared, 3)
                z_out(0, 0)
                per_pair = 2 * 12
                with dve.Fori(0, NT // 2) as i:
                    for par in range(2):
                        n = 2 * i + par
                        if par == 0:
                            base[0], steps[0] = i * per_pair, 0
                        dve.wait_ge(t_free.sem, t_free.done(n, G_T))
                        m_prev = mrow[par ^ 1][:, P - 1:P]
                        dve.tensor_tensor_scan(mrow[par][:, :], frow[:, :], lrow[:, :], m_prev, ALU.add, ALU.max)
                        link(dve.tensor_tensor_scan(brow[:, :], frow[:, :], zero4[:, :], 0.0, ALU.add, ALU.add))
                        dve.tensor_tensor(rows[0:HA, :], lrow[:, :], brow[:, :], ALU.subtract)
                        dve.tensor_copy(rows[64:64 + HA, :], mrow[par][:, :])
                        link(dve.tensor_tensor(rrow[:, :], brow[:, :], mrow[par][:, :], ALU.subtract))
                        dve.tensor_scalar(rows[32:32 + HA, :], rows[0:HA, :], rrow[:, P - 1:P], None, ALU.add)
                        dve.tensor_scalar(rows[96:96 + HA, :], rrow[:, :], m_prev, None, ALU.add)
                        link(dve.tensor_tensor(ial[:, :], rrow[:, P - 1:P], m_prev, ALU.add))
                        dve.tensor_scalar(ild[:, 0:HA], ident[0:HA, 0:HA], ial[:, :], None, ALU.mult)\
                            .then_inc(rows_ready.sem, 1)
                        dve.wait_ge(d_full.sem, d_full.done(n))
                        dve.tensor_tensor(wt[:, :, :], ps_d[:, :].rearrange("p (h t) -> p h t", h=HA),
                                          cst("m_causalT").rearrange("p (o t) -> p o t", o=1).broadcast_to([P, HA, P]),
                                          ALU.add).then_inc(masked.sem, 1)
                        dve.wait_ge(s_full.sem, s_full.done(n))
                        dve.wait_ge(w_ready.sem, w_ready.done(n))
                        dve.tensor_tensor(wt[:, :, :], ps_s[:, :].rearrange("p (h t) -> p h t", h=HA), wt[:, :, :], ALU.mult)\
                            .then_inc(sw_ready.sem, 1)
                        z_out(n + 1, par ^ 1)
                        dve.wait_ge(sig_ready.sem, sig_ready.done(n))
                        link(dve.tensor_scalar(sig[:, :], sig[:, :], 1.0, None, ALU.add))
                        link(dve.reciprocal(sig[:, :], sig[:, :]))
                        dve.wait_ge(num_copied.sem, num_copied.done(n))
                        link(dve.tensor_copy(nq[:, 0:2 * HA], ps_m[:, 0:2 * HA]))
                        link(dve.tensor_tensor(nq[:, HA:2 * HA], nq[:, HA:2 * HA], ecol[:, 2 * HA:3 * HA], ALU.mult))
                        link(dve.tensor_tensor(nq[:, 0:HA], nq[:, 0:HA], nq[:, HA:2 * HA], ALU.add))
                        link(dve.scalar_tensor_tensor(out=nq[:, 0:HA], in0=nq[:, 0:HA], scalar=-1.0, in1=nq[:, 0:HA],
                                                      op0=ALU.mult, op1=ALU.max))
                        link(dve.tensor_tensor(nq[:, 0:HA], nq[:, 0:HA], ecol[:, HA:2 * HA], ALU.max))
                        dve.reciprocal(nq[:, 2 * HA:3 * HA], nq[:, 0:HA])
                        for h in range(HA):
                            last = dve.scalar_tensor_tensor(out=num[:, h, :], in0=head(ps_s, h), scalar=ecol[:, 2 * HA + h:2 * HA + h + 1],
                                                            in1=num_in[:, h, :], op0=ALU.mult, op1=ALU.add)
                        link(last)
                        dve.wait_ge(ga_stored[par], 16 * (i + 1))
                        for h in range(HA):
                            last = dve.scalar_tensor_tensor(out=head(ga[par], h), in0=num[:, h, :],
                                                            scalar=nq[:, 2 * HA + h:2 * HA + h + 1], in1=head(sig, h),
                                                            op0=ALU.mult, op1=ALU.mult)
                        last.then_inc(ga_ready.sem, 1)
                        for h in range(HA):
                            dve.scalar_tensor_tensor(out=C[:, h, :], in0=C[:, h, :], scalar=il[:, h:h + 1], in1=head(ps_d, h),
                                                     op0=ALU.mult, op1=ALU.add)
                        link(dve.tensor_tensor(nst[:, :], nst[:, :], il[:, 0:HA], ALU.mult))
                        dve.tensor_tensor(nst[:, :], nst[:, :], ps_m[:, 2 * HA:3 * HA], ALU.add).then_inc(state_ready.sem, 1)
                assert steps[0] == per_pair, steps[0]

        bank_stack.close()
        mlstm_sample(nc, env, cfg, dict(z=z[0], logs=logs[0], qT=qT, kT=kT, sb=sb, sem=sem, ctx=ctx))


def mlstm_sample(nc, env, cfg, m):
    z, logs, qT, kT, sb, sem, ctx = (m[k] for k in ("z", "logs", "qT", "kT", "sb", "sem", "ctx"))
    cst = env["cst"]
    ident, sel, ones, blk = cst("ident"), cst("sel"), cst("ones"), cst("blk")
    C0 = cfg["w"][:, 4:8, 0:2 * HA * DA].rearrange("p k (b h e) -> p k b h e", b=2, h=HA)
    n0 = sb("s_n0", [P, HA, BD])
    m0 = sb("s_m0", [HA, BD])
    lrow, frow, brow, rrow, mrow, urow, zero = (sb(f"s_{nm}", [HA, NS]) for nm in ("lrow", "frow", "brow", "rrow", "mrow", "urow", "zero"))
    rows = sb("s_rows", [P, P])
    ial = sb("s_ial", [HA, BD])
    ild = sb("s_ild", [HA, HA, BD])
    il = sb("s_il", [P, HA * BD])
    cols = sb("s_cols", [NS, P])
    ecol = sb("s_ecol", [NS, 3 * HA])
    wt = sb("s_wt", [NS, HA, NS])
    kw = sb("s_kw", [NS, HA, P])
    vblk = cfg["w"][0:NS, 0:HA, 0:BD * DA].rearrange("p h (b d) -> p h b d", b=BD)
    qn = sb("s_qn", [P, HA, NS])
    inter = sb("s_inter", [P, HA, P])
    num_in = sb("s_num_in", [NS, WA])
    num = sb("s_num", [NS, WA])
    sig = sb("s_sig", [NS, WA])
    nq = sb("s_nq", [NS, 3 * HA])
    ga = sb("s_ga", [NS, WA])
    loaded, cleared, stored = sem("s_loaded"), sem("s_cleared"), sem("s_stored")
    qk_full, qk_out, rows_out, scanned, d_full = (sem(f"s_{x}") for x in ("qk_full", "qk_out", "rows_out", "scanned", "d_full"))
    cols_out, ecol_out, il_out, masked, w_out, sw_out = (sem(f"s_{x}") for x in ("cols_out", "ecol_out", "il_out", "masked", "w_out", "sw_out"))
    kw_out, vb_out, qn_out, inter_full, inter_out, n_full = (sem(f"s_{x}") for x in ("kw_out", "vb_out", "qn_out", "inter_full", "inter_out", "n_full"))
    num_out, back_full, sig_out, c_full, c_out, ga_out, nn_out, step = (sem(f"s_{x}") for x in ("num_out", "back_full", "sig_out", "c_full", "c_out", "ga_out", "nn_out", "step"))
    A, B, S, Dm, X, Y, N, M = (ctx.enter_context(nc.psum_tensor(f"m_s_ps{i}", [P, 512], F32)) for i in range(8))

    with nc.Block() as block:
        @block.sync
        def _(sp):
            with nc.allow_non_contiguous_dma(reason="the state's vectors"):
                for k in range(4):
                    sp.dma_start(C0[:, k, :, :, :].rearrange("p b h e -> p (b h) e"),
                                 cfg["C0"][2 * k:2 * k + 2].rearrange("b h d e -> d (b h) e")).then_inc(loaded, 16)
                for h in range(HA):
                    sp.dma_start(n0[:, h, :], cfg["n0"][:, h, :].rearrange("b d -> d b")).then_inc(loaded, 16)
                sp.dma_start(m0[:, :], cfg["m0"].rearrange("b h -> h b")).then_inc(loaded, 16)
                sp.wait_ge(ga_out, 1)
                sp.dma_start(cfg["out"][SEQ:SEQ + NS, 0:WA], ga[:, :]).then_inc(stored, 16)
                sp.wait_ge(c_out, 2 * HA)
                for k in range(4):
                    sp.dma_start(cfg["C_s"][2 * k:2 * k + 2].rearrange("b h d e -> d (b h) e"),
                                 C0[:, k, :, :, :].rearrange("p b h e -> p (b h) e")).then_inc(stored, 16)
                sp.wait_ge(nn_out, 1)
                for h in range(HA):
                    sp.dma_start(cfg["n_s"][:, h, :].rearrange("b d -> d b"), n0[:, h, :]).then_inc(stored, 16)
                sp.dma_start(cfg["m_s"].rearrange("b (h o) -> h b o", o=1),
                             mrow[:, :].rearrange("h (b t) -> h b t", t=TD)[:, :, TD - 1:TD]).then_inc(stored, 16)
            sp.wait_ge(stored, 16 * (6 + HA))

        @block.gpsimd
        def _(pool):
            pool.memset(zero[:, :], 0.0)
            pool.memset(inter[:, :, NS:P], 0.0)
            pool.memset(rows[:, :], 0.0).then_inc(cleared, 1)
            v = z[0:NS, 2 * WA:3 * WA].rearrange("p (h o d) -> p h o d", h=HA, o=1)
            for h in range(HA):
                last = pool.tensor_tensor(vblk[:, h, :, :], v[:, h, :, :].broadcast_to([NS, BD, DA]),
                                          blk[0:NS, :].rearrange("p (b o) -> p b o", o=1).broadcast_to([NS, BD, DA]), ALU.mult)
            last.then_inc(vb_out, 1)
            pool.wait_ge(ecol_out, 1)
            pool.tensor_tensor(kw[:, :, :], z[0:NS, WA:2 * WA].rearrange("p (h d) -> p h d", d=P),
                               ecol[:, 0:HA].rearrange("p (h o) -> p h o", o=1).broadcast_to([NS, HA, P]), ALU.mult)\
                .then_inc(kw_out, 1)

        @block.tensor
        def _(pe):
            for h in range(HA):
                pe.transpose(A[:, h * NS:(h + 1) * NS], z[0:NS, h * P:(h + 1) * P], ident[0:NS, 0:NS])
            for h in range(HA):
                pe.transpose(A[:, (HA + h) * NS:(HA + h + 1) * NS], z[0:NS, WA + h * P:WA + (h + 1) * P], ident[0:NS, 0:NS])
            pe.transpose(B[:, 0:NS], logs[0:NS, :], ident[0:NS, 0:NS]).then_inc(qk_full, 1)
            pe.wait_ge(qk_out, 1)
            for h in range(HA):
                pe.matmul(S[0:NS, h * NS:(h + 1) * NS], kT[:, h, 0:NS], qT[:, h, 0:NS], start=True, stop=True)
            pe.wait_ge(scanned, 1)
            for h in range(HA):
                pe.matmul(Dm[0:NS, h * NS:(h + 1) * NS], sel[0:HA, h * P:h * P + NS], rrow[:, :], start=True, stop=True)
            pe.transpose(X[:, 0:P], rows[:, :], ident)
            pe.matmul(M[:, 0:HA * BD], ones[0:HA, :], ild[:, :, :].rearrange("h g b -> h (g b)"), start=True, stop=True)\
                .then_inc(d_full, 1)
            pe.wait_ge(loaded, 16 * (HA + 5))
            for b in range(BD):
                for h in range(HA):
                    last = pe.matmul(Y[:, h * NS + b * TD:h * NS + (b + 1) * TD], C0[:, b // 2, b % 2, h, :],
                                     qT[:, h, b * TD:(b + 1) * TD], start=True, stop=True)
            last.then_inc(inter_full, 1)
            pe.wait_ge(sw_out, 1)
            for h in range(HA):
                pe.matmul(N[0:NS, h * P:(h + 1) * P], wt[:, h, :], z[0:NS, 2 * WA + h * P:2 * WA + (h + 1) * P], start=True, stop=True)
            pe.wait_ge(qn_out, 1)
            pe.wait_ge(il_out, 1)
            for h in range(HA):
                pe.matmul(M[0:NS, h:h + 1], wt[:, h, :], ones[0:NS, 0:1], start=True, stop=True)
                last = pe.matmul(M[0:NS, HA + h:HA + h + 1], qn[:, h, :], ones[:, 0:1], start=True, stop=True)
            pe.wait_ge(kw_out, 1)
            for h in range(HA):
                last = pe.matmul(M[:, 64 + h * BD:64 + (h + 1) * BD], kw[:, h, :], blk[0:NS, :], start=True, stop=True)
            last.then_inc(n_full, 1)
            pe.wait_ge(inter_out, 1)
            for h in range(HA):
                last = pe.transpose(A[:, h * P:(h + 1) * P], inter[:, h, :], ident)
            last.then_inc(back_full, 1)
            pe.wait_ge(vb_out, 1)
            pe.wait_ge(masked, 1)
            for u in range(2 * HA):
                if u >= 2:
                    pe.wait_ge(c_out, u - 1)
                h, half = u // 2, u % 2
                pe.matmul((B, X)[u % 2][:, :], kw[:, h, :],
                          vblk[:, h, 4 * half:4 * half + 4, :].rearrange("p b d -> p (b d)"), start=True, stop=True)\
                    .then_inc(c_full, 1)

        @block.scalar
        def _(act):
            act.wait_ge(qk_full, 1)
            nc.scalar.copy(lrow[:, :], B[0:HA, 0:NS])
            nc.scalar.copy(frow[:, :], B[32:32 + HA, 0:NS]).then_inc(rows_out, 1)
            nc.scalar.copy(qT[:, :, 0:NS], A[:, 0:HA * NS].rearrange("p (h t) -> p h t", t=NS))
            nc.scalar.copy(kT[:, :, 0:NS], A[:, HA * NS:2 * HA * NS].rearrange("p (h t) -> p h t", t=NS)).then_inc(qk_out, 1)
            nc.scalar.activation(sig[:, :], z[0:NS, 3 * WA:4 * WA], ACT.Exp, scale=-1.0).then_inc(sig_out, 1)
            act.wait_ge(d_full, 1)
            nc.scalar.copy(cols[:, :], X[0:NS, 0:P]).then_inc(cols_out, 1)
            nc.scalar.activation(il[:, :], M[:, 0:HA * BD], ACT.Exp).then_inc(il_out, 1)
            act.wait_ge(cols_out, 1)
            nc.scalar.activation(ecol[:, 0:HA], cols[:, 32:32 + HA], ACT.Exp)
            nc.scalar.activation(ecol[:, HA:2 * HA], cols[:, 64:64 + HA], ACT.Exp, scale=-1.0)
            nc.scalar.activation(ecol[:, 2 * HA:3 * HA], cols[:, 96:96 + HA], ACT.Exp).then_inc(ecol_out, 1)
            act.wait_ge(masked, 1)
            for h in range(HA):
                last = nc.scalar.activation(wt[:, h, :], wt[:, h, :], ACT.Exp, bias=cols[:, h:h + 1])
            last.then_inc(w_out, 1)
            act.wait_ge(inter_full, 1)
            nc.scalar.copy(inter[:, :, 0:NS], Y[:, 0:HA * NS].rearrange("p (h t) -> p h t", t=NS)).then_inc(inter_out, 1)
            act.wait_ge(n_full, 1)
            nc.scalar.copy(num_in[:, :], N[0:NS, :]).then_inc(num_out, 1)

        @block.vector
        def _(dve):
            count = [0]

            def link(ins):
                count[0] += 1
                ins.then_inc(step, 1)
                dve.wait_ge(step, count[0])

            def by_seq(t):
                return t.rearrange("p (b t) -> p b t", t=TD)

            dve.wait_ge(loaded, 16 * (HA + 5))
            dve.wait_ge(cleared, 1)
            dve.wait_ge(rows_out, 1)
            for b in range(BD):
                c = slice(b * TD, (b + 1) * TD)
                dve.tensor_tensor_scan(mrow[:, c], frow[:, c], lrow[:, c], m0[:, b:b + 1], ALU.add, ALU.max)
                last = dve.tensor_tensor_scan(brow[:, c], frow[:, c], zero[:, c], 0.0, ALU.add, ALU.add)
            link(last)
            dve.tensor_tensor(urow[:, :], lrow[:, :], brow[:, :], ALU.subtract)
            dve.tensor_copy(rows[64:64 + HA, 0:NS], mrow[:, :])
            link(dve.tensor_tensor(rrow[:, :], brow[:, :], mrow[:, :], ALU.subtract))
            end = by_seq(rrow[:, :])[:, :, TD - 1:TD]
            dve.tensor_copy(rows[0:HA, 0:NS], urow[:, :])
            dve.tensor_tensor(by_seq(rows[32:32 + HA, 0:NS]), by_seq(urow[:, :]), end.broadcast_to([HA, BD, TD]), ALU.add)
            dve.tensor_tensor(by_seq(rows[96:96 + HA, 0:NS]), by_seq(rrow[:, :]),
                              m0[:, :].rearrange("h (b o) -> h b o", o=1).broadcast_to([HA, BD, TD]), ALU.add)
            link(dve.tensor_tensor(ial[:, :].rearrange("h (b o) -> h b o", o=1), end, m0[:, :].rearrange("h (b o) -> h b o", o=1), ALU.add))
            dve.tensor_tensor(ild[:, :, :], ident[0:HA, 0:HA].rearrange("h (g o) -> h g o", o=1).broadcast_to([HA, HA, BD]),
                              ial[:, :].rearrange("h (o b) -> h o b", o=1).broadcast_to([HA, HA, BD]), ALU.mult)\
                .then_inc(scanned, 1)
            dve.wait_ge(d_full, 1)
            dve.tensor_tensor(wt[:, :, :], Dm[0:NS, 0:HA * NS].rearrange("p (h t) -> p h t", t=NS),
                              cst("m_sampleT")[0:NS, :].rearrange("p (o t) -> p o t", o=1).broadcast_to([NS, HA, NS]),
                              ALU.add).then_inc(masked, 1)
            dve.wait_ge(w_out, 1)
            dve.tensor_tensor(wt[:, :, :], S[0:NS, 0:HA * NS].rearrange("p (h t) -> p h t", t=NS), wt[:, :, :], ALU.mult)\
                .then_inc(sw_out, 1)
            dve.wait_ge(qk_out, 1)
            for h in range(HA):
                last = dve.tensor_tensor(by_seq(qn[:, h, :]), by_seq(qT[:, h, 0:NS]),
                                         n0[:, h, :].rearrange("p (b o) -> p b o", o=1).broadcast_to([P, BD, TD]), ALU.mult)
            last.then_inc(qn_out, 1)
            dve.wait_ge(sig_out, 1)
            link(dve.tensor_scalar(sig[:, :], sig[:, :], 1.0, None, ALU.add))
            link(dve.reciprocal(sig[:, :], sig[:, :]))
            dve.wait_ge(num_out, 1)
            dve.wait_ge(ecol_out, 1)
            dve.wait_ge(back_full, 1)
            link(dve.tensor_copy(nq[:, 0:2 * HA], M[0:NS, 0:2 * HA]))
            link(dve.tensor_tensor(nq[:, HA:2 * HA], nq[:, HA:2 * HA], ecol[:, 2 * HA:3 * HA], ALU.mult))
            link(dve.tensor_tensor(nq[:, 0:HA], nq[:, 0:HA], nq[:, HA:2 * HA], ALU.add))
            link(dve.scalar_tensor_tensor(out=nq[:, 0:HA], in0=nq[:, 0:HA], scalar=-1.0, in1=nq[:, 0:HA],
                                          op0=ALU.mult, op1=ALU.max))
            link(dve.tensor_tensor(nq[:, 0:HA], nq[:, 0:HA], ecol[:, HA:2 * HA], ALU.max))
            dve.reciprocal(nq[:, 2 * HA:3 * HA], nq[:, 0:HA])
            for h in range(HA):
                c = slice(h * P, (h + 1) * P)
                last = dve.scalar_tensor_tensor(out=num[:, c], in0=A[0:NS, c], scalar=ecol[:, 2 * HA + h:2 * HA + h + 1],
                                                in1=num_in[:, c], op0=ALU.mult, op1=ALU.add)
            link(last)
            for h in range(HA):
                c = slice(h * P, (h + 1) * P)
                last = dve.scalar_tensor_tensor(out=ga[:, c], in0=num[:, c], scalar=nq[:, 2 * HA + h:2 * HA + h + 1],
                                                in1=sig[:, c], op0=ALU.mult, op1=ALU.mult)
            last.then_inc(ga_out, 1)
            dve.wait_ge(il_out, 1)
            for u in range(2 * HA):
                h, half = u // 2, u % 2
                dve.wait_ge(c_full, u + 1)
                for q in range(4):
                    b = 4 * half + q
                    last = dve.scalar_tensor_tensor(out=C0[:, b // 2, b % 2, h, :], in0=C0[:, b // 2, b % 2, h, :],
                                                    scalar=il[:, h * BD + b:h * BD + b + 1],
                                                    in1=(B, X)[u % 2][:, q * DA:(q + 1) * DA], op0=ALU.mult, op1=ALU.add)
                last.then_inc(c_out, 1)
            n_all = n0[:, :, :].rearrange("p h b -> p (h b)")
            link(dve.tensor_tensor(n_all, n_all, il[:, :], ALU.mult))
            dve.tensor_tensor(n_all, n_all, M[:, 64:64 + HA * BD], ALU.add).then_inc(nn_out, 1)


@own_semaphores
def sample_attention(nc, env, cfg):
    cst = env["cst"]
    ident = cst("ident")
    NB = 9
    ROWS = HB * TD
    KEYS = NB * P + NG * TD
    with ExitStack() as ctx:
        def sb(nm, shape):
            return ctx.enter_context(nc.sbuf_tensor(f"s_{nm}", shape, F32))

        def ps(nm):
            return ctx.enter_context(nc.psum_tensor(f"s_{nm}", [P, 512], F32))

        def sem(nm):
            return env["sems"].enter_context(nc.semaphore(f"sa_{nm}"))

        kv = [sb(f"kv{i}", [P, NB, 2 * WB]) for i in range(2)]
        new = [sb(f"new{i}", [TD, 3, NG, WB]) for i in range(2)]
        qk_new = sb("qk_new", [P, 2, NG * 4, TD])
        qblk = sb("qblk", [P, NG, 4, ROWS])
        kT = [sb(f"kT{i}", [P, 4, P]) for i in range(2)]
        prob = sb("prob", [ROWS, KEYS])
        mx = sb("mx", [ROWS, 4])
        nmx = sb("nmx", [ROWS, 1])
        den = sb("den", [ROWS, 1])
        rden = sb("rden", [ROWS, 1])
        pT = sb("pT", [P, NB, ROWS])
        pTn = sb("pTn", [TD, NG, ROWS])
        sel = sb("sel", [ROWS, HB, DH])
        ob = [sb(f"ob{i}", [ROWS, DH]) for i in range(2)]
        ob_raw = sb("ob_raw", [ROWS, DH])
        ps_n = ps("ps_n")
        ps_t = [ps("ps_t0"), ps("ps_t1")]
        ps_s = [ps(f"ps_s{i}") for i in range(3)]
        ps_o = ps("ps_o")
        loaded = [sem(f"loaded{i}") for i in range(2)]
        stored = [sem(f"stored{i}") for i in range(2)]
        TU = NB + 4
        t_full, t_free = Count(sem("t_full"), TU), Count(sem("t_free"), TU, credit=2)
        n_full, q_ready, s_full, e_done, o_full, o_free, ob_ready, max_ready = (
            Count(sem(x)) for x in ("n_full", "q_ready", "s_full", "e_done", "o_full", "o_free", "ob_ready", "max_ready"))
        n_out, step = Count(sem("n_out")), sem("step")
        o_free = Count(o_free.sem, 1, credit=1)
        AMT = 16 * 5

        with nc.Block() as block:
            @block.sync
            def _(sp):
                def load(i, par):
                    def seq(t):
                        return t.rearrange("(b two) s x h d -> two b s (x h d)", two=2)[par, i]

                    c1, c2, c3 = (seq(c) for c in cfg["caches"])
                    sp.dma_start(kv[par][:, 0, :], c1).then_inc(loaded[par], 16)
                    sp.dma_start(kv[par][:, 1:5, :], c2.rearrange("(p j) c -> p j c", j=4)).then_inc(loaded[par], 16)
                    c3 = c3.rearrange("(p a j) c -> a p j c", a=4, j=4)
                    for a in range(2):
                        sp.dma_start(kv[par][64 * a:64 * a + 64, 5:9, :], c3[a]).then_inc(loaded[par], 16)
                    sp.dma_start(new[par][:, :, :, :],
                                 cfg["zs"].rearrange("(b two t) (j g c) -> two b t j g c", two=2, t=TD, j=3, g=NG)[par, i])\
                        .then_inc(loaded[par], 16)


                def store(i, par, n):
                    sp.wait_ge(ob_ready.sem, ob_ready.done(n))
                    out = cfg["out"].rearrange("(b two t) (h d) -> two b h t d", two=2, t=TD, d=DH)[par, i]
                    for h in range(HB):
                        sp.dma_start(out[h], ob[par][h * TD:(h + 1) * TD, :]).then_inc(stored[par], 16)

                load(0, 0)
                load(0, 1)
                cfg["prefetch"](sp)
                with sp.Fori(0, BD // 2 - 1) as i:
                    for par in range(2):
                        n = 2 * i + par
                        sp.wait_ge(o_full.sem, o_full.done(n))
                        load(i + 1, par)
                        store(i, par, n)
                for par in range(2):
                    store(BD // 2 - 1, par, BD - 2 + par)
                for par in range(2):
                    sp.wait_ge(stored[par], 16 * HB * (BD // 2 + 1))

            @block.tensor
            def _(pe):
                with pe.Fori(0, BD // 2) as i:
                    for par in range(2):
                        n = 2 * i + par
                        pe.wait_ge(loaded[par], AMT * (i + 1))
                        pe.wait_ge(o_free.sem, o_free.done(n, back=1))
                        hold(pe)
                        for kind in range(2):
                            for g in range(NG):
                                for u in range(4):
                                    c = (kind * NG * 4 + g * 4 + u) * TD
                                    last = pe.transpose(ps_n[:, c:c + TD], new[par][:, kind, g, u * P:(u + 1) * P], ident[0:TD, 0:TD])
                        last.then_inc(n_full.sem, 1)

                        def block_transposes(c):
                            pe.wait_ge(t_free.sem, t_free.done(n, c, back=2))
                            for u in range(4):
                                last = pe.transpose(ps_t[(par * TU + c) % 2][:, u * P:(u + 1) * P],
                                                    kv[par][:, c, u * P:(u + 1) * P], ident)
                            last.then_inc(t_full.sem, 1)

                        def group(c):
                            return 0 if c == 0 else (1 if c < 5 else 2)

                        block_transposes(0)
                        for c in range(NB):
                            if c + 1 < NB:
                                block_transposes(c + 1)
                            if c == 0:
                                pe.wait_ge(q_ready.sem, q_ready.done(n))
                            pe.wait_ge(t_free.sem, t_free.done(n, c))
                            for u in range(4):
                                pe.matmul(ps_s[c // 4][0:ROWS, (c % 4) * P:(c % 4 + 1) * P], qblk[:, group(c), u, :],
                                          kT[(par * TU + c) % 2][:, u, :], start=(u == 0), stop=(u == 3))
                        for g in range(NG):
                            for u in range(4):
                                last = pe.matmul(ps_s[2][0:ROWS, P + g * TD:P + (g + 1) * TD], qblk[:, g, u, :],
                                                 qk_new[:, 1, g * 4 + u, :], start=(u == 0), stop=(u == 3))
                        last.then_inc(s_full.sem, 1)
                        pe.wait_ge(e_done.sem, e_done.done(n))
                        for t, (a, b) in enumerate(((0, 4), (4, 8), (8, 9))):
                            pe.wait_ge(t_free.sem, t_free.done(n, NB + t, back=2))
                            hold(pe)
                            bank = ps_t[(par * TU + NB + t) % 2]
                            for c in range(a, b):
                                last = pe.transpose(bank[:, (c - a) * ROWS:(c - a + 1) * ROWS], prob[:, c * P:(c + 1) * P],
                                                    ident[0:ROWS, 0:ROWS])
                            last.then_inc(t_full.sem, 1)
                        pe.wait_ge(t_free.sem, t_free.done(n, NB + 3, back=2))
                        hold(pe)
                        for g in range(NG):
                            last = pe.transpose(ps_t[(par * TU + NB + 3) % 2][0:TD, g * ROWS:(g + 1) * ROWS],
                                                prob[:, NB * P + g * TD:NB * P + (g + 1) * TD], ident[0:ROWS, 0:ROWS])
                        last.then_inc(t_full.sem, 1)
                        pe.wait_ge(t_free.sem, t_free.done(n, NB + 3))
                        for c in range(NB):
                            pe.matmul(ps_o[0:ROWS, :], pT[:, c, :], kv[par][:, c, WB:2 * WB], start=(c == 0), stop=False)
                        for g in range(NG):
                            last = pe.matmul(ps_o[0:ROWS, :], pTn[:, g, :], new[par][:, 2, g, :], start=False, stop=(g == NG - 1))
                        last.then_inc(o_full.sem, 1)

            @block.scalar
            def _(act):
                with act.Fori(0, BD // 2) as i:
                    for par in range(2):
                        n = 2 * i + par
                        act.wait_ge(n_full.sem, n_full.done(n))
                        nc.scalar.copy(qk_new[:, :, :, :].rearrange("p a b t -> p (a b t)"), ps_n[:, 0:2 * NG * 4 * TD])\
                            .then_inc(n_out.sem, 1)
                        for c in range(NB):
                            act.wait_ge(t_full.sem, t_full.done(n, c))
                            nc.scalar.copy(kT[(par * TU + c) % 2][:, :, :].rearrange("p u t -> p (u t)"), ps_t[(par * TU + c) % 2][:, :])\
                                .then_inc(t_free.sem, 1)
                        act.wait_ge(max_ready.sem, max_ready.done(n))
                        nc.scalar.activation(prob[:, :], prob[:, :], ACT.Exp, bias=nmx[:, :], scale=SCALE, accum_out=den[:, :])\
                            .then_inc(e_done.sem, 1)
                        for t, (a, b) in enumerate(((0, 4), (4, 8), (8, 9))):
                            act.wait_ge(t_full.sem, t_full.done(n, NB + t))
                            nc.scalar.copy(pT[:, a:b, :].rearrange("p c r -> p (c r)"), ps_t[(par * TU + NB + t) % 2][:, 0:(b - a) * ROWS])\
                                .then_inc(t_free.sem, 1)
                        act.wait_ge(t_full.sem, t_full.done(n, NB + 3))
                        nc.scalar.copy(pTn[:, :, :].rearrange("p c r -> p (c r)"), ps_t[(par * TU + NB + 3) % 2][0:TD, 0:NG * ROWS])\
                            .then_inc(t_free.sem, 1)

            @block.gpsimd
            def _(pool):
                for c, k in ((t_free, 2), (o_free, 1)):
                    pool.sem_inc(c.sem, k)
                for par in range(2):
                    pool.sem_inc(stored[par], 16 * HB)

            @block.vector
            def _(dve):
                steps, base, per_pair = [0], [0], 2 * 3

                def link(ins):
                    steps[0] += 1
                    ins.then_inc(step, 1)
                    dve.wait_ge(step, base[0] + steps[0])

                with dve.Fori(0, BD // 2) as i:
                    for par in range(2):
                        n = 2 * i + par
                        if par == 0:
                            base[0], steps[0] = i * per_pair, 0
                        dve.wait_ge(n_out.sem, n_out.done(n))
                        for g in range(NG):
                            for u in range(4):
                                last = dve.tensor_tensor(
                                    qblk[:, g, u, :].rearrange("p (h t) -> p h t", t=TD),
                                    qk_new[:, 0, g * 4 + u, :].rearrange("p (o t) -> p o t", o=1).broadcast_to([P, HB, TD]),
                                    cst("headsel").rearrange("p (u h t) -> p u h t", u=4, h=HB)[:, u, :, :], ALU.mult)
                        last.then_inc(q_ready.sem, 1)
                        dve.wait_ge(s_full.sem, s_full.done(n))
                        hold(dve)
                        for t, (a, w) in enumerate(((0, 512), (512, 512), (1024, KEYS - 1024))):
                            last = dve.tensor_tensor_reduce(out=prob[:, a:a + w], in0=ps_s[t][0:ROWS, 0:w],
                                                            in1=cst("m_samp")[0:ROWS, a:a + w], scale=1.0, scalar=NEG,
                                                            op0=ALU.add, op1=ALU.max, accum_out=mx[:, t:t + 1])
                        link(last)
                        link(dve.tensor_reduce(mx[:, 3:4], mx[:, 0:3], AX.X, ALU.max))
                        dve.tensor_scalar(nmx[:, :], mx[:, 3:4], -SCALE, None, ALU.mult).then_inc(max_ready.sem, 1)
                        dve.wait_ge(o_full.sem, o_full.done(n))
                        dve.wait_ge(stored[par], 16 * HB * (i + 1))
                        dve.reciprocal(rden[:, :], den[:, :])
                        dve.tensor_tensor(sel[:, :, :], ps_o[0:ROWS, :].rearrange("p (h d) -> p h d", d=DH),
                                               cst("diag")[0:ROWS, :].rearrange("p (h o) -> p h o", o=1).broadcast_to([ROWS, HB, DH]),
                                               ALU.mult).then_inc(o_free.sem, 1)
                        dve.wait_ge(o_free.sem, o_free.done(n))
                        link(dve.tensor_reduce(ob_raw[:, :], sel[:, :, :].rearrange("p h d -> p d h"), AX.X, ALU.add))
                        dve.tensor_scalar(ob[par][:, :], ob_raw[:, :], rden[:, :], None, ALU.mult).then_inc(ob_ready.sem, 1)
                assert steps[0] == per_pair


@own_semaphores
def swa_sample(nc, env, cfg):
    cst = env["cst"]
    ident = cst("ident")
    KEYS = P + TD
    KV = KVC * DH
    with ExitStack() as ctx:
        def sb(nm, shape):
            return ctx.enter_context(nc.sbuf_tensor(f"w_{nm}", shape, F32))

        def ps(nm):
            return ctx.enter_context(nc.psum_tensor(f"w_{nm}", [P, 512], F32))

        def sem(nm):
            return env["sems"].enter_context(nc.semaphore(f"ws_{nm}"))

        kv = [sb(f"kv{i}", [P, 2 * KV]) for i in range(2)]
        new = [sb(f"new{i}", [TD, (HC + 2 * KVC) * DH]) for i in range(2)]
        q2 = sb("q2", [TD, HC, 2, DH])
        kT = sb("kT", [P, P])
        knT = sb("knT", [P, TD])
        qT = sb("qT", [P, HC, TD])
        prob = sb("prob", [P, KEYS])
        mx, nmx, den, rden, sk = (sb(x, [P, 1]) for x in ("mx", "nmx", "den", "rden", "sk"))
        sinkc = sb("sinkc", [P, 1])
        sink8 = sb("sink8", [P, 1])
        pT = sb("pT", [P, P])
        pTn = sb("pTn", [TD, P])
        ob = [sb(f"ob{i}", [P, DH]) for i in range(2)]
        ps_q, ps_k, ps_s, ps_p, ps_o = (ps(x) for x in ("ps_q", "ps_k", "ps_s", "ps_p", "ps_o"))
        loaded = [sem(f"loaded{i}") for i in range(2)]
        stored = [sem(f"stored{i}") for i in range(2)]
        sink_loaded, cleared, step = sem("sink_loaded"), sem("cleared"), sem("step")
        q2_ready, tr_full, tr_out, s_full, sk_ready, e_done, p_full, p_out, o_full = (
            Count(sem(x)) for x in ("q2_ready", "tr_full", "tr_out", "s_full", "sk_ready", "e_done", "p_full", "p_out", "o_full"))
        ob_ready = Count(sem("ob_ready"), 1, credit=2)

        with nc.Block() as block:
            @block.sync
            def _(sp):
                def load(i, par):
                    sp.dma_start(kv[par][:, :], cfg["cache"].rearrange("(b two) s x h d -> two b s (x h d)", two=2)[par, i])\
                        .then_inc(loaded[par], 16)
                    sp.dma_start(new[par][:, :], cfg["zs"].rearrange("(b two t) c -> two b t c", two=2, t=TD)[par, i])\
                        .then_inc(loaded[par], 16)

                def store(i, par, n):
                    sp.wait_ge(ob_ready.sem, ob_ready.done(n))
                    out = cfg["out"].rearrange("(b two t) (h d) -> two b h t d", two=2, t=TD, d=DH)[par, i]
                    for h in range(HC):
                        sp.dma_start(out[h], ob[par][h * TD:(h + 1) * TD, :]).then_inc(stored[par], 16)

                for h in range(HC):
                    sp.dma_start(sinkc[h * TD:(h + 1) * TD, :], cfg["sinks"][:, h:h + 1].to_broadcast([TD, 1])).then_inc(sink_loaded, 16)
                load(0, 0)
                load(0, 1)
                with sp.Fori(0, BD // 2 - 1) as i:
                    for par in range(2):
                        store(i, par, 2 * i + par)
                        load(i + 1, par)
                for par in range(2):
                    store(BD // 2 - 1, par, BD - 2 + par)
                for par in range(2):
                    sp.wait_ge(stored[par], 16 * HC * (BD // 2 + 1))

            @block.gpsimd
            def _(pool):
                pool.sem_inc(ob_ready.sem, 2)
                for par in range(2):
                    pool.sem_inc(stored[par], 16 * HC)
                pool.memset(q2[:, :, :, :], 0.0).then_inc(cleared, 1)

            @block.tensor
            def _(pe):
                with pe.Fori(0, BD // 2) as i:
                    for par in range(2):
                        n = 2 * i + par
                        pe.wait_ge(q2_ready.sem, q2_ready.done(n))
                        pe.wait_ge(loaded[par], 32 * (i + 1))
                        hold(pe)
                        for h in range(HC):
                            pe.transpose(ps_q[:, h * TD:(h + 1) * TD], q2[:, h, :, :].rearrange("p a d -> p (a d)"), ident[0:TD, 0:TD])
                        pe.transpose(ps_k[:, 0:P], kv[par][:, 0:KV], ident)
                        pe.transpose(ps_k[:, P:P + TD], new[par][:, HC * DH:HC * DH + KV], ident[0:TD, 0:TD]).then_inc(tr_full.sem, 1)
                        pe.wait_ge(tr_out.sem, tr_out.done(n))
                        qt = qT[:, :, :].rearrange("p h t -> p (h t)")
                        pe.matmul(ps_s[:, 0:P], qt, kT[:, :], start=True, stop=True)
                        pe.matmul(ps_s[:, P:KEYS], qt, knT[:, :], start=True, stop=True).then_inc(s_full.sem, 1)
                        pe.wait_ge(e_done.sem, e_done.done(n))
                        pe.transpose(ps_p[:, 0:P], prob[:, 0:P], ident)
                        pe.transpose(ps_p[0:TD, P:2 * P], prob[:, P:KEYS], ident).then_inc(p_full.sem, 1)
                        pe.wait_ge(p_out.sem, p_out.done(n))
                        pe.matmul(ps_o[:, 0:KV], pT[:, :], kv[par][:, KV:2 * KV], start=True, stop=False)
                        pe.matmul(ps_o[:, 0:KV], pTn[:, :], new[par][:, HC * DH + KV:HC * DH + 2 * KV], start=False, stop=True)\
                            .then_inc(o_full.sem, 1)

            @block.scalar
            def _(act):
                with act.Fori(0, BD // 2) as i:
                    for par in range(2):
                        n = 2 * i + par
                        act.wait_ge(tr_full.sem, tr_full.done(n))
                        nc.scalar.copy(qT[:, :, :].rearrange("p h t -> p (h t)"), ps_q[:, 0:P])
                        nc.scalar.copy(kT[:, :], ps_k[:, 0:P])
                        nc.scalar.copy(knT[:, :], ps_k[:, P:P + TD]).then_inc(tr_out.sem, 1)
                        act.wait_ge(sk_ready.sem, sk_ready.done(n))
                        nc.scalar.activation(sk[:, :], sk[:, :], ACT.Exp)
                        nc.scalar.activation(prob[:, :], prob[:, :], ACT.Exp, bias=nmx[:, :], scale=SCALE, accum_out=den[:, :])\
                            .then_inc(e_done.sem, 1)
                        act.wait_ge(p_full.sem, p_full.done(n))
                        nc.scalar.copy(pT[:, :], ps_p[:, 0:P])
                        nc.scalar.copy(pTn[:, :], ps_p[0:TD, P:2 * P]).then_inc(p_out.sem, 1)

            @block.vector
            def _(dve):
                steps, base, per_pair = [0], [0], 2 * 5

                def link(ins):
                    steps[0] += 1
                    ins.then_inc(step, 1)
                    dve.wait_ge(step, base[0] + steps[0])

                dve.wait_ge(sink_loaded, 16 * HC)
                dve.wait_ge(cleared, 1)
                dve.tensor_scalar(sink8[:, :], sinkc[:, :], 1.0 / SCALE, None, ALU.mult)
                with dve.Fori(0, BD // 2) as i:
                    for par in range(2):
                        n = 2 * i + par
                        if par == 0:
                            base[0], steps[0] = i * per_pair, 0
                        dve.wait_ge(loaded[par], 32 * (i + 1))
                        G = HC // KVC
                        for a in range(KVC):
                            last = dve.tensor_copy(q2[:, a * G:(a + 1) * G, a, :],
                                                   new[par][:, a * G * DH:(a + 1) * G * DH].rearrange("p (h d) -> p h d", d=DH))
                        last.then_inc(q2_ready.sem, 1)
                        dve.wait_ge(s_full.sem, s_full.done(n))
                        hold(dve)
                        link(dve.tensor_tensor_reduce(out=prob[:, :], in0=ps_s[:, 0:KEYS], in1=cst("m_swas"), scale=1.0,
                                                      scalar=NEG, op0=ALU.add, op1=ALU.max, accum_out=mx[:, :]))
                        link(dve.tensor_tensor(mx[:, :], mx[:, :], sink8[:, :], ALU.max))
                        link(dve.tensor_scalar(nmx[:, :], mx[:, :], -SCALE, None, ALU.mult))
                        dve.tensor_tensor(sk[:, :], sinkc[:, :], nmx[:, :], ALU.add).then_inc(sk_ready.sem, 1)
                        dve.wait_ge(o_full.sem, o_full.done(n))
                        dve.wait_ge(stored[par], 16 * HC * (i + 1))
                        link(dve.tensor_tensor(rden[:, :], den[:, :], sk[:, :], ALU.add))
                        link(dve.reciprocal(rden[:, :], rden[:, :]))
                        for a in range(KVC):
                            rows = slice(64 * a, 64 * a + 64)
                            last = dve.tensor_scalar(ob[par][rows, :], ps_o[rows, a * DH:(a + 1) * DH], rden[rows, :], None, ALU.mult)
                        last.then_inc(ob_ready.sem, 1)
                assert steps[0] == per_pair


def layer_norm(nc, dve, link, t, rows, y, ln_ready, rstd_ready, n, normed, normed_sem):
    for half in range(2):
        last = dve.bn_stats(t["stats"][0:rows, half, :], y[:, half * 512:(half + 1) * 512])
    link(last)
    hold(dve)
    link(dve.bn_aggr(t["mv"][0:rows, :], t["stats"][0:rows, :, :].rearrange("p a b -> p (a b)")))
    dve.tensor_scalar(t["ve"][0:rows, :], t["mv"][0:rows, 1:2], EPS, None, ALU.add).then_inc(ln_ready.sem, 1)
    dve.wait_ge(rstd_ready.sem, rstd_ready.done(n))
    r, a, ve = t["r"][0:rows, :], t["a"][0:rows, :], t["ve"][0:rows, :]
    link(dve.tensor_tensor(a, r, r, ALU.mult))
    link(dve.tensor_tensor(a, a, ve, ALU.mult))
    link(dve.tensor_scalar(a, a, -0.5, 1.5, ALU.mult, ALU.add))
    link(dve.tensor_tensor(r, r, a, ALU.mult))
    dve.tensor_scalar(normed, y, t["mv"][0:rows, 0:1], r, ALU.subtract, ALU.mult).then_inc(normed_sem, 1)


LN_LINKS = 6


def root(nc, act, t, rows, ln_ready, log_done, rstd_ready, n):
    act.wait_ge(ln_ready.sem, ln_ready.done(n))
    nc.scalar.activation(t["r"][0:rows, :], t["ve"][0:rows, :], ACT.Ln).then_inc(log_done.sem, 1)
    act.wait_ge(log_done.sem, log_done.done(n))
    nc.scalar.activation(t["r"][0:rows, :], t["r"][0:rows, :], ACT.Exp, scale=-0.5).then_inc(rstd_ready.sem, 1)


def ln_tiles(sb):
    return {"stats": sb("stats", [P, 2, 6]), "mv": sb("mv", [P, 2]), "ve": sb("ve", [P, 1]), "r": sb("r", [P, 1]), "a": sb("a", [P, 1])}


def split_passes(hi, lo):
    return [(hi[0], hi[1]), (hi[0], lo[1]), (lo[0], hi[1])]


@own_semaphores
def output_projection(nc, env, name, cfg):
    cst, merge, W = env["cst"], cfg["merge"], cfg["w"]
    ident = cst("ident")
    with ExitStack() as ctx:
        def sb(nm, shape, dt=F32):
            return ctx.enter_context(nc.sbuf_tensor(f"{name}_{nm}", shape, dt))

        def ps(nm):
            return ctx.enter_context(nc.psum_tensor(f"{name}_{nm}", [P, 512], F32))

        def sem(nm):
            return env["sems"].enter_context(nc.semaphore(f"{name}_{nm}"))

        xt = [sb(f"xt{i}", [P, D]) for i in range(2)]
        mixt = [sb(f"mixt{i}", [P, D]) for i in range(2)]
        mT = [[sb(f"mT{i}_{x}", [P, KT, P], F32R) for x in ("hi", "lo")] for i in range(2)]
        wo = [sb(f"wo_{x}", [P, KT, D], F32R) for x in ("hi", "lo")]
        y = sb("y", [P, D])
        yn = [sb(f"yn{i}", [P, D]) for i in range(2)]
        gb, bb = sb("gb", [P, D]), sb("bb", [P, D])
        t = ln_tiles(sb)
        if merge:
            og = [sb(f"og{i}", [P, NG, SROW]) for i in range(2)]
            top, dl, ed, tot, rt, cw = sb("top", [P, HB]), sb("dl", [P, NG, HB]), sb("ed", [P, NG, HB]), sb("tot", [P, HB]), sb("rt", [P, HB]), sb("cw", [P, NG, HB])
            part = [sb(f"part{i}", [P, WB]) for i in range(2)]
        ps_t = [ps(f"ps_t{i}") for i in range(2)]
        ps_y = [ps(f"ps_y{i}") for i in range(4)]
        x_loaded = [sem(f"x_loaded{i}") for i in range(2)]
        m_loaded = [sem(f"m_loaded{i}") for i in range(2)]
        stored = [sem(f"stored{i}") for i in range(2)]
        gb_loaded, step = sem("gb_loaded"), sem("step")
        delta_ready, exp_done, merged, ln_ready, log_done, rstd_ready, out_ready, normed = (
            Count(sem(x)) for x in ("delta_ready", "exp_done", "merged", "ln_ready", "log_done", "rstd_ready", "out_ready", "normed"))
        normed = Count(normed.sem, 1, credit=1)
        t_full, t_free = Count(sem("t_full"), 2), Count(sem("t_free"), 2, credit=2)
        m_hi, w_hi, w_lo = Count(sem("m_hi"), 2), sem("w_hi"), sem("w_lo")
        y_full, y_free = Count(sem("y_full"), 2), Count(sem("y_free"), 2, credit=4)
        MAMT = 16 * (NG + 1) if merge else 16

        with nc.Block() as block:
            @block.sync
            def _(sp):
                def ahead(t, i, par, pairs):
                    return row_tiles(t[2 * P * pairs:SEQ], 1, i, par)[0]

                def load_x(i, par, pairs=0):
                    sp.dma_start(xt[par][:, :], ahead(cfg["x"], i, par, pairs)).then_inc(x_loaded[par], 16)

                def load_mix(i, par, pairs=0):
                    if merge:
                        sp.dma_start(mixt[par][:, 0:WA], ahead(cfg["mix"][:, 0:WA], i, par, pairs)).then_inc(m_loaded[par], 16)
                        for g in range(NG):
                            sp.dma_start(og[par][:, g, :], ahead(cfg["og"][g], i, par, pairs)).then_inc(m_loaded[par], 16)
                    else:
                        sp.dma_start(mixt[par][:, :], ahead(cfg["mix"], i, par, pairs)).then_inc(m_loaded[par], 16)

                def load_sample_mix():
                    rows = NS // (MAMT // 16)
                    for q in range(MAMT // 16):
                        sp.dma_start(mixt[0][q * rows:(q + 1) * rows, :], cfg["mix"][SEQ + q * rows:SEQ + (q + 1) * rows, :])\
                            .then_inc(m_loaded[0], 16)

                def store(i, par, n):
                    sp.wait_ge(out_ready.sem, out_ready.done(n))
                    hold(sp)
                    sp.dma_start(row_tiles(cfg["out"][0:SEQ, :], 1, i, par)[0], yn[par][:, :]).then_inc(stored[par], 16)

                for par in range(2):
                    load_mix(0, par)
                    load_x(0, par)
                sp.dma_start(gb[:, :], cfg["g"].to_broadcast([P, D])).then_inc(gb_loaded, 16)
                sp.dma_start(bb[:, :], cfg["b"].to_broadcast([P, D])).then_inc(gb_loaded, 16)
                sp.wait_ge(t_full.sem, t_full.done(0, 1))
                load_mix(1, 0)
                with sp.Fori(0, NT // 2 - 2) as i:
                    for par in range(2):
                        n = 2 * i + par
                        sp.wait_ge(t_full.sem, t_full.done(n + 1, 1))
                        load_mix(i, par ^ 1, 1 + par)
                        sp.wait_ge(normed.sem, normed.done(n))
                        load_x(i, par, 1)
                        store(i, par, n)
                for n in range(NT - 4, NT):
                    if n + 3 <= NT:
                        sp.wait_ge(t_full.sem, t_full.done(n + 1, 1))
                        if n + 3 < NT:
                            load_mix((n + 3) // 2, (n + 3) % 2)
                        else:
                            load_sample_mix()
                    if n + 2 <= NT:
                        sp.wait_ge(normed.sem, normed.done(n))
                        if n + 2 < NT:
                            load_x((n + 2) // 2, n % 2)
                        else:
                            sp.dma_start(xt[0][0:NS, :], cfg["xs"]).then_inc(x_loaded[0], 16)
                    store(n // 2, n % 2, n)
                sp.wait_ge(out_ready.sem, out_ready.done(NT))
                sp.dma_start(cfg["out"][SEQ:SEQ + NS, :], yn[0][0:NS, :]).then_inc(stored[0], 16)
                sp.wait_ge(stored[0], 16 * (NT // 2 + 2))
                sp.wait_ge(stored[1], 16 * (NT // 2 + 1))

            @block.tensor
            def _(pe):
                def transposes(n, par, i_n):
                    if merge and not (isinstance(n, int) and n == NT):
                        pe.wait_ge(merged.sem, merged.done(n))
                    pe.wait_ge(m_loaded[par], MAMT * (i_n + 1))
                    for half in range(2):
                        pe.wait_ge(t_free.sem, t_free.done(n, half, back=2))
                        rows = NS if isinstance(n, int) and n == NT else P
                        for j in range(4):
                            c = (4 * half + j) * P
                            last = pe.transpose(ps_t[half][:, j * P:j * P + rows], mixt[par][0:rows, c:c + P], ident[0:rows, 0:rows])
                        last.then_inc(t_full.sem, 1)

                def project(n, par):
                    pe.wait_ge(t_free.sem, t_free.done(n, 1))
                    for c in range(2):
                        pe.wait_ge(y_free.sem, y_free.done(n, c, back=4))
                        for k in range(KT):
                            for q, (mp, wp) in enumerate(split_passes((mT[par][0], wo[0]), (mT[par][1], wo[1]))):
                                last = pe.matmul(ps_y[2 * par + c][:, :], mp[:, k, :], wp[:, k, c * 512:(c + 1) * 512],
                                                 start=(k == 0 and q == 0), stop=(k == KT - 1 and q == 2))
                        last.then_inc(y_full.sem, 1)

                transposes(0, 0, 0)
                pe.wait_ge(w_lo, 2)
                with pe.Fori(0, NT // 2 - 1) as i:
                    for par in range(2):
                        n = 2 * i + par
                        transposes(n + 1, par ^ 1, i + par)
                        project(n, par)
                for n in range(NT - 2, NT + 1):
                    if n < NT:
                        transposes(n + 1, (n + 1) % 2, (n + 1) // 2)
                    project(n, n % 2)

            @block.scalar
            def _(act):
                def transposed(n, par, rows=P):
                    for half in range(2):
                        act.wait_ge(t_full.sem, t_full.done(n, half))
                        nc.scalar.copy(mT[par][0][:, 4 * half:4 * half + 4, 0:rows],
                                       ps_t[half][:, :].rearrange("p (k t) -> p k t", t=P)[:, :, 0:rows]).then_inc(m_hi.sem, 1)

                def weights(n):
                    if merge:
                        act.wait_ge(delta_ready.sem, delta_ready.done(n))
                        nc.scalar.activation(dl[:, :, :], dl[:, :, :], ACT.Exp, scale=SCALE).then_inc(exp_done.sem, 1)

                act.wait_ge(cfg["w_sem"], 16)
                for c in range(2):
                    cs = slice(c * 512, (c + 1) * 512)
                    nc.scalar.copy(wo[0][:, :, cs], W[:, :, cs]).then_inc(w_hi, 1)
                weights(0)
                transposed(0, 0)
                weights(1)
                with act.Fori(0, NT // 2 - 1) as i:
                    for par in range(2):
                        n = 2 * i + par
                        transposed(n + 1, par ^ 1)
                        weights(n + 2)
                        root(nc, act, t, P, ln_ready, log_done, rstd_ready, n)
                for n in range(NT - 2, NT + 1):
                    if n < NT:
                        transposed(n + 1, (n + 1) % 2, P if n + 1 < NT else NS)
                    root(nc, act, t, P if n < NT else NS, ln_ready, log_done, rstd_ready, n)

            @block.gpsimd
            def _(pool):
                pool.sem_inc(t_free.sem, 2)
                pool.sem_inc(y_free.sem, 4)
                pool.sem_inc(normed.sem, 1)
                for par in range(2):
                    pool.sem_inc(stored[par], 16)
                pool.wait_ge(gb_loaded, 32)

                def gain(n, par, rows=P):
                    pool.wait_ge(normed.sem, normed.done(n))
                    hold(pool)
                    o = yn[par][0:rows, :]
                    pool.tensor_tensor(o, o, gb[0:rows, :], ALU.mult).then_inc(gained.sem, 1)
                    pool.wait_ge(gained.sem, gained.done(n))
                    pool.tensor_tensor(o, o, bb[0:rows, :], ALU.add).then_inc(out_ready.sem, 1)

                gained = Count(sem("gained"))
                with pool.Fori(0, NT // 2) as i:
                    for par in range(2):
                        gain(2 * i + par, par)
                gain(NT, 0, NS)

            @block.vector
            def _(dve):
                MERGE_LINKS = 7 if merge else 0
                steps, base, per_pair = [0], [0], 2 * (MERGE_LINKS + LN_LINKS + 1)

                def link(ins):
                    steps[0] += 1
                    ins.then_inc(step, 1)
                    dve.wait_ge(step, base[0] + steps[0])

                def merge_tile(n, par, i_n):
                    if not merge:
                        return
                    dve.wait_ge(m_loaded[par], MAMT * (i_n + 1))
                    mx = og[par][:, :, WB:WB + HB]
                    link(dve.tensor_tensor(top[:, :], mx[:, 0, :], mx[:, 1, :], ALU.max))
                    link(dve.tensor_tensor(top[:, :], top[:, :], mx[:, 2, :], ALU.max))
                    dve.tensor_tensor(dl[:, :, :], mx, top[:, :].rearrange("p (o h) -> p o h", o=1).broadcast_to([P, NG, HB]),
                                      ALU.subtract).then_inc(delta_ready.sem, 1)
                    dve.wait_ge(exp_done.sem, exp_done.done(n))
                    link(dve.tensor_tensor(ed[:, :, :], dl[:, :, :], og[par][:, :, WB + HB:WB + 2 * HB], ALU.mult))
                    link(dve.tensor_reduce(tot[:, :], ed[:, :, :].rearrange("p g h -> p h g"), AX.X, ALU.add))
                    link(dve.reciprocal(rt[:, :], tot[:, :]))
                    link(dve.tensor_tensor(cw[:, :, :], dl[:, :, :], rt[:, :].rearrange("p (o h) -> p o h", o=1).broadcast_to([P, NG, HB]), ALU.mult))
                    dst = [mixt[par][:, WA:D], part[0][:, :], part[1][:, :]]
                    for g in range(NG):
                        last = dve.tensor_tensor(dst[g].rearrange("p (h d) -> p h d", d=DH),
                                                 og[par][:, g, 0:WB].rearrange("p (h d) -> p h d", d=DH),
                                                 cw[:, g, :].rearrange("p (h o) -> p h o", o=1).broadcast_to([P, HB, DH]), ALU.mult)
                    link(last)
                    dve.tensor_tensor(part[0][:, :], part[0][:, :], part[1][:, :], ALU.add).then_inc(summed.sem, 1)
                    dve.wait_ge(summed.sem, summed.done(n))
                    dve.tensor_tensor(mixt[par][:, WA:D], mixt[par][:, WA:D], part[0][:, :], ALU.add).then_inc(merged.sem, 1)

                def rest(n, par, rows=P):
                    for half in range(2):
                        dve.wait_ge(m_hi.sem, m_hi.done(n, half))
                        ks = slice(4 * half, 4 * half + 4)
                        dve.tensor_tensor(mT[par][1][:, ks, 0:rows], ps_t[half][:, :].rearrange("p (k t) -> p k t", t=P)[:, :, 0:rows],
                                          mT[par][0][:, ks, 0:rows].bitcast(F32), ALU.subtract).then_inc(t_free.sem, 1)

                def norm_tile(n, par, i, rows=P):
                    dve.wait_ge(x_loaded[par], 16 * (i + 1))
                    dve.wait_ge(normed.sem, normed.done(n, back=1))
                    for c in range(2):
                        dve.wait_ge(y_full.sem, y_full.done(n, c))
                        cs = slice(c * 512, (c + 1) * 512)
                        dve.scalar_tensor_tensor(out=y[0:rows, cs], in0=xt[par][0:rows, cs], scalar=ALPHA, in1=ps_y[2 * par + c][0:rows, :],
                                                 op0=ALU.mult, op1=ALU.add).then_inc(y_free.sem, 1)
                    dve.wait_ge(y_free.sem, y_free.done(n, 1))
                    dve.wait_ge(stored[par], 16 * (i + 1))
                    layer_norm(nc, dve, link, t, rows, y[0:rows, :], ln_ready, rstd_ready, n, yn[par][0:rows, :], normed.sem)

                summed = Count(sem("summed"))
                for c in range(2):
                    cs = slice(c * 512, (c + 1) * 512)
                    dve.wait_ge(w_hi, c + 1)
                    dve.tensor_tensor(wo[1][:, :, cs], W[:, :, cs], wo[0][:, :, cs].bitcast(F32), ALU.subtract).then_inc(w_lo, 1)
                merge_tile(0, 0, 0)
                rest(0, 0)
                merge_tile(1, 1, 0)
                before = steps[0]
                per_pair = before + 2 * LN_LINKS
                with dve.Fori(0, NT // 2 - 1) as i:
                    base[0], steps[0] = i * per_pair + before, 0
                    for par in range(2):
                        rest(2 * i + par + 1, par ^ 1)
                        merge_tile(2 * i + par + 2, par, i + 1)
                        norm_tile(2 * i + par, par, i)
                    assert steps[0] == per_pair, (steps[0], per_pair)
                base[0], steps[0] = (NT // 2 - 1) * per_pair + before, 0
                for n in range(NT - 2, NT + 1):
                    if n < NT:
                        rest(n + 1, (n + 1) % 2, P if n + 1 < NT else NS)
                    norm_tile(n, n % 2, n // 2, P if n < NT else NS)


NTOK = SEQ + NS
NPAD = (NT + 1) * P
TOK_CHUNKS = [(0, 384), (384, 384), (768, 320)]
FG = 256
NFG = FF // FG
FT = FG // P


@own_semaphores
def mlp(nc, env, name, cfg):
    cst = env["cst"]
    ident = cst("ident")
    NTT = NT + 1
    UP, DN = FT * len(TOK_CHUNKS), 2 * NTT
    up_v = cfg["w_up"].rearrange("(k p) (j n) -> j p k n", p=P, n=FG)
    dn_v = cfg["w_down"].rearrange("(j f p) n -> j p f n", p=P, f=FT)
    with ExitStack() as ctx:
        def sb(nm, shape, dt=F32):
            return ctx.enter_context(nc.sbuf_tensor(f"{name}_{nm}", shape, dt))

        def ps(nm):
            return ctx.enter_context(nc.psum_tensor(f"{name}_{nm}", [P, 512], F32))

        def sem(nm):
            return env["sems"].enter_context(nc.semaphore(f"{name}_{nm}"))

        up_raw, dn_raw = sb("up_raw", [P, KT, FG]), sb("dn_raw", [P, FT, D])
        up = [sb(f"up_{x}", [P, KT, FG], F32R) for x in ("hi", "lo")]
        dn = [sb(f"dn_{x}", [P, FT, D], F32R) for x in ("hi", "lo")]
        xT = [sb(f"xT_{x}", [P, KT, NTOK], F32R) for x in ("hi", "lo")]
        acc = sb("acc", [P, NTT, D])
        hT = [[sb(f"hT{i}_{x}", [P, FT, NPAD], F32R) for x in ("hi", "lo")] for i in range(2)]
        h = [sb(f"h{i}", [P, 384]) for i in range(3)]
        yn = [dn_raw[:, i, :] for i in range(2)]
        gb, bb = up_raw[:, 0:4, :].rearrange("p k n -> p (k n)"), up_raw[:, 4:8, :].rearrange("p k n -> p (k n)")
        t = ln_tiles(sb)
        ps_u = [ps(f"ps_u{i}") for i in range(4)]
        ps_d = [ps(f"ps_d{i}") for i in range(4)]
        x_loaded = [sem(f"x_loaded{i}") for i in range(2)]
        stored = [sem(f"stored{i}") for i in range(2)]
        up_loaded, dn_loaded = sem("up_loaded"), sem("dn_loaded")
        gb_loaded, step, cleared = sem("gb_loaded"), sem("step"), sem("cleared")
        t_full, t_free, x_split, scaled = sem("t_full"), sem("t_free"), sem("x_split"), sem("scaled")
        up_hi, up_lo, dn_hi, dn_lo = (Count(sem(x)) for x in ("up_hi", "up_lo", "dn_hi", "dn_lo"))
        u_full, relu_done, squared = Count(sem("u_full"), UP), Count(sem("relu_done"), UP, credit=3), Count(sem("squared"), UP)
        h_hi, h_lo = Count(sem("h_hi"), UP), Count(sem("h_lo"), UP, credit=3)
        d_full, d_free = Count(sem("d_full"), DN), Count(sem("d_free"), DN, credit=4)
        ln_ready, log_done, rstd_ready, normed, gained, out_ready = (
            Count(sem(x)) for x in ("ln_ready", "log_done", "rstd_ready", "normed", "gained", "out_ready"))

        def rows_of(n):
            return P if n < NT else NS

        def as32(ap):
            return ap.bitcast(F32)

        with nc.Block() as block:
            @block.sync
            def _(sp):
                def load_up(n):
                    sp.dma_start(up_raw[:, :, :], up_v[n]).then_inc(up_loaded, 16)

                def load_dn(n):
                    sp.dma_start(dn_raw[:, :, :], dn_v[n]).then_inc(dn_loaded, 16)

                for n in range(NTT):
                    if n >= 2:
                        sp.wait_ge(t_full, 2 * n - 2)
                        sp.wait_ge(scaled, n - 1)
                    sp.dma_start(yn[n % 2][0:rows_of(n), :], cfg["x"][n * P:n * P + rows_of(n), :]).then_inc(x_loaded[n % 2], 16)
                    if n == 1:
                        load_up(0)
                sp.wait_ge(t_full, 2 * NTT)
                sp.wait_ge(scaled, NTT)
                load_dn(0)
                with sp.Fori(0, NFG - 1) as i:
                    sp.wait_ge(up_lo.sem, up_lo.done(i))
                    load_up(i + 1)
                    sp.wait_ge(dn_lo.sem, dn_lo.done(i))
                    load_dn(i + 1)
                sp.wait_ge(up_lo.sem, up_lo.done(NFG - 1))
                sp.dma_start(gb, cfg["g"].to_broadcast([P, D])).then_inc(gb_loaded, 16)
                sp.dma_start(bb, cfg["b"].to_broadcast([P, D])).then_inc(gb_loaded, 16)
                for n in range(NTT):
                    sp.wait_ge(out_ready.sem, out_ready.done(n))
                    sp.dma_start(cfg["out"](n), yn[n % 2][0:rows_of(n), :]).then_inc(stored[n % 2], 16)
                sp.wait_ge(stored[0], 16 * (NTT // 2 + 1))
                sp.wait_ge(stored[1], 16 * (NTT // 2))

            @block.tensor
            def _(pe):
                for n in range(NTT):
                    rows = rows_of(n)
                    pe.wait_ge(x_loaded[n % 2], 16 * (n // 2 + 1))
                    for half in range(2):
                        if n >= 2:
                            pe.wait_ge(x_split, 2 * (n - 2) + half + 1)
                        for j in range(4):
                            c = (4 * half + j) * P
                            last = pe.transpose(ps_u[2 * (n % 2) + half][:, j * P:j * P + rows], yn[n % 2][0:rows, c:c + P], ident[0:rows, 0:rows])
                        last.then_inc(t_full, 1)
                pe.wait_ge(x_split, 2 * NTT)

                def hidden(n):
                    pe.wait_ge(up_lo.sem, up_lo.done(n))
                    for f in range(FT):
                        for c, (t0, w) in enumerate(TOK_CHUNKS):
                            b = f * len(TOK_CHUNKS) + c
                            bank = ps_u[b % 3]
                            pe.wait_ge(relu_done.sem, relu_done.done(n, b, back=3))
                            for k in range(KT):
                                for q, (wp, xp) in enumerate(split_passes((up[0], xT[0]), (up[1], xT[1]))):
                                    last = pe.matmul(bank[:, 0:w], wp[:, k, f * P:(f + 1) * P], xp[:, k, t0:t0 + w],
                                                     start=(k == 0 and q == 0), stop=(k == KT - 1 and q == 2))
                            last.then_inc(u_full.sem, 1)

                def down(n, par):
                    pe.wait_ge(dn_lo.sem, dn_lo.done(n))
                    pe.wait_ge(h_lo.sem, h_lo.done(n, UP - 1))
                    for m in range(NTT):
                        for c in range(2):
                            b = 2 * m + c
                            pe.wait_ge(d_free.sem, d_free.done(n, b, back=4))
                            for f in range(FT):
                                for q, (hp, wp) in enumerate(split_passes((hT[par][0], dn[0]), (hT[par][1], dn[1]))):
                                    last = pe.matmul(ps_d[(par * DN + b) % 4][:, :], hp[:, f, m * P:(m + 1) * P],
                                                     wp[:, f, c * 512:(c + 1) * 512], start=(f == 0 and q == 0),
                                                     stop=(f == FT - 1 and q == 2))
                            last.then_inc(d_full.sem, 1)

                hidden(0)
                pe.wait_ge(cleared, 1)
                with pe.Fori(0, NFG // 2 - 1) as i:
                    for par in range(2):
                        hidden(2 * i + par + 1)
                        down(2 * i + par, par)
                hidden(NFG - 1)
                down(NFG - 2, 0)
                down(NFG - 1, 1)

            @block.scalar
            def _(act):
                def split_weights(n, raw, hi, loaded, used, ready):
                    act.wait_ge(loaded, 16 * (n + 1))
                    if used is not None:
                        act.wait_ge(*used)
                    nc.scalar.copy(hi[:, :, :].rearrange("p k n -> p (k n)"), raw[:, :, :].rearrange("p k n -> p (k n)"))\
                        .then_inc(ready.sem, 1)

                for n in range(NTT):
                    rows = rows_of(n)
                    for half in range(2):
                        act.wait_ge(t_full, 2 * n + half + 1)
                        nc.scalar.copy(xT[0][:, 4 * half:4 * half + 4, n * P:n * P + rows],
                                       ps_u[2 * (n % 2) + half][:, :].rearrange("p (k t) -> p k t", t=P)[:, :, 0:rows]).then_inc(t_free, 1)
                    if n == 2:
                        split_weights(0, up_raw, up[0], up_loaded, None, up_hi)
                split_weights(0, dn_raw, dn[0], dn_loaded, None, dn_hi)

                def step_(n, par, last=False):
                    for b in range(UP + 1):
                        if b < UP:
                            f, (t0, w) = b // len(TOK_CHUNKS), TOK_CHUNKS[b % len(TOK_CHUNKS)]
                            act.wait_ge(u_full.sem, u_full.done(n, b))
                            act.wait_ge(h_lo.sem, h_lo.done(n, b, back=3))
                            nc.scalar.activation(h[(par * UP + b) % 3][:, 0:w], ps_u[b % 3][:, 0:w], ACT.Relu)\
                                .then_inc(relu_done.sem, 1)
                        if b >= 1:
                            f, (t0, w) = (b - 1) // len(TOK_CHUNKS), TOK_CHUNKS[(b - 1) % len(TOK_CHUNKS)]
                            act.wait_ge(squared.sem, squared.done(n, b - 1))
                            nc.scalar.copy(hT[par][0][:, f, t0:t0 + w], h[(par * UP + b - 1) % 3][:, 0:w]).then_inc(h_hi.sem, 1)
                    if not last:
                        split_weights(n + 1, up_raw, up[0], up_loaded, (u_full.sem, u_full.done(n, UP - 1)), up_hi)

                def next_down(n):
                    split_weights(n + 1, dn_raw, dn[0], dn_loaded, (d_full.sem, d_full.done(n, DN - 1)), dn_hi)

                step_(0, 0)
                with act.Fori(0, NFG // 2 - 1) as i:
                    for par in range(2):
                        step_(2 * i + par + 1, par ^ 1)
                        next_down(2 * i + par)
                step_(NFG - 1, 1, last=True)
                next_down(NFG - 2)
                for n in range(NTT):
                    root(nc, act, t, rows_of(n), ln_ready, log_done, rstd_ready, n)

            @block.gpsimd
            def _(pool):
                pool.sem_inc(relu_done.sem, 3)
                pool.sem_inc(d_free.sem, 4)
                pool.sem_inc(h_lo.sem, 3)
                for par in range(2):
                    for part in range(2):
                        last = pool.memset(hT[par][part][:, :, NTOK:NPAD].bitcast(F32), 0.0)
                last.then_inc(cleared, 1)
                with pool.Fori(0, NFG // 2) as i:
                    for par in range(2):
                        n = 2 * i + par
                        for b in range(UP):
                            w = TOK_CHUNKS[b % len(TOK_CHUNKS)][1]
                            hs = h[(par * UP + b) % 3][:, 0:w]
                            pool.wait_ge(relu_done.sem, relu_done.done(n, b))
                            pool.tensor_tensor(hs, hs, hs, ALU.mult).then_inc(squared.sem, 1)
                pool.wait_ge(gb_loaded, 32)
                for n in range(NTT):
                    o = yn[n % 2][0:rows_of(n), :]
                    pool.wait_ge(normed.sem, normed.done(n))
                    pool.tensor_tensor(o, o, gb[0:rows_of(n), :], ALU.mult).then_inc(gained.sem, 1)
                    pool.wait_ge(gained.sem, gained.done(n))
                    pool.tensor_tensor(o, o, bb[0:rows_of(n), :], ALU.add).then_inc(out_ready.sem, 1)

            @block.vector
            def _(dve):
                steps = [0]

                def link(ins):
                    steps[0] += 1
                    ins.then_inc(step, 1)
                    dve.wait_ge(step, steps[0])

                def rest(n, raw, parts, hi, lo):
                    dve.wait_ge(hi.sem, hi.done(n))
                    dve.tensor_tensor(parts[1][:, :, :], raw[:, :, :], as32(parts[0][:, :, :]), ALU.subtract).then_inc(lo.sem, 1)

                for n in range(NTT):
                    rows = rows_of(n)
                    dve.wait_ge(x_loaded[n % 2], 16 * (n // 2 + 1))
                    dve.tensor_scalar(acc[0:rows, n, :], yn[n % 2][0:rows, :], ALPHA, None, ALU.mult).then_inc(scaled, 1)
                    for half in range(2):
                        dve.wait_ge(t_free, 2 * n + half + 1)
                        dst = slice(4 * half, 4 * half + 4), slice(n * P, n * P + rows)
                        dve.tensor_tensor(xT[1][:, dst[0], dst[1]],
                                          ps_u[2 * (n % 2) + half][:, :].rearrange("p (k t) -> p k t", t=P)[:, :, 0:rows],
                                          as32(xT[0][:, dst[0], dst[1]]), ALU.subtract).then_inc(x_split, 1)
                    if n == 2:
                        rest(0, up_raw, up, up_hi, up_lo)
                rest(0, dn_raw, dn, dn_hi, dn_lo)
                dve.wait_ge(scaled, NTT)

                def hidden_rest(n, par, b):
                    f, (t0, w) = b // len(TOK_CHUNKS), TOK_CHUNKS[b % len(TOK_CHUNKS)]
                    dve.wait_ge(h_hi.sem, h_hi.done(n, b))
                    dve.tensor_tensor(hT[par][1][:, f, t0:t0 + w], h[(par * UP + b) % 3][:, 0:w],
                                      as32(hT[par][0][:, f, t0:t0 + w]), ALU.subtract).then_inc(h_lo.sem, 1)

                def add(n, par, m):
                    rows = rows_of(m)
                    for c in range(2):
                        b = 2 * m + c
                        dve.wait_ge(d_full.sem, d_full.done(n, b))
                        a = acc[0:rows, m, c * 512:(c + 1) * 512]
                        dve.tensor_tensor(a, a, ps_d[(par * DN + b) % 4][0:rows, :], ALU.add).then_inc(d_free.sem, 1)

                def hiddens(n, par, last=False):
                    for b in range(UP):
                        hidden_rest(n, par, b)
                    if not last:
                        rest(n + 1, up_raw, up, up_hi, up_lo)

                def adds(n, par):
                    dve.wait_ge(d_free.sem, d_free.done(n, 0, back=1))
                    for m in range(NTT):
                        add(n, par, m)

                hiddens(0, 0)
                with dve.Fori(0, NFG // 2 - 1) as i:
                    for par in range(2):
                        hiddens(2 * i + par + 1, par ^ 1)
                        adds(2 * i + par, par)
                        rest(2 * i + par + 1, dn_raw, dn, dn_hi, dn_lo)
                hiddens(NFG - 1, 1, last=True)
                adds(NFG - 2, 0)
                rest(NFG - 1, dn_raw, dn, dn_hi, dn_lo)
                dve.wait_ge(d_free.sem, d_free.done(NFG - 1, 0, back=1))
                for m in range(NTT):
                    add(NFG - 1, 1, m)
                    dve.wait_ge(d_free.sem, d_free.done(NFG - 1, 2 * m + 1))
                    if m >= 2:
                        dve.wait_ge(stored[m % 2], 16 * (m // 2))
                    layer_norm(nc, dve, link, t, rows_of(m), acc[0:rows_of(m), m, :], ln_ready, rstd_ready, m,
                               yn[m % 2][0:rows_of(m), :], normed.sem)


def program(nc, a, o):
    with ExitStack() as ctx:
        def dram(nm, shape):
            return nc.dram_tensor(nm, shape, F32, kind="Internal").ap()

        def sem(nm):
            return ctx.enter_context(nc.semaphore(nm))

        consts = ctx.enter_context(nc.sbuf_tensor("consts", [P, CONST.shape[1]], F32))
        front = ctx.enter_context(ExitStack())
        w_slot = [front.enter_context(nc.sbuf_tensor("w_slot0", [P, KT, 4 * WA + 2 * HA], F32)), front.enter_context(nc.sbuf_tensor("w_slot1", [P, KT, 3 * WB], F32))]

        def cst(nm, DRAM=False):
            c0, w = CONST_AT[nm]
            return (a["const"] if DRAM else consts)[:, c0:c0 + w]

        og = [dram(f"og{g}", (SEQ, SROW)) for g in range(NG)]
        zs = dram("zs", (NS, 3 * NG * WB))
        mix = dram("mix", (SEQ + NS, D))
        xp = a["x_prompt"][0]
        xs = a["x_sample"].rearrange("b t d -> (b t) d")
        w_in = a["w_in_ab"][0]
        const_loaded = sem("const_loaded")
        copied = sem("copied")
        env = {"cst": cst, "sems": ctx, "const_loaded": const_loaded}
        w_sems = {}

        def load_columns(eng, slot, name, ranges, src):
            w_sems[name] = []
            col = 0
            for c, (c0, width) in enumerate(ranges):
                s = sem(f"w_{name}{c}")
                w_sems[name].append(s)
                eng.dma_start(slot[:, :, col:col + width], src.rearrange("(k p) n -> p k n", p=P)[:, :, c0:c0 + width])\
                    .then_inc(s, 16)
                col += width

        def group_ranges(g):
            return [(QB0 + j * NG * WB + g * WB, WB) for j in range(3)]

        with nc.Block() as block:
            @block.sync
            def _(sp):
                sp.dma_start(consts[:, :], a["const"]).then_inc(const_loaded, 16)
                load_columns(sp, w_slot[0], "m", [(j * WA, WA) for j in range(4)] + [(4 * WA, 2 * HA)], w_in)
                sp.wait_ge(const_loaded, 16)

        mlstm(nc, env, dict(
            x=xp, xs=xs, w=w_slot[0], w_sems=w_sems["m"], bias=a["b_gate_ab"][0:1, :], out=mix,
            C_p=o[2][0, 0], C_s=o[3][0], n_p=o[4][0, 0], n_s=o[5][0], m_p=o[6][0, 0], m_s=o[7][0],
            C0=a["state_mlstm_C"][0], n0=a["state_mlstm_n"][0], m0=a["state_mlstm_m"][0],
            prefetch=lambda sp: load_columns(sp, w_slot[1], "g0", group_ranges(0), w_in)))

        def dilated(g):
            cache_in, out_p, out_s = a[f"cache_dil{g + 1}_kv"][0], o[8 + 2 * g][0, 0], o[9 + 2 * g][0]
            keep, rate = KEEP_P[g], RATES[g]
            out_rows = out_p.rearrange("s two h d -> s two (h d)")

            def kv_rows(i, par, which):
                if rate == 1:
                    return [out_rows[:, which, :]]
                if rate == 4:
                    return [out_rows.rearrange("(p j) two c -> j two p c", j=4)[i, which]]
                v = out_rows.rearrange("(p j four) two c -> four j two p c", j=4, four=4)
                return [v[2 * par, i, which], v[2 * par + 1, i, which]]

            def spread(sp, i, par):
                old = CACHE[g]
                kept = KEEP_S[g] - TD
                src = cache_in.rearrange("(b two) s x h d -> two b s (x h d)", two=2)[par, i, old - kept:old, :]
                dst = out_s.rearrange("(b two) s x h d -> two b s (x h d)", two=2)[par, i, 0:kept, :]
                sp.dma_start(dst, src).then_inc(copied, 16)

            def store_sample(sp, z, s):
                n = 0
                for j in range(3):
                    zc = z[0:NS, j * WB:(j + 1) * WB]
                    sp.dma_start(zs[:, (j * NG + g) * WB:(j * NG + g + 1) * WB], zc).then_inc(s, 16)
                    n += 1
                    if j:
                        dst = out_s.rearrange("b s x h d -> b s x (h d)")
                        for b in range(BD):
                            sp.dma_start(dst[b, KEEP_S[g] - TD:KEEP_S[g], j - 1, :], z[b * TD:(b + 1) * TD, j * WB:(j + 1) * WB])\
                                .then_inc(s, 16)
                            n += 1
                return n

            def prefetch(sp):
                if g + 1 < NG:
                    load_columns(sp, w_slot[g % 2], f"g{g + 1}", group_ranges(g + 1), w_in)

            attention(nc, env, f"g{g}", dict(
                heads=HB, widths=[WB] * 3, qw=WB, kw=WB, prev=rate < 16, rate=rate, sinks=None, x=xp, xs=xs,
                w=w_slot[(g + 1) % 2], w_sems=w_sems[f"g{g}"], mask="m_pair" if rate == 16 else "m_dil",
                mask_even_after=rate == 1, rope=a["rope"][g], out=og[g], out_norm=False,
                kv_tiles=("last", "odd", "all")[g], kv_rows=kv_rows, spread=spread, store_sample=store_sample,
                prefetch=prefetch))

        for g in range(NG):
            dilated(g)
        front.close()

        x_mid = [dram(f"x_mid{i}", (SEQ + NS, D)) for i in range(3)]
        zs_c = dram("zs_c", (NS, (HC + 2 * KVC) * DH))
        mix_c = dram("mix_c", (SEQ + NS, D))

        def after_mixing(layer, mixing, x_in, x_in_s, mix_in, og_in):
            with ExitStack() as inner:
                wo = inner.enter_context(nc.sbuf_tensor(f"wo{layer}", [P, KT, D], F32))
                wo_sem = sem(f"wo_loaded{layer}")
                w_o = a[("w_out_ab", "w_out_c")[layer]][0]

                def prefetch_wo(sp):
                    sp.dma_start(wo[:, :, :], w_o.rearrange("(k p) n -> p k n", p=P)).then_inc(wo_sem, 16)

                mixing(prefetch_wo)
                output_projection(nc, env, f"p{layer}", dict(
                    merge=layer == 0, w=wo, w_sem=wo_sem, x=x_in, xs=x_in_s, mix=mix_in, og=og_in, out=x_mid[2 * layer],
                    g=a["ln1_g"][layer:layer + 1, :], b=a["ln1_b"][layer:layer + 1, :]))
            if layer == 0:
                def out(n):
                    return x_mid[1][n * P:n * P + (P if n < NT else NS), :]
            else:
                def out(n):
                    return o[0][0, n * P:(n + 1) * P, :] if n < NT else o[1].rearrange("b t d -> (b t) d")
            mlp(nc, env, f"f{layer}", dict(x=x_mid[2 * layer], w_up=a["w_up"][layer], w_down=a["w_down"][layer], out=out,
                                          g=a["ln2_g"][layer:layer + 1, :], b=a["ln2_b"][layer:layer + 1, :]))

        def sample_dilated(prefetch_wo):
            sample_attention(nc, env, dict(
                caches=[a[f"cache_dil{g + 1}_kv"][0] for g in range(NG)], zs=zs, out=mix[SEQ:SEQ + NS, WA:D],
                prefetch=prefetch_wo))

        def windowed(prefetch_wo):
            out_p = o[14][0, 0].rearrange("s x h d -> s x (h d)")
            out_s = o[15][0].rearrange("b s x h d -> b s (x h d)")
            cache = a["cache_swa_kv"][0]
            def spread(sp, i, par):
                v = cache.rearrange("(b two) s x h d -> two b s (x h d)", two=2)
                sp.dma_start(out_s.rearrange("(b two) s c -> two b s c", two=2)[par, i, 0:P - TD, :], v[par, i, TD:P, :])\
                    .then_inc(copied, 16)

            def store_sample(sp, z, s):
                sp.dma_start(zs_c, z[0:NS, 0:(HC + 2 * KVC) * DH]).then_inc(s, 16)
                for b in range(BD):
                    sp.dma_start(out_s[b, P - TD:P, :], z[b * TD:(b + 1) * TD, HC * DH:(HC + 2 * KVC) * DH]).then_inc(s, 16)
                return BD + 1

            with nc.sbuf_tensor("w_c", [P, KT, (HC + 2 * KVC) * DH], F32) as w_c:
                with nc.Block() as block:
                    @block.sync
                    def _(sp):
                        load_columns(sp, w_c, "c", [(0, 512), (512, 512), (1024, 256)], a["w_in_c"][0])

                attention(nc, env, "c", dict(
                    heads=HC, widths=[512, 512, 256], qw=HC * DH, kw=KVC * DH, prev=True, rate=1, sinks=a["sinks_c"][0:1, :],
                    x=x_mid[1][0:SEQ, :], xs=x_mid[1][SEQ:SEQ + NS, :], w=w_c, w_sems=w_sems["c"], mask="m_swa",
                    mask_even_after=True, rope=a["rope"][0], out=mix_c[0:SEQ, :], out_norm=True, kv_tiles="last",
                    kv_rows=lambda i, par, which: [out_p[:, which, :]], spread=spread, store_sample=store_sample,
                    prefetch=prefetch_wo))
            swa_sample(nc, env, dict(cache=cache, zs=zs_c, out=mix_c[SEQ:SEQ + NS, :], sinks=a["sinks_c"][0:1, :]))

        after_mixing(0, sample_dilated, xp, xs, mix, og)
        after_mixing(1, windowed, x_mid[1][0:SEQ, :], x_mid[1][SEQ:SEQ + NS, :], mix_c, None)

        with nc.Block() as block:
            @block.sync
            def _(sp):
                sp.wait_ge(copied, 16 * (NG + 1) * BD)


OUTS = [(1, SEQ, D), (BD, TD, D), (1, 1, HA, DA, DA), (1, BD, HA, DA, DA), (1, 1, HA, DA), (1, BD, HA, DA), (1, 1, HA),
        (1, BD, HA)]
for _g in range(NG):
    OUTS += [(1, 1, KEEP_P[_g], 2, HB, DH), (1, BD, KEEP_S[_g], 2, HB, DH)]
OUTS += [(1, 1, P, 2, KVC, DH), (1, BD, P, 2, KVC, DH)]
INS = ["x_prompt", "x_sample", "state_mlstm_C", "state_mlstm_n", "state_mlstm_m", "cache_dil1_kv", "cache_dil2_kv",
       "cache_dil3_kv", "cache_swa_kv", "w_in_ab", "b_gate_ab", "w_out_ab", "w_in_c", "sinks_c", "w_out_c",
       "ln1_g", "ln1_b", "ln2_g", "ln2_b", "w_up", "w_down"]


def kernel(**inputs):
    import concourse.bacc as bacc
    from concourse.bass_utils import run_bass_kernel_spmd

    nc = bacc.Bacc("TRN2", target_bir_lowering=False, num_devices=1)
    arrays = {n: np.ascontiguousarray(inputs[n]) for n in INS}
    arrays["const"] = CONST
    arrays["rope"] = ROPE
    a = {n: nc.dram_tensor(f"in_{n}", v.shape, F32, kind="ExternalInput").ap() for n, v in arrays.items()}
    o = [nc.dram_tensor(f"out_{i}", s, F32, kind="ExternalOutput").ap() for i, s in enumerate(OUTS)]
    program(nc, a, o)
    r = run_bass_kernel_spmd(nc, [{f"in_{n}": v for n, v in arrays.items()}], core_ids=[0])
    return tuple(r.results[0][f"out_{i}"] for i in range(len(OUTS)))
```

```python
from contextlib import ExitStack

import numpy as np

import concourse.bass as bass
from concourse import mybir

F32 = mybir.dt.float32
F32R = mybir.dt.float32r
ALU = mybir.AluOpType
ACT = mybir.ActivationFunctionType
AX = mybir.AxisListType

P = 128
D = 1024
KT = D // P
SEQ = 1024
NT = SEQ // P
BD, TD = 8, 8
NS = BD * TD
PAST = 1024
HA, DA = 4, 128
WA = HA * DA
HB, DH = 8, 64
WB = HB * DH
NG = 3
RATES = (1, 4, 16)
KEEP_P = (128, 512, 1024)
CACHE = (128, 512, 1024)
KEEP_S = (128, 512, 1032)
HC, KVC = 16, 2
FF = 4096
ALPHA = 4.0 ** 0.25
EPS = 1e-5
SCALE = DH ** -0.5
NEG = -1e30
SROW = WB + 2 * HB
IN_AB = 4 * WA + 2 * HA + 3 * NG * WB
QB0 = 4 * WA + 2 * HA


def constants():
    c = {}
    q, k = np.arange(P)[:, None], np.arange(P)[None, :]
    off = np.full((P, P), NEG)
    cur = np.where(k <= q, 0.0, NEG)
    c["ident"] = np.eye(P)
    c["m_dil"] = np.concatenate([np.where(k >= q, 0.0, NEG), cur], 1)
    c["m_swa"] = np.concatenate([np.where(k > q, 0.0, NEG), cur], 1)
    c["m_first"] = np.concatenate([off, cur], 1)
    c["m_pair"] = np.concatenate([off, np.where((k <= q) & (k // 64 == q // 64), 0.0, NEG)], 1)
    c["m_causalT"] = cur.T
    c["m_sampleT"] = np.full((P, NS), NEG)
    s = np.arange(NS)
    c["m_sampleT"][:NS] = np.where((s[:, None] <= s[None, :]) & (s[:, None] // TD == s[None, :] // TD), 0.0, NEG)
    inv = 500000.0 ** (-np.arange(8, dtype=np.float32) / np.float32(8))

    def rope(pos):
        ang = pos.astype(np.float32)[..., None] * inv.astype(np.float32)
        co, si = np.cos(ang), np.sin(ang)
        return np.concatenate([co, co, -si, si], -1)

    n, p = np.arange(NT)[:, None], np.arange(P)[None, :]
    tok = [n * P + p, n // 2 + 4 * (P * (n % 2) + p), 2 * n + p // 64 + 16 * (p % 64)]
    rp = np.stack([rope(t) for t in tok])
    rs = np.zeros((P, 32))
    rs[:NS] = rope(PAST + s % TD)
    c["rope_s"] = rs
    sel = np.zeros((P, HA * P))
    for h in range(HA):
        sel[h, h * P:(h + 1) * P] = 1
    c["sel"] = sel
    c["ones"] = np.ones((P, P))
    blk = np.zeros((P, BD))
    blk[s, s // TD] = 1
    c["blk"] = blk
    r = np.arange(NS)
    h, t = (r // TD)[:, None], (r % TD)[:, None]
    kk = np.arange(P)[None, :]
    ms = [np.where(kk >= t, 0.0, NEG)]
    for j in range(4):
        ms.append(np.where((t % 4 == j) & ((t < 4) | (kk > 0)), 0.0, NEG))
    for j in range(4):
        ms.append(np.where((t % 4 == j) & (t // 4 == kk // 64), 0.0, NEG))
    u = np.arange(TD)[None, :]
    ms += [np.where(u <= t, 0.0, NEG), np.where((u <= t) & ((t - u) % 4 == 0), 0.0, NEG), np.where(u == t, 0.0, NEG)]
    m = np.zeros((P, 9 * P + 3 * TD))
    m[:NS] = np.concatenate(ms, 1)
    c["m_samp"] = m
    dg = np.zeros((P, HB))
    dg[r, r // TD] = 1
    c["diag"] = dg
    hm = np.zeros((P, 4, HB, TD))
    for uu in range(4):
        hm[:64, uu, 2 * uu] = 1
        hm[64:, uu, 2 * uu + 1] = 1
    c["headsel"] = hm.reshape(P, -1)
    t = (np.arange(P) % TD)[:, None]
    c["m_swas"] = np.concatenate([np.where(kk >= t + 1, 0.0, NEG), np.where(u <= t, 0.0, NEG)], 1)
    for late in ("m_samp", "headsel"):
        c[late] = c.pop(late)
    at, cols = {}, 0
    for name, a in c.items():
        at[name] = (cols, a.shape[1])
        cols += a.shape[1]
    table = np.concatenate([a for a in c.values()], 1).astype(np.float32)
    return table, at, rp.astype(np.float32)


CONST, CONST_AT, ROPE = constants()
RESIDENT = CONST_AT["m_samp"][0]


class Count:

    def __init__(self, sem, per=1, credit=0, pre=0):
        self.sem, self.per, self.credit, self.pre = sem, per, credit, pre

    def done(self, n, c=0, back=0):
        return n * self.per + (self.credit + self.pre + c + 1 - back)


def hold(eng):
    eng.nop(nofuse=True)


class Phase:

    def __init__(self, nc, env):
        self.nc, self.env, self.stack, self.given = nc, env, ExitStack(), []

    def enter_context(self, manager):
        self.given.append(self.stack.enter_context(manager))
        return self.given[-1]

    def __enter__(self):
        self.env["sems"] = self
        return self

    def __exit__(self, *error):
        if not error[0]:
            with self.nc.Block() as block:
                @block.sync
                def _(sp):
                    for s in self.given:
                        sp.sem_clear(s)
        self.stack.close()
        return False


def own_semaphores(phase):
    def run(nc, env, *more):
        with Phase(nc, env):
            phase(nc, env, *more)
    return run


def row_tiles(t, rate, n_half, par):
    if rate == 1:
        return [t.rearrange("(n two p) c -> two n p c", two=2, p=P)[par, n_half]]
    if rate == 4:
        return [t.rearrange("(b p j) c -> b j p c", j=4, b=2)[par, n_half]]
    v = t.rearrange("(p j four) c -> four j p c", j=4, four=4)
    return [v[2 * par, n_half], v[2 * par + 1, n_half]]


def halves(tile, parts):
    return [tile] if len(parts) == 1 else [tile[0:64], tile[64:128]]


def split_passes(hi, lo):
    return [(hi[0], hi[1]), (hi[0], lo[1]), (lo[0], hi[1])]


@own_semaphores
def attention(nc, env, name, cfg):
    H, widths, prev, rate = cfg["heads"], cfg["widths"], cfg["prev"], cfg["rate"]
    swa = cfg["sinks"] is not None
    QW, KW = cfg["qw"], cfg["kw"]
    ZW = sum(widths)
    NCH = len(widths)
    QT = QW // P
    UT = 2 if swa else KW // P
    NROPE = (QW + KW) // DH
    NK = 2 * P if prev else P
    K0 = 0 if prev else P
    PAIRS = H // 2
    jobs = [[(0, t) for t in range(a, a + 4)] for a in range(0, QT, 4)] + [[(1, u) for u in range(UT)]]
    NQK = len(jobs)
    U = NQK + 2 + PAIRS
    NX = 2 if rate == 16 else 1
    XAMT = 16 * (NX + 1)
    W, w_sems = cfg["w"], cfg["w_sems"]
    cst = env["cst"]
    ident = cst("ident")

    with ExitStack() as ctx:
        def sb(nm, shape, dt=F32):
            return ctx.enter_context(nc.sbuf_tensor(f"{name}_{nm}", shape, dt))

        def ps(nm):
            return ctx.enter_context(nc.psum_tensor(f"{name}_{nm}", [P, 512], F32))

        def sem(nm):
            return env["sems"].enter_context(nc.semaphore(f"{name}_{nm}"))

        def staged(c):
            return W[:, :, c % 2 * 512:c % 2 * 512 + widths[c]]

        xn = [sb(f"xn{i}", [P, D]) for i in range(2)]
        rt = [sb(f"rt{i}", [P, 32]) for i in range(2)]
        xT = [[sb(f"xT{i}_{x}", [P, KT, P], F32R) for x in ("hi", "lo")] for i in range(2)]
        w_parts = [sb(f"w_{x}", [P, KT, ZW], F32R) for x in ("hi", "lo")]
        halves_of_k = [slice(0, KT // 2), slice(KT // 2, KT)]
        z = [sb(f"z{i}", [P, ZW + (P if swa else 0)]) for i in range(2)]
        qT = sb("qT", [P, QT, P])
        kT = [sb(f"kT{i}", [P, UT, P]) for i in range(2)]
        VW = ZW - QW - KW
        vb = [sb(f"vb{i}", [P, VW]) for i in range(2)]
        prob = sb("prob", [P, H, NK])
        pT = sb("pT", [P, PAIRS, 4 if prev else 2, P])
        osb = [sb(f"o{i}", [P, H * DH + 2 * H]) for i in range(2)]
        nmx = sb("nmx", [P, H])
        rot = sb("rot", [P, 2 * NROPE * 16])
        mask_even = sb("mask_even", [P, 2 * P])
        if swa:
            sinkb = sb("sinkb", [P, H])
            sink8 = sb("sink8", [P, H])
            sk = sb("sk", [P, H])
            rden = sb("rden", [P, H])
        mask_odd = cst(cfg["mask"])
        ps_z = [ps(f"ps_z{i}") for i in range(2)]
        ps_t = [ps(f"ps_t{i}") for i in range(2)]
        ps_s = [ps(f"ps_s{i}") for i in range(2)]
        ps_o = [ps(f"ps_o{i}") for i in range(H * DH // 512)]

        x_loaded = [sem(f"x_loaded{i}") for i in range(2)]
        o_stored = [sem(f"o_stored{i}") for i in range(2)]
        kv_stored = [sem(f"kv_stored{i}") for i in range(2)]
        s_stored = sem("s_stored")
        sink_loaded = sem("sink_loaded")
        t_full = Count(sem("t_full"), U, pre=2)
        t_free = Count(sem("t_free"), U, pre=2, credit=2)
        x_hi, w_hi, w_lo = Count(sem("x_hi"), 2, pre=2), sem("w_hi"), sem("w_lo")
        z_full = Count(sem("z_full"), NCH)
        z_free = Count(sem("z_free"), NCH, credit=2)
        s_full = Count(sem("s_full"), PAIRS)
        s_free = Count(sem("s_free"), PAIRS, credit=2)
        max_ready = Count(sem("max_ready"), H // 4)
        exp_done = Count(sem("exp_done"), PAIRS)
        sk_ready = Count(sem("sk_ready"), 1)
        sink_done = Count(sem("sink_done"), 1)
        roped = Count(sem("roped"), 1)
        v_ready = Count(sem("v_ready"), 1, credit=1)
        o_full = Count(sem("o_full"), 1, credit=1)
        o_free = Count(sem("o_free"), 1, credit=1)
        cleared = sem("cleared")
        dve_step = sem("dve_step")
        KVAMT = 32 * NX if cfg["kv_tiles"] != "last" else 0

        block = ctx.enter_context(nc.Block())

        @block.sync
        def _(sp):
            def load(i, par):
                parts = row_tiles(cfg["x"], rate, i, par)
                for dst, src in zip(halves(xn[par][:, :], parts), parts):
                    sp.dma_start(dst, src).then_inc(x_loaded[par], 16)
                sp.dma_start(rt[par][:, :], cfg["rope"].rearrange("(n two) p c -> two n p c", two=2)[par, i])\
                    .then_inc(x_loaded[par], 16)

            def load_sample():
                for a in range(NX):
                    rows = NS // NX
                    sp.dma_start(xn[0][a * rows:(a + 1) * rows, :], cfg["xs"][a * rows:(a + 1) * rows, :])\
                        .then_inc(x_loaded[0], 16)
                sp.dma_start(rt[0][0:NS, :], cst("rope_s", DRAM=True)[0:NS, :]).then_inc(x_loaded[0], 16)

            def store_kv(i, par):
                for which, col in ((0, QW), (1, QW + KW)):
                    parts = cfg["kv_rows"](i, par, which)
                    for src, dst in zip(halves(z[par][:, col:col + KW], parts), parts):
                        sp.dma_start(dst, src).then_inc(kv_stored[par], 16)

            def store_o(i, par, n):
                sp.wait_ge(o_free.sem, o_free.done(n))
                if cfg["out_norm"]:
                    parts, width = row_tiles(cfg["out"], rate, i, par), H * DH
                else:
                    parts, width = row_tiles(cfg["out"], rate, i, par), SROW
                for src, dst in zip(halves(osb[par][:, 0:width], parts), parts):
                    sp.dma_start(dst, src).then_inc(o_stored[par], 16)

            if swa:
                sp.dma_start(sinkb[:, :], cfg["sinks"].to_broadcast([P, H])).then_inc(sink_loaded, 16)
            load(0, 0)
            if swa:
                cfg["load_chunks"](sp, (0, 1))
            load(0, 1)
            sp.wait_ge(w_lo, 2)
            cfg["load_chunks"](sp, (2,))
            sp.wait_ge(w_lo, 2 * NCH)
            cfg["prefetch"](sp)

            def step(i, par, n, more):
                sp.wait_ge(roped.sem, roped.done(n))
                if KVAMT and (cfg["kv_tiles"] == "all" or par == 1):
                    store_kv(i, par)
                if par == 1 and not more and cfg["kv_tiles"] == "last":
                    store_kv(i, par)
                if more:
                    load(i + 1, par)
                elif par == 0:
                    load_sample()
                else:
                    sp.wait_ge(roped.sem, roped.done(NT))
                    cfg["store_sample"](sp, z[0], s_stored)
                    sp.wait_ge(s_stored, 16)
                    cfg["copy_sample"](sp)
                store_o(i, par, n)

            with sp.Fori(0, NT // 2 - 1) as i:
                for par in range(2):
                    cfg["spread"](sp, i, par)
                    step(i, par, 2 * i + par, True)
            for par in range(2):
                cfg["spread"](sp, NT // 2 - 1, par)
                step(NT // 2 - 1, par, NT - 2 + par, False)
            for par in range(2):
                sp.wait_ge(o_stored[par], 16 * NX * (NT // 2 + 1))
            if KVAMT:
                sp.wait_ge(kv_stored[1], KVAMT * (NT // 2 + 1))
                if cfg["kv_tiles"] == "all":
                    sp.wait_ge(kv_stored[0], KVAMT * (NT // 2 + 1))
            else:
                sp.wait_ge(kv_stored[1], 32 * NX)

        @block.tensor
        def _(pe):
            def transposes(n, c, bank, ins):
                pe.wait_ge(t_free.sem, t_free.done(n, c, back=2))
                for j, a in enumerate(ins):
                    last = pe.transpose(ps_t[bank][:, j * P:(j + 1) * P], a, ident)
                last.then_inc(t_full.sem, 1)

            def x_transposes(n, c, i_next, par):
                pe.wait_ge(x_loaded[par], XAMT * (i_next + 1))
                for half in range(2):
                    transposes(n, c + half, (bank_of(par ^ 1, c + half) if c >= 0 else half),
                               [xn[par][:, (4 * half + j) * P:(4 * half + j + 1) * P] for j in range(4)])

            def bank_of(par, c):
                return (par * U + c) % 2

            def project(n, par, xT_count):
                pe.wait_ge(t_free.sem, xT_count)
                col = 0
                for c, width in enumerate(widths):
                    pe.wait_ge(z_free.sem, z_free.done(n, c, back=2))
                    for k in range(KT):
                        if isinstance(n, int) and n == 0 and k % (KT // 2) == 0:
                            pe.wait_ge(w_lo, 2 * c + k // (KT // 2) + 1)
                        for q, (xp, wp) in enumerate(split_passes((xT[par][0], w_parts[0]), (xT[par][1], w_parts[1]))):
                            last = pe.matmul(ps_z[(par * NCH + c) % 2][:, 0:width], xp[:, k, :], wp[:, k, col:col + width],
                                             start=(k == 0 and q == 0), stop=(k == KT - 1 and q == 2))
                    last.then_inc(z_full.sem, 1)
                    col += width

            def step(i, par, n):
                pe.wait_ge(roped.sem, roped.done(n))
                for j, job in enumerate(jobs):
                    cols = [t * P if kind == 0 else QW + t * P for kind, t in job]
                    if swa and job[0][0] == 1:
                        cols = [QW, ZW]
                    transposes(n, j, bank_of(par, j), [z[par][:, a:a + P] for a in cols])
                x_transposes(n, NQK, i + par, par ^ 1)
                pe.wait_ge(t_free.sem, t_free.done(n, NQK - 1))
                for s in range(PAIRS):
                    r, a = s // 2, s % 2
                    pe.wait_ge(s_free.sem, s_free.done(n, s, back=2))
                    for j in range(2):
                        h = 4 * r + 2 * j + a
                        u = (0 if h // 8 == a else 1) if swa else h // 2
                        rows = slice(64 * a, 64 * a + 64)
                        out = ps_s[a][:, j * NK:(j + 1) * NK]
                        if prev:
                            pe.matmul(out[:, 0:P], qT[rows, h // 2, :], kT[par ^ 1][rows, u, :], start=True, stop=True)
                        last = pe.matmul(out[:, NK - P:NK], qT[rows, h // 2, :], kT[par][rows, u, :], start=True, stop=True)
                    last.then_inc(s_full.sem, 1)
                project(n + 1, par ^ 1, t_free.done(n, NQK + 1))
                pe.wait_ge(o_free.sem, o_free.done(n, back=1))
                pe.wait_ge(v_ready.sem, v_ready.done(n))
                nb = 4 if prev else 2
                for pr in range(PAIRS + 1):
                    if pr < PAIRS:
                        pe.wait_ge(exp_done.sem, exp_done.done(n, pr))
                        transposes(n, NQK + 2 + pr, bank_of(par, NQK + 2 + pr),
                                   [prob[:, 2 * pr + m // (nb // 2), (m % (nb // 2)) * P:(m % (nb // 2) + 1) * P]
                                    for m in range(nb)])
                    if pr >= 1:
                        pe.wait_ge(t_free.sem, t_free.done(n, NQK + 2 + pr - 1))
                        for hh in range(2):
                            h = 2 * (pr - 1) + hh
                            v0 = (h // 8 if swa else h) * DH
                            out = ps_o[h // 8][:, (h % 8) * DH:(h % 8 + 1) * DH]
                            if prev:
                                pe.matmul(out, pT[:, pr - 1, 2 * hh, :], vb[par ^ 1][:, v0:v0 + DH], start=True, stop=False)
                            last = pe.matmul(out, pT[:, pr - 1, (nb // 2) * hh + nb // 2 - 1, :], vb[par][:, v0:v0 + DH],
                                             start=not prev, stop=True)
                last.then_inc(o_full.sem, 1)

            x_transposes(0, -2, 0, 0)
            project(0, 0, t_free.done(0, -1))
            pe.wait_ge(cleared, 1)
            with pe.Fori(0, NT // 2) as i:
                for par in range(2):
                    step(i, par, 2 * i + par)

        @block.scalar
        def _(act):
            def evacuate(n, c, bank, dst, src=None):
                act.wait_ge(t_full.sem, t_full.done(n, c))
                nc.scalar.copy(dst, ps_t[bank][:, 0:512] if src is None else ps_t[bank][:, 0:src])\
                    .then_inc(t_free.sem, 1)

            def x_out(n, c, par):
                for half in range(2):
                    act.wait_ge(t_full.sem, t_full.done(n, c + half))
                    bank = ps_t[((par ^ 1) * U + c + half) % 2 if c >= 0 else half]
                    nc.scalar.copy(xT[par][0][:, halves_of_k[half], :].rearrange("p k t -> p (k t)"), bank[:, :]).then_inc(x_hi.sem, 1)

            def round_weights(c):
                act.wait_ge(w_sems[c], 16)
                col = sum(widths[:c])
                for ks in halves_of_k:
                    nc.scalar.copy(w_parts[0][:, ks, col:col + widths[c]], staged(c)[:, ks, :]).then_inc(w_hi, 1)

            if not swa:
                round_weights(0)
            x_out(0, -2, 0)
            for c in range(0 if swa else 1, NCH):
                round_weights(c)
            with act.Fori(0, NT // 2) as i:
                for par in range(2):
                    n = 2 * i + par
                    for j, job in enumerate(jobs):
                        kind, t0 = job[0]
                        dst = qT[:, t0:t0 + 4, :] if kind == 0 else kT[par][:, :, :]
                        evacuate(n, j, (par * U + j) % 2, dst.rearrange("p k t -> p (k t)"), len(job) * P)
                    x_out(n, NQK, par ^ 1)
                    for h in range(H):
                        if h % 4 == 0:
                            act.wait_ge(max_ready.sem, max_ready.done(n, h // 4))
                        e = nc.scalar.activation(prob[:, h, :], prob[:, h, :], ACT.Exp, bias=nmx[:, h:h + 1], scale=SCALE,
                                                 accum_out=osb[par][:, H * DH + H + h:H * DH + H + h + 1])
                        if h % 2:
                            e.then_inc(exp_done.sem, 1)
                    if swa:
                        act.wait_ge(sk_ready.sem, sk_ready.done(n))
                        nc.scalar.activation(sk[:, :], sk[:, :], ACT.Exp).then_inc(sink_done.sem, 1)
                    for pr in range(PAIRS):
                        evacuate(n, NQK + 2 + pr, (par * U + NQK + 2 + pr) % 2,
                                 pT[:, pr, :, :].rearrange("p k t -> p (k t)"), (4 if prev else 2) * P)

        @block.gpsimd
        def _(pool):
            pool.memset(kT[1][:, :, :], 0.0)
            pool.memset(vb[1][:, :], 0.0).then_inc(cleared, 1)
            for c, k in ((t_free, 2), (z_free, 2), (s_free, 2), (v_ready, 1), (o_full, 1), (o_free, 1)):
                pool.sem_inc(c.sem, k)
            for par in range(2):
                pool.sem_inc(o_stored[par], 16 * NX)
                if KVAMT and (par == 1 or cfg["kv_tiles"] == "all"):
                    pool.sem_inc(kv_stored[par], KVAMT)
            with pool.Fori(0, NT // 2) as i:
                for par in range(2):
                    n = 2 * i + par
                    pool.wait_ge(cleared, 1)
                    pool.wait_ge(roped.sem, roped.done(n))
                    pool.wait_ge(o_full.sem, o_full.done(n, back=1))
                    hold(pool)
                    pool.tensor_copy(vb[par][:, :], z[par][:, QW + KW:ZW]).then_inc(v_ready.sem, 1)

        @block.vector
        def _(dve):
            steps = [0]
            base = [0]

            def link(ins):
                steps[0] += 1
                ins.then_inc(dve_step, 1)
                dve.wait_ge(dve_step, base[0] + steps[0])

            def x_rest(n, c, par):
                for half in range(2):
                    dve.wait_ge(x_hi.sem, x_hi.done(n, half if c >= 0 else half - 2))
                    bank = ps_t[((par ^ 1) * U + c + half) % 2 if c >= 0 else half]
                    ks = halves_of_k[half]
                    dve.tensor_tensor(xT[par][1][:, ks, :], bank[:, :].rearrange("p (k t) -> p k t", t=P),
                                      xT[par][0][:, ks, :].bitcast(F32), ALU.subtract).then_inc(t_free.sem, 1)

            def z_out(n, par, i_next):
                col = 0
                if KVAMT and (cfg["kv_tiles"] == "all" or par == 1):
                    dve.wait_ge(kv_stored[par], KVAMT * (i_next + 1))
                dve.wait_ge(v_ready.sem, v_ready.done(n, back=2) if not isinstance(n, int) else 1)
                for c, width in enumerate(widths):
                    dve.wait_ge(z_full.sem, z_full.done(n, c))
                    last = dve.tensor_copy(z[par][:, col:col + width], ps_z[(par * NCH + c) % 2][:, 0:width])
                    last.then_inc(z_free.sem, 1)
                    col += width
                dve.wait_ge(z_free.sem, z_free.done(n, NCH - 1))
                dve.wait_ge(x_loaded[par], XAMT * (i_next + 1))
                zr = z[par][:, 0:NROPE * DH].rearrange("p (h d) -> p h d", d=DH)
                ra = rot[:, 0:NROPE * 16].rearrange("p (h d) -> p h d", d=16)
                rb = rot[:, NROPE * 16:2 * NROPE * 16].rearrange("p (h d) -> p h d", d=16)

                def tab(a, b):
                    return rt[par][:, a:b].rearrange("p (o d) -> p o d", o=1).broadcast_to([P, NROPE, b - a])

                dve.tensor_tensor(ra, zr[:, :, 0:16], tab(0, 16), ALU.mult)
                dve.tensor_tensor(rb[:, :, 0:8], zr[:, :, 8:16], tab(16, 24), ALU.mult)
                link(dve.tensor_tensor(rb[:, :, 8:16], zr[:, :, 0:8], tab(24, 32), ALU.mult))
                if not swa:
                    dve.tensor_tensor(zr[:, :, 0:16], ra, rb, ALU.add).then_inc(roped.sem, 1)
                    return
                link(dve.tensor_tensor(zr[:, :, 0:16], ra, rb, ALU.add))
                dve.tensor_copy(z[par][:, ZW:ZW + DH], z[par][:, QW + DH:QW + 2 * DH])
                dve.tensor_copy(z[par][:, ZW + DH:ZW + 2 * DH], z[par][:, QW:QW + DH]).then_inc(roped.sem, 1)

            if swa:
                dve.wait_ge(sink_loaded, 16)
                dve.tensor_scalar(sink8[:, :], sinkb[:, :], 1.0 / SCALE, None, ALU.mult)
            if prev:
                link(dve.tensor_copy(mask_even[:, :], cst("m_first")))
            def rest_of_weights(c):
                cols = slice(sum(widths[:c]), sum(widths[:c + 1]))
                for half, ks in enumerate(halves_of_k):
                    dve.wait_ge(w_hi, 2 * c + half + 1)
                    dve.tensor_tensor(w_parts[1][:, ks, cols], staged(c)[:, ks, :], w_parts[0][:, ks, cols].bitcast(F32),
                                      ALU.subtract).then_inc(w_lo, 1)

            if not swa:
                rest_of_weights(0)
            x_rest(0, -2, 0)
            for c in range(0 if swa else 1, NCH):
                rest_of_weights(c)
            z_out(0, 0, 0)
            before, per_pair = steps[0], 2 * (H // 4 + 4 if swa else 1) + (prev and cfg["mask_even_after"])
            with dve.Fori(0, NT // 2) as i:
                for par in range(2):
                    n = 2 * i + par
                    if par == 0:
                        base[0], steps[0] = i * per_pair + before, 0
                    mask = mask_odd if (par == 1 or not prev) else mask_even[:, :]
                    dve.wait_ge(t_full.sem, t_full.done(n, 0))
                    dve.wait_ge(o_stored[par], 16 * NX * (i + 1))
                    x_rest(n, NQK, par ^ 1)
                    for s in range(PAIRS):
                        r, a = s // 2, s % 2
                        dve.wait_ge(s_full.sem, s_full.done(n, s))
                        hold(dve)
                        for j in range(2):
                            h = 4 * r + 2 * j + a
                            last = dve.tensor_tensor_reduce(
                                out=prob[:, h, :], in0=ps_s[a][:, j * NK:(j + 1) * NK], in1=mask[:, K0:2 * P],
                                scale=1.0, scalar=NEG, op0=ALU.add, op1=ALU.max,
                                accum_out=osb[par][:, H * DH + h:H * DH + h + 1])
                        last.then_inc(s_free.sem, 1)
                        if a == 1:
                            hs = slice(4 * r, 4 * r + 4)
                            mx = osb[par][:, H * DH + 4 * r:H * DH + 4 * r + 4]
                            dve.wait_ge(s_free.sem, s_free.done(n, s))
                            if swa:
                                link(dve.tensor_tensor(mx, mx, sink8[:, hs], ALU.max))
                            dve.tensor_scalar(nmx[:, hs], mx, -SCALE, None, ALU.mult).then_inc(max_ready.sem, 1)
                    if swa:
                        dve.wait_ge(max_ready.sem, max_ready.done(n, H // 4 - 1))
                        dve.tensor_tensor(sk[:, :], sinkb[:, :], nmx[:, :], ALU.add).then_inc(sk_ready.sem, 1)
                    if prev and par == 0 and cfg["mask_even_after"]:
                        link(dve.tensor_copy(mask_even[:, :], mask_odd))
                    z_out(n + 1, par ^ 1, i + par)
                    dve.wait_ge(o_full.sem, o_full.done(n))
                    if not swa:
                        dve.tensor_copy(osb[par][:, 0:512], ps_o[0][:, :]).then_inc(o_free.sem, 1)
                    else:
                        dve.wait_ge(sink_done.sem, sink_done.done(n))
                        den = osb[par][:, H * DH + H:H * DH + 2 * H]
                        link(dve.tensor_tensor(rden[:, :], den, sk[:, :], ALU.add))
                        link(dve.reciprocal(rden[:, :], rden[:, :]))
                        for b in range(2):
                            last = dve.tensor_tensor(
                                osb[par][:, b * 512:(b + 1) * 512].rearrange("p (h d) -> p h d", d=DH),
                                ps_o[b][:, :].rearrange("p (h d) -> p h d", d=DH),
                                rden[:, 8 * b:8 * b + 8].rearrange("p (h o) -> p h o", o=1).broadcast_to([P, 8, DH]),
                                ALU.mult)
                        last.then_inc(o_free.sem, 1)
            assert steps[0] == per_pair


@own_semaphores
def mlstm(nc, env, cfg):
    widths = [WA, WA, WA, WA, 2 * HA]
    NCH, U = len(widths), 6
    Q_T, K_T, G_T, X_T, C_T = 0, 1, 2, 3, 5
    W, w_sems, cst = cfg["w"], cfg["w_sems"], env["cst"]
    ident, sel, ones = cst("ident"), cst("sel"), cst("ones")
    KSCALE = DA ** -0.5

    with ExitStack() as ctx:
        def sb(nm, shape):
            return ctx.enter_context(nc.sbuf_tensor(f"m_{nm}", shape, F32))

        def sem(nm):
            return env["sems"].enter_context(nc.semaphore(f"m_{nm}"))

        xn = [sb(f"xn{i}", [P, D]) for i in range(2)]
        xT = [sb(f"xT{i}", [P, KT, P]) for i in range(2)]
        z = [sb(f"z{i}", [P, 4 * WA]) for i in range(2)]
        gate = sb("gate", [P, 2 * HA])
        absf = sb("absf", [P, HA])
        logs = [sb(f"logs{i}", [P, P]) for i in range(2)]
        biasb = sb("biasb", [P, 2 * HA])
        qT = sb("qT", [P, HA, P])
        kT = sb("kT", [P, HA, P])
        lrow, frow, brow, rrow = (sb(nm, [HA, P]) for nm in ("lrow", "frow", "brow", "rrow"))
        mrow = [sb(f"mrow{i}", [HA, P]) for i in range(2)]
        zero4 = sb("zero4", [HA, P])
        rows = sb("rows", [P, P])
        ial = sb("ial", [HA, 1])
        ild = sb("ild", [HA, HA * BD])
        cols = sb("cols", [P, P])
        ecol = sb("ecol", [P, 3 * HA])
        il = sb("il", [P, HA * BD])
        wt = sb("wt", [P, HA, P])
        kw = sb("kw", [P, HA, P])
        sig = sb("sig", [P, WA])
        num_in = sb("num_in", [P, HA, P])
        num = sb("num", [P, HA, P])
        nq = sb("nq", [P, 3 * HA])
        ga = [sb(f"ga{i}", [P, WA]) for i in range(2)]
        C = sb("C", [P, HA, DA])
        nst = sb("nst", [P, HA])

        x_loaded = [sem(f"x_loaded{i}") for i in range(2)]
        ga_stored = [sem(f"ga_stored{i}") for i in range(2)]
        bias_loaded, cleared, out_stored = sem("bias_loaded"), sem("cleared"), sem("out_stored")
        t_full, t_free = Count(sem("t_full"), U, pre=2), Count(sem("t_free"), U, pre=2, credit=2)
        z_full, z_free = Count(sem("z_full"), NCH), Count(sem("z_free"), NCH, credit=2)
        abs_ready, log_ready, z_ready = (Count(sem(s)) for s in ("abs_ready", "log_ready", "z_ready"))
        rows_ready, d_full, s_full = (Count(sem(s)) for s in ("rows_ready", "d_full", "s_full"))
        cols_ready, masked, w_ready, sw_ready = (Count(sem(s)) for s in ("cols_ready", "masked", "w_ready", "sw_ready"))
        kw_ready, sig_ready, all_full, num_copied = (Count(sem(s)) for s in ("kw_ready", "sig_ready", "all_full", "num_copied"))
        ga_ready = Count(sem("ga_ready"))
        state_ready = Count(sem("state_ready"), 1, credit=1)
        exp_gate = Count(sem("exp_gate"))
        dve_step = sem("dve_step")

        bank_stack = ctx.enter_context(ExitStack())

        def ps(nm):
            return bank_stack.enter_context(nc.psum_tensor(f"m_{nm}", [P, 512], F32))

        ps_z = [ps(f"ps_z{i}") for i in range(2)]
        ps_t = [ps(f"ps_t{i}") for i in range(2)]
        ps_s, ps_d, ps_o, ps_m = ps("ps_s"), ps("ps_d"), ps("ps_o"), ps("ps_m")

        def head(t, h, w=P):
            return t[:, h * w:(h + 1) * w]

        def tbank(par, c):
            return ps_t[(par * U + c) % 2] if c >= 0 else ps_t[c % 2]

        with nc.Block() as block:
            @block.sync
            def _(sp):
                def load(i, par):
                    sp.dma_start(xn[par][:, :], row_tiles(cfg["x"], 1, i, par)[0]).then_inc(x_loaded[par], 16)

                sp.dma_start(biasb[:, :], cfg["bias"].to_broadcast([P, 2 * HA])).then_inc(bias_loaded, 16)
                load(0, 0)
                cfg["load_consts"](sp)
                cfg["load_weights"](sp, range(2))
                load(0, 1)
                cfg["load_weights"](sp, range(2, NCH))
                cfg["prefetch"](sp)

                def step(i, par, n, more):
                    sp.wait_ge(z_ready.sem, z_ready.done(n))
                    if more:
                        load(i + 1, par)
                    elif par == 0:
                        sp.dma_start(xn[0][0:NS, :], cfg["xs"]).then_inc(x_loaded[0], 16)
                    sp.wait_ge(ga_ready.sem, ga_ready.done(n))
                    sp.dma_start(row_tiles(cfg["out"][0:SEQ, 0:WA], 1, i, par)[0], ga[par][:, :]).then_inc(ga_stored[par], 16)

                with sp.Fori(0, NT // 2 - 1) as i:
                    for par in range(2):
                        step(i, par, 2 * i + par, True)
                for par in range(2):
                    step(NT // 2 - 1, par, NT - 2 + par, False)
                sp.wait_ge(state_ready.sem, state_ready.done(NT - 1))
                with nc.allow_non_contiguous_dma(reason="a few numbers"):
                    sp.dma_start(cfg["C_p"].rearrange("h d e -> d h e"), C[:, :, :]).then_inc(out_stored, 16)
                    sp.dma_start(cfg["n_p"].rearrange("h d -> d h"), nst[:, :]).then_inc(out_stored, 16)
                    sp.dma_start(cfg["m_p"].rearrange("(h o) -> h o", o=1), mrow[1][:, P - 1:P]).then_inc(out_stored, 16)
                sp.wait_ge(out_stored, 48)
                for par in range(2):
                    sp.wait_ge(ga_stored[par], 16 * (NT // 2 + 1))

            @block.tensor
            def _(pe):
                def x_transposes(n, c, i_next, par):
                    pe.wait_ge(x_loaded[par], 16 * (i_next + 1))
                    for half in range(2):
                        bank = tbank(par ^ 1, c + half) if c >= 0 else ps_t[half]
                        pe.wait_ge(t_free.sem, t_free.done(n, c + half, back=2))
                        for j in range(4):
                            last = pe.transpose(head(bank, j), head(xn[par], 4 * half + j), ident)
                        last.then_inc(t_full.sem, 1)

                def project(n, par, chunks):
                    for c in chunks:
                        pe.wait_ge(z_free.sem, z_free.done(n, c, back=2))
                        if isinstance(n, int) and n == 0:
                            pe.wait_ge(w_sems[c], 16)
                        for k in range(KT):
                            last = pe.matmul(ps_z[(par * NCH + c) % 2][:, 0:widths[c]], xT[par][:, k, :],
                                             W[:, k, c * WA:c * WA + widths[c]], start=(k == 0), stop=(k == KT - 1))
                        last.then_inc(z_full.sem, 1)

                def step(i, par, n):
                    zt = z[par]
                    pe.wait_ge(z_ready.sem, z_ready.done(n))
                    for c, col in ((Q_T, 0), (K_T, WA)):
                        pe.wait_ge(t_free.sem, t_free.done(n, c, back=2))
                        for h in range(HA):
                            last = pe.transpose(head(tbank(par, c), h), zt[:, col + h * P:col + (h + 1) * P], ident)
                        last.then_inc(t_full.sem, 1)
                    pe.wait_ge(t_free.sem, t_free.done(n, G_T, back=2))
                    pe.transpose(tbank(par, G_T)[:, 0:P], logs[par][:, :], ident).then_inc(t_full.sem, 1)
                    x_transposes(n, X_T, i + par, par ^ 1)
                    pe.wait_ge(t_free.sem, t_free.done(n, X_T + 1))
                    project(n + 1, par ^ 1, (0, 1))
                    pe.wait_ge(state_ready.sem, state_ready.done(n, back=1))
                    pe.wait_ge(rows_ready.sem, rows_ready.done(n))
                    for h in range(HA):
                        pe.matmul(head(ps_d, h), sel[0:HA, h * P:(h + 1) * P], rrow[:, :], start=True, stop=True)
                    pe.matmul(ps_m[:, 12:16], ones[0:HA, :], ild[:, 0:HA], start=True, stop=True).then_inc(d_full.sem, 1)
                    pe.wait_ge(t_free.sem, t_free.done(n, C_T, back=2))
                    pe.transpose(tbank(par, C_T)[:, 0:P], rows[:, :], ident).then_inc(t_full.sem, 1)
                    for h in range(HA):
                        last = pe.matmul(head(ps_s, h), kT[:, h, :], qT[:, h, :], start=True, stop=True)
                    last.then_inc(s_full.sem, 1)
                    project(n + 1, par ^ 1, (2, 3, 4))
                    pe.wait_ge(cols_ready.sem, cols_ready.done(n))
                    pe.wait_ge(sw_ready.sem, sw_ready.done(n))
                    for h in range(HA):
                        pe.matmul(head(ps_o, h), wt[:, h, :], zt[:, 2 * WA + h * P:2 * WA + (h + 1) * P], start=True, stop=True)
                        pe.matmul(ps_m[:, h:h + 1], wt[:, h, :], ones[:, 0:1], start=True, stop=True)
                    for h in range(HA):
                        pe.matmul(head(ps_s, h), qT[:, h, :], C[:, h, :], start=True, stop=True)
                        pe.matmul(ps_m[:, HA + h:HA + h + 1], qT[:, h, :], nst[:, h:h + 1], start=True, stop=True)
                    pe.wait_ge(kw_ready.sem, kw_ready.done(n))
                    for h in range(HA):
                        pe.matmul(head(ps_d, h), kw[:, h, :], zt[:, 2 * WA + h * P:2 * WA + (h + 1) * P], start=True, stop=True)
                        last = pe.matmul(ps_m[:, 2 * HA + h:2 * HA + h + 1], kw[:, h, :], ones[:, 0:1], start=True, stop=True)
                    last.then_inc(all_full.sem, 1)

                pe.wait_ge(env["const_loaded"], 16)
                x_transposes(0, -2, 0, 0)
                pe.wait_ge(t_free.sem, t_free.done(0, -1))
                project(0, 0, range(NCH))
                pe.wait_ge(cleared, 3)
                with pe.Fori(0, NT // 2) as i:
                    for par in range(2):
                        step(i, par, 2 * i + par)

            @block.scalar
            def _(act):
                def evacuate(n, c, bank, dst, w=512):
                    act.wait_ge(t_full.sem, t_full.done(n, c))
                    nc.scalar.copy(dst, bank[:, 0:w]).then_inc(t_free.sem, 1)

                def x_out(n, c, par):
                    for half in range(2):
                        bank = tbank(par ^ 1, c + half) if c >= 0 else ps_t[half]
                        evacuate(n, c + half, bank, xT[par][:, 4 * half:4 * half + 4, :].rearrange("p k t -> p (k t)"))

                def log_gate(n):
                    act.wait_ge(abs_ready.sem, abs_ready.done(n))
                    nc.scalar.activation(absf[:, :], absf[:, :], ACT.Exp, scale=-1.0).then_inc(exp_gate.sem, 1)
                    act.wait_ge(exp_gate.sem, exp_gate.done(n))
                    nc.scalar.activation(absf[:, :], absf[:, :], ACT.Ln, bias=1.0).then_inc(log_ready.sem, 1)

                x_out(0, -2, 0)
                log_gate(0)
                with act.Fori(0, NT // 2) as i:
                    for par in range(2):
                        n = 2 * i + par
                        evacuate(n, Q_T, tbank(par, Q_T), qT[:, :, :].rearrange("p h t -> p (h t)"))
                        evacuate(n, K_T, tbank(par, K_T), kT[:, :, :].rearrange("p h t -> p (h t)"))
                        act.wait_ge(t_full.sem, t_full.done(n, G_T))
                        nc.scalar.copy(lrow[:, :], tbank(par, G_T)[0:HA, 0:P])
                        nc.scalar.copy(frow[:, :], tbank(par, G_T)[32:32 + HA, 0:P]).then_inc(t_free.sem, 1)
                        x_out(n, X_T, par ^ 1)
                        evacuate(n, C_T, tbank(par, C_T), cols[:, :], P)
                        act.wait_ge(t_free.sem, t_free.done(n, C_T))
                        nc.scalar.activation(ecol[:, 0:HA], cols[:, 32:32 + HA], ACT.Exp)
                        nc.scalar.activation(ecol[:, HA:2 * HA], cols[:, 64:64 + HA], ACT.Exp, scale=-1.0)
                        nc.scalar.activation(ecol[:, 2 * HA:3 * HA], cols[:, 96:96 + HA], ACT.Exp)
                        nc.scalar.activation(il[:, 0:HA], ps_m[:, 12:16], ACT.Exp).then_inc(cols_ready.sem, 1)
                        act.wait_ge(masked.sem, masked.done(n))
                        for h in range(HA):
                            last = nc.scalar.activation(wt[:, h, :], wt[:, h, :], ACT.Exp, bias=cols[:, h:h + 1])
                        last.then_inc(w_ready.sem, 1)
                        nc.scalar.activation(sig[:, :], z[par][:, 3 * WA:4 * WA], ACT.Exp, scale=-1.0).then_inc(sig_ready.sem, 1)
                        log_gate(n + 1)
                        act.wait_ge(all_full.sem, all_full.done(n))
                        nc.scalar.copy(num_in[:, :, :].rearrange("p h t -> p (h t)"), ps_o[:, :]).then_inc(num_copied.sem, 1)

            @block.gpsimd
            def _(pool):
                for c, k in ((t_free, 2), (z_free, 2), (state_ready, 1)):
                    pool.sem_inc(c.sem, k)
                for par in range(2):
                    pool.sem_inc(ga_stored[par], 16)
                    pool.memset(mrow[par][:, :], 0.0)
                    pool.memset(logs[par][:, :], 0.0)
                pool.memset(C[:, :, :], 0.0)
                pool.memset(nst[:, :], 0.0)
                pool.memset(zero4[:, :], 0.0)
                pool.memset(rows[:, :], 0.0).then_inc(cleared, 3)
                with pool.Fori(0, NT // 2) as i:
                    for par in range(2):
                        n = 2 * i + par
                        pool.wait_ge(state_ready.sem, state_ready.done(n, back=1))
                        pool.wait_ge(cols_ready.sem, cols_ready.done(n))
                        pool.tensor_tensor(kw[:, :, :], z[par][:, WA:2 * WA].rearrange("p (h d) -> p h d", d=P),
                                           ecol[:, 0:HA].rearrange("p (h o) -> p h o", o=1).broadcast_to([P, HA, P]),
                                           ALU.mult).then_inc(kw_ready.sem, 1)

            @block.vector
            def _(dve):
                steps, base = [0], [0]

                def link(ins):
                    steps[0] += 1
                    ins.then_inc(dve_step, 1)
                    dve.wait_ge(dve_step, base[0] + steps[0])

                def z_out(n, par, chunks):
                    for c in chunks:
                        dve.wait_ge(z_full.sem, z_full.done(n, c))
                        src = ps_z[(par * NCH + c) % 2][:, 0:widths[c]]
                        dst = z[par][:, c * WA:(c + 1) * WA] if c < 4 else None
                        if c == 1:
                            last = dve.tensor_scalar(dst, src, KSCALE, None, ALU.mult)
                        elif c == 4:
                            last = dve.tensor_tensor(gate[:, :], src, biasb[:, :], ALU.add)
                        else:
                            last = dve.tensor_copy(dst, src)
                        last.then_inc(z_free.sem, 1)

                def gates(n, par):
                    dve.wait_ge(z_free.sem, z_free.done(n, NCH - 1))
                    dve.tensor_copy(logs[par][:, 0:HA], gate[:, 0:HA])
                    dve.scalar_tensor_tensor(out=absf[:, :], in0=gate[:, HA:2 * HA], scalar=-1.0, in1=gate[:, HA:2 * HA],
                                             op0=ALU.mult, op1=ALU.max).then_inc(abs_ready.sem, 1)
                    dve.wait_ge(log_ready.sem, log_ready.done(n))
                    dve.scalar_tensor_tensor(out=logs[par][:, 32:32 + HA], in0=gate[:, HA:2 * HA], scalar=0.0,
                                             in1=absf[:, :], op0=ALU.min, op1=ALU.subtract).then_inc(z_ready.sem, 1)

                dve.wait_ge(env["const_loaded"], 16)
                dve.wait_ge(bias_loaded, 16)
                dve.wait_ge(cleared, 3)
                z_out(0, 0, range(NCH))
                gates(0, 0)
                per_pair = 2 * 12
                with dve.Fori(0, NT // 2) as i:
                    for par in range(2):
                        n = 2 * i + par
                        if par == 0:
                            base[0], steps[0] = i * per_pair, 0
                        dve.wait_ge(t_free.sem, t_free.done(n, G_T))
                        m_prev = mrow[par ^ 1][:, P - 1:P]
                        dve.tensor_tensor_scan(mrow[par][:, :], frow[:, :], lrow[:, :], m_prev, ALU.add, ALU.max)
                        link(dve.tensor_tensor_scan(brow[:, :], frow[:, :], zero4[:, :], 0.0, ALU.add, ALU.add))
                        dve.tensor_tensor(rows[0:HA, :], lrow[:, :], brow[:, :], ALU.subtract)
                        dve.tensor_copy(rows[64:64 + HA, :], mrow[par][:, :])
                        link(dve.tensor_tensor(rrow[:, :], brow[:, :], mrow[par][:, :], ALU.subtract))
                        dve.tensor_scalar(rows[32:32 + HA, :], rows[0:HA, :], rrow[:, P - 1:P], None, ALU.add)
                        dve.tensor_scalar(rows[96:96 + HA, :], rrow[:, :], m_prev, None, ALU.add)
                        link(dve.tensor_tensor(ial[:, :], rrow[:, P - 1:P], m_prev, ALU.add))
                        dve.tensor_scalar(ild[:, 0:HA], ident[0:HA, 0:HA], ial[:, :], None, ALU.mult)\
                            .then_inc(rows_ready.sem, 1)
                        z_out(n + 1, par ^ 1, (0,))
                        dve.wait_ge(d_full.sem, d_full.done(n))
                        dve.tensor_tensor(wt[:, :, :], ps_d[:, :].rearrange("p (h t) -> p h t", h=HA),
                                          cst("m_causalT").rearrange("p (o t) -> p o t", o=1).broadcast_to([P, HA, P]),
                                          ALU.add).then_inc(masked.sem, 1)
                        z_out(n + 1, par ^ 1, (1,))
                        dve.wait_ge(s_full.sem, s_full.done(n))
                        dve.wait_ge(w_ready.sem, w_ready.done(n))
                        dve.tensor_tensor(wt[:, :, :], ps_s[:, :].rearrange("p (h t) -> p h t", h=HA), wt[:, :, :], ALU.mult)\
                            .then_inc(sw_ready.sem, 1)
                        z_out(n + 1, par ^ 1, (2, 3, 4))
                        gates(n + 1, par ^ 1)
                        dve.wait_ge(sig_ready.sem, sig_ready.done(n))
                        link(dve.tensor_scalar(sig[:, :], sig[:, :], 1.0, None, ALU.add))
                        link(dve.reciprocal(sig[:, :], sig[:, :]))
                        dve.wait_ge(num_copied.sem, num_copied.done(n))
                        link(dve.tensor_copy(nq[:, 0:2 * HA], ps_m[:, 0:2 * HA]))
                        link(dve.tensor_tensor(nq[:, HA:2 * HA], nq[:, HA:2 * HA], ecol[:, 2 * HA:3 * HA], ALU.mult))
                        link(dve.tensor_tensor(nq[:, 0:HA], nq[:, 0:HA], nq[:, HA:2 * HA], ALU.add))
                        link(dve.scalar_tensor_tensor(out=nq[:, 0:HA], in0=nq[:, 0:HA], scalar=-1.0, in1=nq[:, 0:HA],
                                                      op0=ALU.mult, op1=ALU.max))
                        link(dve.tensor_tensor(nq[:, 0:HA], nq[:, 0:HA], ecol[:, HA:2 * HA], ALU.max))
                        dve.reciprocal(nq[:, 2 * HA:3 * HA], nq[:, 0:HA])
                        for h in range(HA):
                            last = dve.scalar_tensor_tensor(out=num[:, h, :], in0=head(ps_s, h), scalar=ecol[:, 2 * HA + h:2 * HA + h + 1],
                                                            in1=num_in[:, h, :], op0=ALU.mult, op1=ALU.add)
                        link(last)
                        dve.wait_ge(ga_stored[par], 16 * (i + 1))
                        for h in range(HA):
                            last = dve.scalar_tensor_tensor(out=head(ga[par], h), in0=num[:, h, :],
                                                            scalar=nq[:, 2 * HA + h:2 * HA + h + 1], in1=head(sig, h),
                                                            op0=ALU.mult, op1=ALU.mult)
                        last.then_inc(ga_ready.sem, 1)
                        for h in range(HA):
                            dve.scalar_tensor_tensor(out=C[:, h, :], in0=C[:, h, :], scalar=il[:, h:h + 1], in1=head(ps_d, h),
                                                     op0=ALU.mult, op1=ALU.add)
                        link(dve.tensor_tensor(nst[:, :], nst[:, :], il[:, 0:HA], ALU.mult))
                        dve.tensor_tensor(nst[:, :], nst[:, :], ps_m[:, 2 * HA:3 * HA], ALU.add).then_inc(state_ready.sem, 1)
                assert steps[0] == per_pair, steps[0]

        bank_stack.close()
        mlstm_sample(nc, env, cfg, dict(z=z[0], logs=logs[0], qT=qT, kT=kT, sb=sb, sem=sem, ctx=ctx))


def mlstm_sample(nc, env, cfg, m):
    z, logs, qT, kT, sb, sem, ctx = (m[k] for k in ("z", "logs", "qT", "kT", "sb", "sem", "ctx"))
    cst = env["cst"]
    ident, sel, ones, blk = cst("ident"), cst("sel"), cst("ones"), cst("blk")
    C0 = cfg["w"][:, 4:8, 0:2 * HA * DA].rearrange("p k (b h e) -> p k b h e", b=2, h=HA)
    n0 = sb("s_n0", [P, HA, BD])
    m0 = sb("s_m0", [HA, BD])
    lrow, frow, brow, rrow, mrow, urow, zero = (sb(f"s_{nm}", [HA, NS]) for nm in ("lrow", "frow", "brow", "rrow", "mrow", "urow", "zero"))
    rows = sb("s_rows", [P, P])
    ial = sb("s_ial", [HA, BD])
    ild = sb("s_ild", [HA, HA, BD])
    il = sb("s_il", [P, HA * BD])
    cols = sb("s_cols", [NS, P])
    ecol = sb("s_ecol", [NS, 3 * HA])
    wt = sb("s_wt", [NS, HA, NS])
    kw = sb("s_kw", [NS, HA, P])
    vblk = cfg["w"][0:NS, 0:HA, 0:BD * DA].rearrange("p h (b d) -> p h b d", b=BD)
    qn = sb("s_qn", [P, HA, NS])
    inter = sb("s_inter", [P, HA, P])
    num_in = sb("s_num_in", [NS, WA])
    num = sb("s_num", [NS, WA])
    sig = sb("s_sig", [NS, WA])
    nq = sb("s_nq", [NS, 3 * HA])
    ga = sb("s_ga", [NS, WA])
    loaded, m0_loaded, cleared, stored = sem("s_loaded"), sem("s_m0_loaded"), sem("s_cleared"), sem("s_stored")
    qk_full, qk_out, rows_out, scanned, d_full = (sem(f"s_{x}") for x in ("qk_full", "qk_out", "rows_out", "scanned", "d_full"))
    cols_out, ecol_out, il_out, masked, w_out, sw_out = (sem(f"s_{x}") for x in ("cols_out", "ecol_out", "il_out", "masked", "w_out", "sw_out"))
    kw_out, vb_out, qn_out, inter_full, inter_out, n_full = (sem(f"s_{x}") for x in ("kw_out", "vb_out", "qn_out", "inter_full", "inter_out", "n_full"))
    num_out, back_full, sig_out, c_full, c_out, ga_out, nn_out, step = (sem(f"s_{x}") for x in ("num_out", "back_full", "sig_out", "c_full", "c_out", "ga_out", "nn_out", "step"))
    A, B, S, Dm, X, Y, N, M = (ctx.enter_context(nc.psum_tensor(f"m_s_ps{i}", [P, 512], F32)) for i in range(8))

    with nc.Block() as block:
        @block.sync
        def _(sp):
            with nc.allow_non_contiguous_dma(reason="the state's vectors"):
                sp.dma_start(m0[:, :], cfg["m0"].rearrange("b h -> h b")).then_inc(m0_loaded, 16)
                for k in range(4):
                    sp.dma_start(C0[:, k, :, :, :].rearrange("p b h e -> p (b h) e"),
                                 cfg["C0"][2 * k:2 * k + 2].rearrange("b h d e -> d (b h) e")).then_inc(loaded, 16)
                for h in range(HA):
                    sp.dma_start(n0[:, h, :], cfg["n0"][:, h, :].rearrange("b d -> d b")).then_inc(loaded, 16)
                sp.wait_ge(ga_out, 1)
                sp.dma_start(cfg["out"][SEQ:SEQ + NS, 0:WA], ga[:, :]).then_inc(stored, 16)
                sp.wait_ge(c_out, 2 * HA)
                for k in range(4):
                    sp.dma_start(cfg["C_s"][2 * k:2 * k + 2].rearrange("b h d e -> d (b h) e"),
                                 C0[:, k, :, :, :].rearrange("p b h e -> p (b h) e")).then_inc(stored, 16)
                sp.wait_ge(nn_out, 1)
                for h in range(HA):
                    sp.dma_start(cfg["n_s"][:, h, :].rearrange("b d -> d b"), n0[:, h, :]).then_inc(stored, 16)
                sp.dma_start(cfg["m_s"].rearrange("b (h o) -> h b o", o=1),
                             mrow[:, :].rearrange("h (b t) -> h b t", t=TD)[:, :, TD - 1:TD]).then_inc(stored, 16)
            sp.wait_ge(stored, 16 * (6 + HA))

        @block.gpsimd
        def _(pool):
            pool.memset(zero[:, :], 0.0)
            pool.memset(inter[:, :, NS:P], 0.0)
            pool.memset(rows[:, :], 0.0).then_inc(cleared, 1)
            v = z[0:NS, 2 * WA:3 * WA].rearrange("p (h o d) -> p h o d", h=HA, o=1)
            for h in range(HA):
                last = pool.tensor_tensor(vblk[:, h, :, :], v[:, h, :, :].broadcast_to([NS, BD, DA]),
                                          blk[0:NS, :].rearrange("p (b o) -> p b o", o=1).broadcast_to([NS, BD, DA]), ALU.mult)
            last.then_inc(vb_out, 1)
            pool.wait_ge(ecol_out, 1)
            pool.tensor_tensor(kw[:, :, :], z[0:NS, WA:2 * WA].rearrange("p (h d) -> p h d", d=P),
                               ecol[:, 0:HA].rearrange("p (h o) -> p h o", o=1).broadcast_to([NS, HA, P]), ALU.mult)\
                .then_inc(kw_out, 1)

        @block.tensor
        def _(pe):
            for h in range(HA):
                pe.transpose(A[:, h * NS:(h + 1) * NS], z[0:NS, h * P:(h + 1) * P], ident[0:NS, 0:NS])
            for h in range(HA):
                pe.transpose(A[:, (HA + h) * NS:(HA + h + 1) * NS], z[0:NS, WA + h * P:WA + (h + 1) * P], ident[0:NS, 0:NS])
            pe.transpose(B[:, 0:NS], logs[0:NS, :], ident[0:NS, 0:NS]).then_inc(qk_full, 1)
            pe.wait_ge(qk_out, 1)
            for h in range(HA):
                pe.matmul(S[0:NS, h * NS:(h + 1) * NS], kT[:, h, 0:NS], qT[:, h, 0:NS], start=True, stop=True)
            pe.wait_ge(scanned, 1)
            for h in range(HA):
                pe.matmul(Dm[0:NS, h * NS:(h + 1) * NS], sel[0:HA, h * P:h * P + NS], rrow[:, :], start=True, stop=True)
            pe.transpose(X[:, 0:P], rows[:, :], ident)
            pe.matmul(M[:, 0:HA * BD], ones[0:HA, :], ild[:, :, :].rearrange("h g b -> h (g b)"), start=True, stop=True)\
                .then_inc(d_full, 1)
            pe.wait_ge(loaded, 16 * (HA + 4))
            for b in range(BD):
                for h in range(HA):
                    last = pe.matmul(Y[:, h * NS + b * TD:h * NS + (b + 1) * TD], C0[:, b // 2, b % 2, h, :],
                                     qT[:, h, b * TD:(b + 1) * TD], start=True, stop=True)
            last.then_inc(inter_full, 1)
            pe.wait_ge(sw_out, 1)
            for h in range(HA):
                pe.matmul(N[0:NS, h * P:(h + 1) * P], wt[:, h, :], z[0:NS, 2 * WA + h * P:2 * WA + (h + 1) * P], start=True, stop=True)
            pe.wait_ge(qn_out, 1)
            pe.wait_ge(il_out, 1)
            for h in range(HA):
                pe.matmul(M[0:NS, h:h + 1], wt[:, h, :], ones[0:NS, 0:1], start=True, stop=True)
                last = pe.matmul(M[0:NS, HA + h:HA + h + 1], qn[:, h, :], ones[:, 0:1], start=True, stop=True)
            pe.wait_ge(kw_out, 1)
            for h in range(HA):
                last = pe.matmul(M[:, 64 + h * BD:64 + (h + 1) * BD], kw[:, h, :], blk[0:NS, :], start=True, stop=True)
            last.then_inc(n_full, 1)
            pe.wait_ge(inter_out, 1)
            for h in range(HA):
                last = pe.transpose(A[:, h * P:(h + 1) * P], inter[:, h, :], ident)
            last.then_inc(back_full, 1)
            pe.wait_ge(vb_out, 1)
            pe.wait_ge(masked, 1)
            for u in range(2 * HA):
                if u >= 2:
                    pe.wait_ge(c_out, u - 1)
                h, half = u // 2, u % 2
                pe.matmul((B, X)[u % 2][:, :], kw[:, h, :],
                          vblk[:, h, 4 * half:4 * half + 4, :].rearrange("p b d -> p (b d)"), start=True, stop=True)\
                    .then_inc(c_full, 1)

        @block.scalar
        def _(act):
            act.wait_ge(qk_full, 1)
            nc.scalar.copy(lrow[:, :], B[0:HA, 0:NS])
            nc.scalar.copy(frow[:, :], B[32:32 + HA, 0:NS]).then_inc(rows_out, 1)
            nc.scalar.copy(qT[:, :, 0:NS], A[:, 0:HA * NS].rearrange("p (h t) -> p h t", t=NS))
            nc.scalar.copy(kT[:, :, 0:NS], A[:, HA * NS:2 * HA * NS].rearrange("p (h t) -> p h t", t=NS)).then_inc(qk_out, 1)
            nc.scalar.activation(sig[:, :], z[0:NS, 3 * WA:4 * WA], ACT.Exp, scale=-1.0).then_inc(sig_out, 1)
            act.wait_ge(d_full, 1)
            nc.scalar.copy(cols[:, :], X[0:NS, 0:P]).then_inc(cols_out, 1)
            nc.scalar.activation(il[:, :], M[:, 0:HA * BD], ACT.Exp).then_inc(il_out, 1)
            act.wait_ge(cols_out, 1)
            nc.scalar.activation(ecol[:, 0:HA], cols[:, 32:32 + HA], ACT.Exp)
            nc.scalar.activation(ecol[:, HA:2 * HA], cols[:, 64:64 + HA], ACT.Exp, scale=-1.0)
            nc.scalar.activation(ecol[:, 2 * HA:3 * HA], cols[:, 96:96 + HA], ACT.Exp).then_inc(ecol_out, 1)
            act.wait_ge(masked, 1)
            for h in range(HA):
                last = nc.scalar.activation(wt[:, h, :], wt[:, h, :], ACT.Exp, bias=cols[:, h:h + 1])
            last.then_inc(w_out, 1)
            act.wait_ge(inter_full, 1)
            nc.scalar.copy(inter[:, :, 0:NS], Y[:, 0:HA * NS].rearrange("p (h t) -> p h t", t=NS)).then_inc(inter_out, 1)
            act.wait_ge(n_full, 1)
            nc.scalar.copy(num_in[:, :], N[0:NS, :]).then_inc(num_out, 1)

        @block.vector
        def _(dve):
            count = [0]

            def link(ins):
                count[0] += 1
                ins.then_inc(step, 1)
                dve.wait_ge(step, count[0])

            def by_seq(t):
                return t.rearrange("p (b t) -> p b t", t=TD)

            dve.wait_ge(m0_loaded, 16)
            dve.wait_ge(cleared, 1)
            dve.wait_ge(rows_out, 1)
            for b in range(BD):
                c = slice(b * TD, (b + 1) * TD)
                dve.tensor_tensor_scan(mrow[:, c], frow[:, c], lrow[:, c], m0[:, b:b + 1], ALU.add, ALU.max)
                last = dve.tensor_tensor_scan(brow[:, c], frow[:, c], zero[:, c], 0.0, ALU.add, ALU.add)
            link(last)
            dve.tensor_tensor(urow[:, :], lrow[:, :], brow[:, :], ALU.subtract)
            dve.tensor_copy(rows[64:64 + HA, 0:NS], mrow[:, :])
            link(dve.tensor_tensor(rrow[:, :], brow[:, :], mrow[:, :], ALU.subtract))
            end = by_seq(rrow[:, :])[:, :, TD - 1:TD]
            dve.tensor_copy(rows[0:HA, 0:NS], urow[:, :])
            dve.tensor_tensor(by_seq(rows[32:32 + HA, 0:NS]), by_seq(urow[:, :]), end.broadcast_to([HA, BD, TD]), ALU.add)
            dve.tensor_tensor(by_seq(rows[96:96 + HA, 0:NS]), by_seq(rrow[:, :]),
                              m0[:, :].rearrange("h (b o) -> h b o", o=1).broadcast_to([HA, BD, TD]), ALU.add)
            link(dve.tensor_tensor(ial[:, :].rearrange("h (b o) -> h b o", o=1), end, m0[:, :].rearrange("h (b o) -> h b o", o=1), ALU.add))
            dve.tensor_tensor(ild[:, :, :], ident[0:HA, 0:HA].rearrange("h (g o) -> h g o", o=1).broadcast_to([HA, HA, BD]),
                              ial[:, :].rearrange("h (o b) -> h o b", o=1).broadcast_to([HA, HA, BD]), ALU.mult)\
                .then_inc(scanned, 1)
            dve.wait_ge(d_full, 1)
            dve.tensor_tensor(wt[:, :, :], Dm[0:NS, 0:HA * NS].rearrange("p (h t) -> p h t", t=NS),
                              cst("m_sampleT")[0:NS, :].rearrange("p (o t) -> p o t", o=1).broadcast_to([NS, HA, NS]),
                              ALU.add).then_inc(masked, 1)
            dve.wait_ge(w_out, 1)
            dve.tensor_tensor(wt[:, :, :], S[0:NS, 0:HA * NS].rearrange("p (h t) -> p h t", t=NS), wt[:, :, :], ALU.mult)\
                .then_inc(sw_out, 1)
            dve.wait_ge(qk_out, 1)
            dve.wait_ge(loaded, 16 * (HA + 4))
            for h in range(HA):
                last = dve.tensor_tensor(by_seq(qn[:, h, :]), by_seq(qT[:, h, 0:NS]),
                                         n0[:, h, :].rearrange("p (b o) -> p b o", o=1).broadcast_to([P, BD, TD]), ALU.mult)
            last.then_inc(qn_out, 1)
            dve.wait_ge(sig_out, 1)
            link(dve.tensor_scalar(sig[:, :], sig[:, :], 1.0, None, ALU.add))
            link(dve.reciprocal(sig[:, :], sig[:, :]))
            dve.wait_ge(num_out, 1)
            dve.wait_ge(ecol_out, 1)
            dve.wait_ge(back_full, 1)
            link(dve.tensor_copy(nq[:, 0:2 * HA], M[0:NS, 0:2 * HA]))
            link(dve.tensor_tensor(nq[:, HA:2 * HA], nq[:, HA:2 * HA], ecol[:, 2 * HA:3 * HA], ALU.mult))
            link(dve.tensor_tensor(nq[:, 0:HA], nq[:, 0:HA], nq[:, HA:2 * HA], ALU.add))
            link(dve.scalar_tensor_tensor(out=nq[:, 0:HA], in0=nq[:, 0:HA], scalar=-1.0, in1=nq[:, 0:HA],
                                          op0=ALU.mult, op1=ALU.max))
            link(dve.tensor_tensor(nq[:, 0:HA], nq[:, 0:HA], ecol[:, HA:2 * HA], ALU.max))
            dve.reciprocal(nq[:, 2 * HA:3 * HA], nq[:, 0:HA])
            for h in range(HA):
                c = slice(h * P, (h + 1) * P)
                last = dve.scalar_tensor_tensor(out=num[:, c], in0=A[0:NS, c], scalar=ecol[:, 2 * HA + h:2 * HA + h + 1],
                                                in1=num_in[:, c], op0=ALU.mult, op1=ALU.add)
            link(last)
            for h in range(HA):
                c = slice(h * P, (h + 1) * P)
                last = dve.scalar_tensor_tensor(out=ga[:, c], in0=num[:, c], scalar=nq[:, 2 * HA + h:2 * HA + h + 1],
                                                in1=sig[:, c], op0=ALU.mult, op1=ALU.mult)
            last.then_inc(ga_out, 1)
            dve.wait_ge(il_out, 1)
            for u in range(2 * HA):
                h, half = u // 2, u % 2
                dve.wait_ge(c_full, u + 1)
                for q in range(4):
                    b = 4 * half + q
                    last = dve.scalar_tensor_tensor(out=C0[:, b // 2, b % 2, h, :], in0=C0[:, b // 2, b % 2, h, :],
                                                    scalar=il[:, h * BD + b:h * BD + b + 1],
                                                    in1=(B, X)[u % 2][:, q * DA:(q + 1) * DA], op0=ALU.mult, op1=ALU.add)
                last.then_inc(c_out, 1)
            n_all = n0[:, :, :].rearrange("p h b -> p (h b)")
            link(dve.tensor_tensor(n_all, n_all, il[:, :], ALU.mult))
            dve.tensor_tensor(n_all, n_all, M[:, 64:64 + HA * BD], ALU.add).then_inc(nn_out, 1)


@own_semaphores
def sample_attention(nc, env, cfg):
    cst = env["cst"]
    ident = cst("ident")
    NB = 9
    ROWS = HB * TD
    KEYS = NB * P + NG * TD
    with ExitStack() as ctx:
        def sb(nm, shape):
            return ctx.enter_context(nc.sbuf_tensor(f"s_{nm}", shape, F32))

        def ps(nm):
            return ctx.enter_context(nc.psum_tensor(f"s_{nm}", [P, 512], F32))

        def sem(nm):
            return env["sems"].enter_context(nc.semaphore(f"sa_{nm}"))

        late = sb("late", [P, CONST.shape[1] - RESIDENT])

        def late_cst(nm):
            c0, w = CONST_AT[nm]
            return late[:, c0 - RESIDENT:c0 - RESIDENT + w]

        kv = [sb(f"kv{i}", [P, NB, 2 * WB]) for i in range(2)]
        new = [sb(f"new{i}", [TD, 3, NG, WB]) for i in range(2)]
        qk_new = sb("qk_new", [P, 2, NG * 4, TD])
        qblk = sb("qblk", [P, NG, 4, ROWS])
        kT = [sb(f"kT{i}", [P, 4, P]) for i in range(2)]
        prob = sb("prob", [ROWS, KEYS])
        mx = sb("mx", [ROWS, 4])
        nmx = sb("nmx", [ROWS, 1])
        den = sb("den", [ROWS, 1])
        rden = sb("rden", [ROWS, 1])
        pT = sb("pT", [P, NB, ROWS])
        pTn = sb("pTn", [TD, NG, ROWS])
        sel = sb("sel", [ROWS, HB, DH])
        ob = [sb(f"ob{i}", [ROWS, DH]) for i in range(2)]
        ob_raw = sb("ob_raw", [ROWS, DH])
        ps_n = ps("ps_n")
        ps_t = [ps("ps_t0"), ps("ps_t1")]
        ps_s = [ps(f"ps_s{i}") for i in range(3)]
        ps_o = ps("ps_o")
        loaded = [[sem(f"loaded{g}_{i}") for i in range(2)] for g in range(NG)]
        AMT = (32, 16, 32)
        TU = NB + 4
        NEXT = NB - 1
        t_full, t_free = Count(sem("t_full"), TU, pre=1), Count(sem("t_free"), TU, credit=2, pre=1)
        n_full, q_ready, s_full, e_done, o_full, ob_ready = (
            Count(sem(x)) for x in ("n_full", "q_ready", "s_full", "e_done", "o_full", "ob_ready"))
        n_out, step = Count(sem("n_out")), sem("step")
        max_ready, o_free = Count(sem("max_ready"), 1, credit=1), Count(sem("o_free"), 1, credit=1)
        stored = [sem(f"stored{i}") for i in range(2)]
        late_loaded = sem("late_loaded")

        def tbank(par, c):
            return ps_t[(par * TU + c + 1) % 2]

        def kslot(par, c):
            return kT[(par * TU + c) % 2]

        with nc.Block() as block:
            @block.sync
            def _(sp):
                def load(i, par):
                    def seq(t):
                        return t.rearrange("(b two) s x h d -> two b s (x h d)", two=2)[par, i]

                    c1, c2, c3 = (seq(c) for c in cfg["caches"])
                    sp.dma_start(new[par][:, :, :, :],
                                 cfg["zs"].rearrange("(b two t) (j g c) -> two b t j g c", two=2, t=TD, j=3, g=NG)[par, i])\
                        .then_inc(loaded[0][par], 16)
                    sp.dma_start(kv[par][:, 0, :], c1).then_inc(loaded[0][par], 16)
                    sp.dma_start(kv[par][:, 1:5, :], c2.rearrange("(p j) c -> p j c", j=4)).then_inc(loaded[1][par], 16)
                    c3 = c3.rearrange("(p a j) c -> a p j c", a=4, j=4)
                    for a in range(2):
                        sp.dma_start(kv[par][64 * a:64 * a + 64, 5:9, :], c3[a]).then_inc(loaded[2][par], 16)

                def store(i, par, n):
                    sp.wait_ge(ob_ready.sem, ob_ready.done(n))
                    hold(sp)
                    out = cfg["out"].rearrange("(b two t) (h d) -> two b h t d", two=2, t=TD, d=DH)[par, i]
                    for h in range(HB):
                        sp.dma_start(out[h], ob[par][h * TD:(h + 1) * TD, :]).then_inc(stored[par], 16)

                sp.dma_start(late[:, :], env["const"][:, RESIDENT:]).then_inc(late_loaded, 16)
                load(0, 0)
                load(0, 1)
                cfg["prefetch"](sp)
                with sp.Fori(0, BD // 2 - 1) as i:
                    for par in range(2):
                        n = 2 * i + par
                        sp.wait_ge(o_full.sem, o_full.done(n))
                        load(i + 1, par)
                        store(i, par, n)
                for par in range(2):
                    store(BD // 2 - 1, par, BD - 2 + par)
                for par in range(2):
                    sp.wait_ge(stored[par], 16 * HB * (BD // 2 + 1))

            @block.tensor
            def _(pe):
                def block_transposes(n, par, i, c, use):
                    for g, first in enumerate((0, 1, 5)):
                        if c == first:
                            pe.wait_ge(loaded[g][par], AMT[g] * (i + 1))
                    pe.wait_ge(t_free.sem, t_free.done(n, use, back=2))
                    hold(pe)
                    for u in range(4):
                        last = pe.transpose(tbank(par, use)[:, u * P:(u + 1) * P],
                                            kv[par][:, c, u * P:(u + 1) * P], ident)
                    last.then_inc(t_full.sem, 1)

                def ahead(n, par, i, use_par):
                    pe.wait_ge(loaded[0][par], AMT[0] * (i + 1))
                    hold(pe)
                    for kind in range(2):
                        for g in range(NG):
                            for u in range(4):
                                c = (kind * NG * 4 + g * 4 + u) * TD
                                last = pe.transpose(ps_n[:, c:c + TD], new[par][:, kind, g, u * P:(u + 1) * P], ident[0:TD, 0:TD])
                    last.then_inc(n_full.sem, 1)
                    pe.wait_ge(t_free.sem, t_free.done(n, NEXT, back=2) if n is not None else 2)
                    hold(pe)
                    for u in range(4):
                        last = pe.transpose(tbank(use_par, NEXT if n is not None else -1)[:, u * P:(u + 1) * P],
                                            kv[par][:, 0, u * P:(u + 1) * P], ident)
                    last.then_inc(t_full.sem, 1)

                def group(c):
                    return 0 if c == 0 else (1 if c < 5 else 2)

                def attend(n, par, i, last_one):
                    first_p = NB - last_one
                    pe.wait_ge(q_ready.sem, q_ready.done(n))
                    pe.wait_ge(max_ready.sem, max_ready.done(n, back=1))
                    for c in range(NB):
                        if c + 1 < NB:
                            block_transposes(n, par, i, c + 1, c)
                        pe.wait_ge(t_free.sem, t_free.done(n, c - 1))
                        hold(pe)
                        for u in range(4):
                            pe.matmul(ps_s[c // 4][0:ROWS, (c % 4) * P:(c % 4 + 1) * P], qblk[:, group(c), u, :],
                                      kslot(par, c)[:, u, :], start=(u == 0), stop=(u == 3))
                    for g in range(NG):
                        for u in range(4):
                            last = pe.matmul(ps_s[2][0:ROWS, P + g * TD:P + (g + 1) * TD], qblk[:, g, u, :],
                                             qk_new[:, 1, g * 4 + u, :], start=(u == 0), stop=(u == 3))
                    last.then_inc(s_full.sem, 1)
                    if not last_one:
                        ahead(n, par ^ 1, i + par, par)
                    pe.wait_ge(e_done.sem, e_done.done(n))
                    for t, (a, b) in enumerate(((0, 4), (4, 8), (8, 9))):
                        pe.wait_ge(t_free.sem, t_free.done(n, first_p + t, back=2))
                        hold(pe)
                        bank = tbank(par, first_p + t)
                        for c in range(a, b):
                            last = pe.transpose(bank[:, (c - a) * ROWS:(c - a + 1) * ROWS], prob[:, c * P:(c + 1) * P],
                                                ident[0:ROWS, 0:ROWS])
                        last.then_inc(t_full.sem, 1)
                    pe.wait_ge(t_free.sem, t_free.done(n, first_p + 3, back=2))
                    hold(pe)
                    for g in range(NG):
                        last = pe.transpose(tbank(par, first_p + 3)[0:TD, g * ROWS:(g + 1) * ROWS],
                                            prob[:, NB * P + g * TD:NB * P + (g + 1) * TD], ident[0:ROWS, 0:ROWS])
                    last.then_inc(t_full.sem, 1)
                    pe.wait_ge(o_free.sem, o_free.done(n, back=1))
                    pe.wait_ge(t_free.sem, t_free.done(n, first_p + 3))
                    hold(pe)
                    for c in range(NB):
                        pe.matmul(ps_o[0:ROWS, :], pT[:, c, :], kv[par][:, c, WB:2 * WB], start=(c == 0), stop=False)
                    for g in range(NG):
                        last = pe.matmul(ps_o[0:ROWS, :], pTn[:, g, :], new[par][:, 2, g, :], start=False, stop=(g == NG - 1))
                    last.then_inc(o_full.sem, 1)

                ahead(None, 0, 0, 0)
                with pe.Fori(0, BD // 2 - 1) as i:
                    for par in range(2):
                        attend(2 * i + par, par, i, False)
                for par in range(2):
                    attend(BD - 2 + par, par, BD // 2 - 1, par == 1)

            @block.scalar
            def _(act):
                def keys_out(n, use, par, slot):
                    act.wait_ge(t_full.sem, t_full.done(n, use) if n is not None else 1)
                    nc.scalar.copy(slot[:, :, :].rearrange("p u t -> p (u t)"), tbank(par, use)[:, :]).then_inc(t_free.sem, 1)

                def new_out(n):
                    act.wait_ge(n_full.sem, n_full.done(n))
                    nc.scalar.copy(qk_new[:, :, :, :].rearrange("p a b t -> p (a b t)"), ps_n[:, 0:2 * NG * 4 * TD])\
                        .then_inc(n_out.sem, 1)

                def attend(n, par, last_one):
                    first_p = NB - last_one
                    for c in range(1, NB):
                        keys_out(n, c - 1, par, kslot(par, c))
                    if not last_one:
                        new_out(n + 1)
                        keys_out(n, NEXT, par, kslot(par ^ 1, 0))
                    act.wait_ge(max_ready.sem, max_ready.done(n))
                    nc.scalar.activation(prob[:, :], prob[:, :], ACT.Exp, bias=nmx[:, :], scale=SCALE, accum_out=den[:, :])\
                        .then_inc(e_done.sem, 1)
                    for t, (a, b) in enumerate(((0, 4), (4, 8), (8, 9))):
                        act.wait_ge(t_full.sem, t_full.done(n, first_p + t))
                        nc.scalar.copy(pT[:, a:b, :].rearrange("p c r -> p (c r)"), tbank(par, first_p + t)[:, 0:(b - a) * ROWS])\
                            .then_inc(t_free.sem, 1)
                    act.wait_ge(t_full.sem, t_full.done(n, first_p + 3))
                    nc.scalar.copy(pTn[:, :, :].rearrange("p c r -> p (c r)"), tbank(par, first_p + 3)[0:TD, 0:NG * ROWS])\
                        .then_inc(t_free.sem, 1)

                new_out(0)
                keys_out(None, -1, 0, kslot(0, 0))
                with act.Fori(0, BD // 2 - 1) as i:
                    for par in range(2):
                        attend(2 * i + par, par, False)
                for par in range(2):
                    attend(BD - 2 + par, par, par == 1)

            @block.gpsimd
            def _(pool):
                for c, k in ((t_free, 2), (o_free, 1), (max_ready, 1)):
                    pool.sem_inc(c.sem, k)
                for par in range(2):
                    pool.sem_inc(stored[par], 16 * HB)

            @block.vector
            def _(dve):
                steps, base, per_pair = [0], [0], 2 * 3

                def link(ins):
                    steps[0] += 1
                    ins.then_inc(step, 1)
                    dve.wait_ge(step, base[0] + steps[0])

                def spread_q(n):
                    dve.wait_ge(n_out.sem, n_out.done(n))
                    for g in range(NG):
                        for u in range(4):
                            last = dve.tensor_tensor(
                                qblk[:, g, u, :].rearrange("p (h t) -> p h t", t=TD),
                                qk_new[:, 0, g * 4 + u, :].rearrange("p (o t) -> p o t", o=1).broadcast_to([P, HB, TD]),
                                late_cst("headsel").rearrange("p (u h t) -> p u h t", u=4, h=HB)[:, u, :, :], ALU.mult)
                    last.then_inc(q_ready.sem, 1)

                def attend(n, i, par, last_one):
                    dve.wait_ge(s_full.sem, s_full.done(n))
                    hold(dve)
                    for t, (a, w) in enumerate(((0, 512), (512, 512), (1024, KEYS - 1024))):
                        last = dve.tensor_tensor_reduce(out=prob[:, a:a + w], in0=ps_s[t][0:ROWS, 0:w],
                                                        in1=late_cst("m_samp")[0:ROWS, a:a + w], scale=1.0, scalar=NEG,
                                                        op0=ALU.add, op1=ALU.max, accum_out=mx[:, t:t + 1])
                    link(last)
                    link(dve.tensor_reduce(mx[:, 3:4], mx[:, 0:3], AX.X, ALU.max))
                    dve.tensor_scalar(nmx[:, :], mx[:, 3:4], -SCALE, None, ALU.mult).then_inc(max_ready.sem, 1)
                    if not last_one:
                        spread_q(n + 1)
                    dve.wait_ge(o_full.sem, o_full.done(n))
                    dve.wait_ge(stored[par], 16 * HB * (i + 1))
                    dve.reciprocal(rden[:, :], den[:, :])
                    dve.tensor_tensor(sel[:, :, :], ps_o[0:ROWS, :].rearrange("p (h d) -> p h d", d=DH),
                                      cst("diag")[0:ROWS, :].rearrange("p (h o) -> p h o", o=1).broadcast_to([ROWS, HB, DH]),
                                      ALU.mult).then_inc(o_free.sem, 1)
                    dve.wait_ge(o_free.sem, o_free.done(n))
                    link(dve.tensor_reduce(ob_raw[:, :], sel[:, :, :].rearrange("p h d -> p d h"), AX.X, ALU.add))
                    dve.tensor_scalar(ob[par][:, :], ob_raw[:, :], rden[:, :], None, ALU.mult).then_inc(ob_ready.sem, 1)

                dve.wait_ge(late_loaded, 16)
                spread_q(0)
                with dve.Fori(0, BD // 2 - 1) as i:
                    base[0], steps[0] = i * per_pair, 0
                    for par in range(2):
                        attend(2 * i + par, i, par, False)
                    assert steps[0] == per_pair
                base[0], steps[0] = (BD // 2 - 1) * per_pair, 0
                for par in range(2):
                    attend(BD - 2 + par, BD // 2 - 1, par, par == 1)


@own_semaphores
def swa_sample(nc, env, cfg):
    cst = env["cst"]
    ident = cst("ident")
    KV, G = KVC * DH, HC // KVC
    KEYS = P + TD
    Q, HB4 = BD * P // 512, 512 // P
    with ExitStack() as ctx:
        def sb(nm, shape):
            return ctx.enter_context(nc.sbuf_tensor(f"w_{nm}", shape, F32))

        def ps(nm):
            return ctx.enter_context(nc.psum_tensor(f"w_{nm}", [P, 512], F32))

        def sem(nm):
            return env["sems"].enter_context(nc.semaphore(f"ws_{nm}"))

        kv = sb("kv", [P, BD, 2 * KV])
        new = sb("new", [NS, (HC + 2 * KVC) * DH])
        qT = sb("qT", [P, BD, HC, TD])
        kT = sb("kT", [P, BD, P])
        knT = sb("knT", [P, NS])
        prob = sb("prob", [P, BD, KEYS])
        pn = sb("pn", [P, BD * (NS + TD)])
        mx, nmx, den, sk = (sb(x, [P, BD]) for x in ("mx", "nmx", "den", "sk"))
        sinkc = sb("sinkc", [P, 1])
        pT = sb("pT", [P, BD, P])
        pnT = sb("pnT", [NS, BD, P])
        ob = sb("ob", [P, BD, DH])
        ps_q, ps_n, ps_sn = ps("ps_q"), ps("ps_n"), ps("ps_sn")
        ps_k = [ps(f"ps_k{i}") for i in range(Q)]
        ps_s = [ps(f"ps_s{i}") for i in range(Q)]
        kv_loaded, new_loaded, sink_loaded, cleared, step, stored = (
            sem(x) for x in ("kv_loaded", "new_loaded", "sink_loaded", "cleared", "step", "stored"))
        q_full, q_out, k_full, k_out, s_full, nmx_ready, e_done, pn_ready, pt_full, pt_out, o_full, ob_ready = (
            sem(x) for x in ("q_full", "q_out", "k_full", "k_out", "s_full", "nmx_ready", "e_done", "pn_ready", "pt_full",
                             "pt_out", "o_full", "ob_ready"))

        def blocks(bank, w=P):
            return bank[:, :].rearrange("p (b w) -> p b w", w=w)

        def seqs(i):
            return slice(i * HB4, (i + 1) * HB4)

        with nc.Block() as block:
            @block.sync
            def _(sp):
                sp.dma_start(new[:, :], cfg["zs"]).then_inc(new_loaded, 16)
                sp.dma_start(kv[:, :, :], cfg["cache"].rearrange("b s x h d -> s b (x h d)")).then_inc(kv_loaded, 16)
                for h in range(HC):
                    sp.dma_start(sinkc[h * TD:(h + 1) * TD, :], cfg["sinks"][:, h:h + 1].to_broadcast([TD, 1])).then_inc(sink_loaded, 16)
                cfg["prefetch"](sp)
                sp.wait_ge(ob_ready, 2 * Q)
                out = cfg["out"].rearrange("(b t) (h d) -> h t b d", t=TD, d=DH)
                for h in range(HC):
                    sp.dma_start(out[h], ob[h * TD:(h + 1) * TD, :, :]).then_inc(stored, 16)
                sp.wait_ge(stored, 16 * HC)

            @block.gpsimd
            def _(pool):
                pool.memset(qT[:, :, :, :], 0.0)
                pool.memset(pn[:, :], 0.0).then_inc(cleared, 1)

            @block.tensor
            def _(pe):
                pe.wait_ge(new_loaded, 16)
                for j in range(HC // 2):
                    last = pe.transpose(ps_q[:, j * NS:(j + 1) * NS], new[:, j * P:(j + 1) * P], ident[0:NS, 0:NS])
                last.then_inc(q_full, 1)
                pe.transpose(ps_n[:, 0:NS], new[:, HC * DH:HC * DH + KV], ident[0:NS, 0:NS]).then_inc(k_full, 1)
                pe.wait_ge(kv_loaded, 16)
                for b in range(BD):
                    last = pe.transpose(blocks(ps_k[b // HB4])[:, b % HB4, :], kv[:, b, 0:KV], ident)
                    if b % HB4 == HB4 - 1:
                        last.then_inc(k_full, 1)
                pe.wait_ge(q_out, 2)
                for b in range(BD):
                    qt = qT[:, b, :, :].rearrange("p h t -> p (h t)")
                    if b == 0:
                        pe.wait_ge(k_out, 1)
                        for c in range(BD):
                            qc = qT[:, c, :, :].rearrange("p h t -> p (h t)")
                            pe.matmul(ps_sn[:, c * TD:(c + 1) * TD], qc, knT[:, c * TD:(c + 1) * TD], start=True, stop=True)
                    if b % HB4 == 0:
                        pe.wait_ge(k_out, 2 + b // HB4)
                    last = pe.matmul(blocks(ps_s[b // HB4])[:, b % HB4, :], qt, kT[:, b, :], start=True, stop=True)
                    if b % HB4 == HB4 - 1:
                        last.then_inc(s_full, 1)
                for b in range(BD):
                    pe.wait_ge(e_done, b + 1)
                    last = pe.transpose(blocks(ps_k[b // HB4])[:, b % HB4, :], prob[:, b, 0:P], ident)
                    if b % HB4 == HB4 - 1:
                        last.then_inc(pt_full, 1)
                pe.wait_ge(pn_ready, 1)
                for b in range(BD):
                    bank = (ps_q, ps_n)[b // HB4]
                    last = pe.transpose(bank[0:NS, (b % HB4) * P:(b % HB4 + 1) * P], pn[:, b * NS:(b + 1) * NS], ident)
                    if b % HB4 == HB4 - 1:
                        last.then_inc(pt_full, 1)
                pe.wait_ge(pt_out, 4)
                for b in range(BD):
                    o = blocks(ps_s[b // HB4])[:, b % HB4, :]
                    pe.matmul(o, pT[:, b, :], kv[:, b, KV:2 * KV], start=True, stop=False)
                    last = pe.matmul(o, pnT[:, b, :], new[:, HC * DH + KV:HC * DH + 2 * KV], start=False, stop=True)
                    if b % HB4 == HB4 - 1:
                        last.then_inc(o_full, 1)

            @block.scalar
            def _(act):
                act.wait_ge(k_full, 1)
                nc.scalar.copy(knT[:, :], ps_n[:, 0:NS]).then_inc(k_out, 1)
                for i in range(Q):
                    act.wait_ge(k_full, 2 + i)
                    nc.scalar.copy(kT[:, seqs(i), :], blocks(ps_k[i])).then_inc(k_out, 1)
                act.wait_ge(nmx_ready, 1)
                for b in range(BD):
                    nc.scalar.activation(prob[:, b, :], prob[:, b, :], ACT.Exp, bias=nmx[:, b:b + 1], scale=SCALE,
                                         accum_out=den[:, b:b + 1]).then_inc(e_done, 1)
                nc.scalar.activation(sk[:, :], sk[:, :], ACT.Exp).then_inc(e_done, 1)
                for i in range(Q):
                    act.wait_ge(pt_full, i + 1)
                    nc.scalar.copy(pT[:, seqs(i), :], blocks(ps_k[i])).then_inc(pt_out, 1)
                for i, bank in enumerate((ps_q, ps_n)):
                    act.wait_ge(pt_full, Q + i + 1)
                    nc.scalar.copy(pnT[:, seqs(i), :], bank[0:NS, :].rearrange("p (b w) -> p b w", w=P)).then_inc(pt_out, 1)

            @block.vector
            def _(dve):
                steps = [0]

                def link(ins):
                    steps[0] += 1
                    ins.then_inc(step, 1)
                    dve.wait_ge(step, steps[0])

                def wide(t, w):
                    return t.rearrange("p (b o) -> p b o", o=1).broadcast_to([t.shape[0], t.shape[1], w])

                dve.wait_ge(cleared, 1)
                dve.wait_ge(q_full, 1)
                heads = ps_q[:, :].rearrange("p (j b t) -> p b j t", b=BD, t=TD)
                for a in range(KVC):
                    for two in range(2):
                        src = heads[two * DH:(two + 1) * DH, :, a * G // 2:(a + 1) * G // 2, :]
                        dst = qT[a * DH:(a + 1) * DH, :, a * G:(a + 1) * G, :].rearrange("p b (j two) t -> p b two j t", two=2)
                        last = dve.tensor_copy(dst[:, :, two, :, :], src)
                    last.then_inc(q_out, 1)
                mask = cst("m_swas")
                for i in range(Q):
                    dve.wait_ge(s_full, i + 1)
                    dve.tensor_tensor(prob[:, seqs(i), 0:P], blocks(ps_s[i]),
                                      mask[:, 0:P].rearrange("p (o w) -> p o w", o=1).broadcast_to([P, HB4, P]), ALU.add)
                link(dve.tensor_tensor(prob[:, :, P:KEYS], ps_sn[:, 0:NS].rearrange("p (b t) -> p b t", t=TD),
                                       mask[:, P:KEYS].rearrange("p (o w) -> p o w", o=1).broadcast_to([P, BD, TD]), ALU.add))
                link(dve.tensor_reduce(mx[:, :], prob[:, :, :], AX.X, ALU.max))
                link(dve.tensor_scalar(mx[:, :], mx[:, :], SCALE, None, ALU.mult))
                dve.wait_ge(sink_loaded, 16 * HC)
                link(dve.tensor_tensor(mx[:, :], mx[:, :], sinkc[:, :].broadcast_to([P, BD]), ALU.max))
                dve.tensor_scalar(nmx[:, :], mx[:, :], -1.0, None, ALU.mult)
                dve.tensor_tensor(sk[:, :], sinkc[:, :].broadcast_to([P, BD]), mx[:, :], ALU.subtract).then_inc(nmx_ready, 1)
                dve.wait_ge(e_done, BD + 1)
                dve.tensor_copy(pn[:, :].rearrange("p (b w) -> p b w", w=NS + TD)[:, :, 0:TD], prob[:, :, P:KEYS]).then_inc(pn_ready, 1)
                link(dve.tensor_tensor(den[:, :], den[:, :], sk[:, :], ALU.add))
                link(dve.reciprocal(den[:, :], den[:, :]))
                for i in range(Q):
                    dve.wait_ge(o_full, i + 1)
                    for a in range(KVC):
                        rows = slice(a * G * TD, (a + 1) * G * TD)
                        dve.tensor_tensor(ob[rows, seqs(i), :], blocks(ps_s[i])[rows, :, a * DH:(a + 1) * DH],
                                          wide(den[rows, seqs(i)], DH), ALU.mult).then_inc(ob_ready, 1)


def layer_norm(nc, dve, link, t, rows, y, ln_ready, rstd_ready, n, normed, normed_sem):
    moments(dve, link, t, rows, y, ln_ready)
    normalise(dve, link, t, rows, y, rstd_ready, n, normed, normed_sem)


def moments(dve, link, t, rows, y, ln_ready):
    for half in range(2):
        last = dve.bn_stats(t["stats"][0:rows, half, :], y[:, half * 512:(half + 1) * 512])
    link(last)
    hold(dve)
    link(dve.bn_aggr(t["mv"][0:rows, :], t["stats"][0:rows, :, :].rearrange("p a b -> p (a b)")))
    dve.tensor_scalar(t["ve"][0:rows, :], t["mv"][0:rows, 1:2], EPS, None, ALU.add).then_inc(ln_ready.sem, 1)


def normalise(dve, link, t, rows, y, rstd_ready, n, normed, normed_sem):
    dve.wait_ge(rstd_ready.sem, rstd_ready.done(n))
    r, a, ve = t["r"][0:rows, :], t["a"][0:rows, :], t["ve"][0:rows, :]
    link(dve.tensor_tensor(a, r, r, ALU.mult))
    link(dve.tensor_tensor(a, a, ve, ALU.mult))
    link(dve.tensor_scalar(a, a, -0.5, 1.5, ALU.mult, ALU.add))
    link(dve.tensor_tensor(r, r, a, ALU.mult))
    dve.tensor_scalar(normed, y, t["mv"][0:rows, 0:1], r, ALU.subtract, ALU.mult).then_inc(normed_sem, 1)


LN_LINKS = 6


def root(nc, act, t, rows, ln_ready, log_done, rstd_ready, n):
    act.wait_ge(ln_ready.sem, ln_ready.done(n))
    nc.scalar.activation(t["r"][0:rows, :], t["ve"][0:rows, :], ACT.Ln).then_inc(log_done.sem, 1)
    act.wait_ge(log_done.sem, log_done.done(n))
    nc.scalar.activation(t["r"][0:rows, :], t["r"][0:rows, :], ACT.Exp, scale=-0.5).then_inc(rstd_ready.sem, 1)


def ln_tiles(sb):
    return {"stats": sb("stats", [P, 2, 6]), "mv": sb("mv", [P, 2]), "ve": sb("ve", [P, 1]), "r": sb("r", [P, 1]), "a": sb("a", [P, 1])}


@own_semaphores
def output_projection(nc, env, name, cfg):
    cst, merge, W = env["cst"], cfg["merge"], cfg["w"]
    ident = cst("ident")
    with ExitStack() as ctx:
        def sb(nm, shape, dt=F32):
            return ctx.enter_context(nc.sbuf_tensor(f"{name}_{nm}", shape, dt))

        def ps(nm):
            return ctx.enter_context(nc.psum_tensor(f"{name}_{nm}", [P, 512], F32))

        def sem(nm):
            return env["sems"].enter_context(nc.semaphore(f"{name}_{nm}"))

        xt = [sb(f"xt{i}", [P, D]) for i in range(2)]
        mixt = [sb(f"mixt{i}", [P, D]) for i in range(2)]
        mT = [[sb(f"mT{i}_{x}", [P, KT, P], F32R) for x in ("hi", "lo")] for i in range(2)]
        wo = [sb(f"wo_{x}", [P, KT, D], F32R) for x in ("hi", "lo")]
        y = sb("y", [P, D])
        yn = [sb(f"yn{i}", [P, D]) for i in range(2)]
        gb, bb = sb("gb", [P, D]), sb("bb", [P, D])
        t = ln_tiles(sb)
        if merge:
            og = [sb(f"og{i}", [P, NG, SROW]) for i in range(2)]
            top, dl, ed, tot, rt, cw = sb("top", [P, HB]), sb("dl", [P, NG, HB]), sb("ed", [P, NG, HB]), sb("tot", [P, HB]), sb("rt", [P, HB]), sb("cw", [P, NG, HB])
            part = [sb(f"part{i}", [P, WB]) for i in range(2)]
        ps_t = [ps(f"ps_t{i}") for i in range(2)]
        ps_y = [ps(f"ps_y{i}") for i in range(4)]
        x_loaded = [sem(f"x_loaded{i}") for i in range(2)]
        m_loaded = [sem(f"m_loaded{i}") for i in range(2)]
        stored = [sem(f"stored{i}") for i in range(2)]
        gb_loaded, step = sem("gb_loaded"), sem("step")
        delta_ready, exp_done, merged, ln_ready, log_done, rstd_ready, out_ready, normed = (
            Count(sem(x)) for x in ("delta_ready", "exp_done", "merged", "ln_ready", "log_done", "rstd_ready", "out_ready", "normed"))
        normed = Count(normed.sem, 1, credit=1)
        t_full, t_free = Count(sem("t_full"), 2), Count(sem("t_free"), 2, credit=2)
        m_hi, w_hi, w_lo = Count(sem("m_hi"), 2), sem("w_hi"), sem("w_lo")
        y_full, y_free = Count(sem("y_full"), 2), Count(sem("y_free"), 2, credit=4)
        MAMT = 16 * (NG + 1) if merge else 16

        with nc.Block() as block:
            @block.sync
            def _(sp):
                def ahead(t, i, par, pairs):
                    return row_tiles(t[2 * P * pairs:SEQ], 1, i, par)[0]

                def load_x(i, par, pairs=0):
                    sp.dma_start(xt[par][:, :], ahead(cfg["x"], i, par, pairs)).then_inc(x_loaded[par], 16)

                def load_mix(i, par, pairs=0):
                    if merge:
                        sp.dma_start(mixt[par][:, 0:WA], ahead(cfg["mix"][:, 0:WA], i, par, pairs)).then_inc(m_loaded[par], 16)
                        for g in range(NG):
                            sp.dma_start(og[par][:, g, :], ahead(cfg["og"][g], i, par, pairs)).then_inc(m_loaded[par], 16)
                    else:
                        sp.dma_start(mixt[par][:, :], ahead(cfg["mix"], i, par, pairs)).then_inc(m_loaded[par], 16)

                def load_sample_mix():
                    rows = NS // (MAMT // 16)
                    for q in range(MAMT // 16):
                        sp.dma_start(mixt[0][q * rows:(q + 1) * rows, :], cfg["mix"][SEQ + q * rows:SEQ + (q + 1) * rows, :])\
                            .then_inc(m_loaded[0], 16)

                def store(i, par, n):
                    sp.wait_ge(out_ready.sem, out_ready.done(n))
                    hold(sp)
                    sp.dma_start(row_tiles(cfg["out"][0:SEQ, :], 1, i, par)[0], yn[par][:, :]).then_inc(stored[par], 16)

                for par in range(2):
                    load_mix(0, par)
                    load_x(0, par)
                sp.dma_start(gb[:, :], cfg["g"].to_broadcast([P, D])).then_inc(gb_loaded, 16)
                sp.dma_start(bb[:, :], cfg["b"].to_broadcast([P, D])).then_inc(gb_loaded, 16)
                sp.wait_ge(t_full.sem, t_full.done(0, 1))
                load_mix(1, 0)
                with sp.Fori(0, NT // 2 - 2) as i:
                    for par in range(2):
                        n = 2 * i + par
                        sp.wait_ge(t_full.sem, t_full.done(n + 1, 1))
                        load_mix(i, par ^ 1, 1 + par)
                        sp.wait_ge(normed.sem, normed.done(n))
                        load_x(i, par, 1)
                        store(i, par, n)
                for n in range(NT - 4, NT):
                    if n + 3 <= NT:
                        sp.wait_ge(t_full.sem, t_full.done(n + 1, 1))
                        if n + 3 < NT:
                            load_mix((n + 3) // 2, (n + 3) % 2)
                        else:
                            load_sample_mix()
                    if n + 2 <= NT:
                        sp.wait_ge(normed.sem, normed.done(n))
                        if n + 2 < NT:
                            load_x((n + 2) // 2, n % 2)
                        else:
                            sp.dma_start(xt[0][0:NS, :], cfg["xs"]).then_inc(x_loaded[0], 16)
                    store(n // 2, n % 2, n)
                sp.wait_ge(out_ready.sem, out_ready.done(NT))
                sp.dma_start(cfg["out"][SEQ:SEQ + NS, :], yn[0][0:NS, :]).then_inc(stored[0], 16)
                sp.wait_ge(stored[0], 16 * (NT // 2 + 2))
                sp.wait_ge(stored[1], 16 * (NT // 2 + 1))

            @block.tensor
            def _(pe):
                def transposes(n, par, i_n):
                    if merge and not (isinstance(n, int) and n == NT):
                        pe.wait_ge(merged.sem, merged.done(n))
                    pe.wait_ge(m_loaded[par], MAMT * (i_n + 1))
                    for half in range(2):
                        pe.wait_ge(t_free.sem, t_free.done(n, half, back=2))
                        rows = NS if isinstance(n, int) and n == NT else P
                        for j in range(4):
                            c = (4 * half + j) * P
                            last = pe.transpose(ps_t[half][:, j * P:j * P + rows], mixt[par][0:rows, c:c + P], ident[0:rows, 0:rows])
                        last.then_inc(t_full.sem, 1)

                def project(n, par):
                    pe.wait_ge(t_free.sem, t_free.done(n, 1))
                    for c in range(2):
                        pe.wait_ge(w_lo, c + 1)
                        pe.wait_ge(y_free.sem, y_free.done(n, c, back=4))
                        for k in range(KT):
                            for q, (mp, wp) in enumerate(split_passes((mT[par][0], wo[0]), (mT[par][1], wo[1]))):
                                last = pe.matmul(ps_y[2 * par + c][:, :], mp[:, k, :], wp[:, k, c * 512:(c + 1) * 512],
                                                 start=(k == 0 and q == 0), stop=(k == KT - 1 and q == 2))
                        last.then_inc(y_full.sem, 1)

                transposes(0, 0, 0)
                with pe.Fori(0, NT // 2 - 1) as i:
                    for par in range(2):
                        n = 2 * i + par
                        transposes(n + 1, par ^ 1, i + par)
                        project(n, par)
                for n in range(NT - 2, NT + 1):
                    if n < NT:
                        transposes(n + 1, (n + 1) % 2, (n + 1) // 2)
                    project(n, n % 2)

            @block.scalar
            def _(act):
                def transposed(n, par, rows=P):
                    for half in range(2):
                        act.wait_ge(t_full.sem, t_full.done(n, half))
                        nc.scalar.copy(mT[par][0][:, 4 * half:4 * half + 4, 0:rows],
                                       ps_t[half][:, :].rearrange("p (k t) -> p k t", t=P)[:, :, 0:rows]).then_inc(m_hi.sem, 1)

                def weights(n):
                    if merge:
                        act.wait_ge(delta_ready.sem, delta_ready.done(n))
                        nc.scalar.activation(dl[:, :, :], dl[:, :, :], ACT.Exp, scale=SCALE).then_inc(exp_done.sem, 1)

                act.wait_ge(cfg["w_sem"], 16)
                for c in range(2):
                    cs = slice(c * 512, (c + 1) * 512)
                    nc.scalar.copy(wo[0][:, :, cs], W[:, :, cs]).then_inc(w_hi, 1)
                weights(0)
                transposed(0, 0)
                weights(1)
                with act.Fori(0, NT // 2 - 1) as i:
                    for par in range(2):
                        n = 2 * i + par
                        transposed(n + 1, par ^ 1)
                        weights(n + 2)
                        root(nc, act, t, P, ln_ready, log_done, rstd_ready, n)
                for n in range(NT - 2, NT + 1):
                    if n < NT:
                        transposed(n + 1, (n + 1) % 2, P if n + 1 < NT else NS)
                    root(nc, act, t, P if n < NT else NS, ln_ready, log_done, rstd_ready, n)

            @block.gpsimd
            def _(pool):
                pool.sem_inc(t_free.sem, 2)
                pool.sem_inc(y_free.sem, 4)
                pool.sem_inc(normed.sem, 1)
                for par in range(2):
                    pool.sem_inc(stored[par], 16)
                pool.wait_ge(gb_loaded, 32)

                def gain(n, par, rows=P):
                    pool.wait_ge(normed.sem, normed.done(n))
                    hold(pool)
                    o = yn[par][0:rows, :]
                    pool.tensor_tensor(o, o, gb[0:rows, :], ALU.mult).then_inc(gained.sem, 1)
                    pool.wait_ge(gained.sem, gained.done(n))
                    pool.tensor_tensor(o, o, bb[0:rows, :], ALU.add).then_inc(out_ready.sem, 1)

                gained = Count(sem("gained"))
                with pool.Fori(0, NT // 2) as i:
                    for par in range(2):
                        gain(2 * i + par, par)
                gain(NT, 0, NS)

            @block.vector
            def _(dve):
                steps, base = [0], [0]

                def link(ins):
                    steps[0] += 1
                    ins.then_inc(step, 1)
                    dve.wait_ge(step, base[0] + steps[0])

                def merge_tile(n, par, i_n):
                    if not merge:
                        return
                    dve.wait_ge(m_loaded[par], MAMT * (i_n + 1))
                    mx = og[par][:, :, WB:WB + HB]
                    link(dve.tensor_tensor(top[:, :], mx[:, 0, :], mx[:, 1, :], ALU.max))
                    link(dve.tensor_tensor(top[:, :], top[:, :], mx[:, 2, :], ALU.max))
                    dve.tensor_tensor(dl[:, :, :], mx, top[:, :].rearrange("p (o h) -> p o h", o=1).broadcast_to([P, NG, HB]),
                                      ALU.subtract).then_inc(delta_ready.sem, 1)
                    dve.wait_ge(exp_done.sem, exp_done.done(n))
                    link(dve.tensor_tensor(ed[:, :, :], dl[:, :, :], og[par][:, :, WB + HB:WB + 2 * HB], ALU.mult))
                    link(dve.tensor_reduce(tot[:, :], ed[:, :, :].rearrange("p g h -> p h g"), AX.X, ALU.add))
                    link(dve.reciprocal(rt[:, :], tot[:, :]))
                    link(dve.tensor_tensor(cw[:, :, :], dl[:, :, :], rt[:, :].rearrange("p (o h) -> p o h", o=1).broadcast_to([P, NG, HB]), ALU.mult))
                    dst = [mixt[par][:, WA:D], part[0][:, :], part[1][:, :]]
                    for g in range(NG):
                        last = dve.tensor_tensor(dst[g].rearrange("p (h d) -> p h d", d=DH),
                                                 og[par][:, g, 0:WB].rearrange("p (h d) -> p h d", d=DH),
                                                 cw[:, g, :].rearrange("p (h o) -> p h o", o=1).broadcast_to([P, HB, DH]), ALU.mult)
                    link(last)
                    dve.tensor_tensor(part[0][:, :], part[0][:, :], part[1][:, :], ALU.add).then_inc(summed.sem, 1)
                    dve.wait_ge(summed.sem, summed.done(n))
                    dve.tensor_tensor(mixt[par][:, WA:D], mixt[par][:, WA:D], part[0][:, :], ALU.add).then_inc(merged.sem, 1)

                def rest(n, par, rows=P):
                    for half in range(2):
                        dve.wait_ge(m_hi.sem, m_hi.done(n, half))
                        ks = slice(4 * half, 4 * half + 4)
                        dve.tensor_tensor(mT[par][1][:, ks, 0:rows], ps_t[half][:, :].rearrange("p (k t) -> p k t", t=P)[:, :, 0:rows],
                                          mT[par][0][:, ks, 0:rows].bitcast(F32), ALU.subtract).then_inc(t_free.sem, 1)

                def norm_tile(n, par, i, rows=P):
                    dve.wait_ge(x_loaded[par], 16 * (i + 1))
                    dve.wait_ge(normed.sem, normed.done(n, back=1))
                    for c in range(2):
                        dve.wait_ge(y_full.sem, y_full.done(n, c))
                        cs = slice(c * 512, (c + 1) * 512)
                        dve.scalar_tensor_tensor(out=y[0:rows, cs], in0=xt[par][0:rows, cs], scalar=ALPHA, in1=ps_y[2 * par + c][0:rows, :],
                                                 op0=ALU.mult, op1=ALU.add).then_inc(y_free.sem, 1)
                    dve.wait_ge(y_free.sem, y_free.done(n, 1))
                    dve.wait_ge(stored[par], 16 * (i + 1))
                    layer_norm(nc, dve, link, t, rows, y[0:rows, :], ln_ready, rstd_ready, n, yn[par][0:rows, :], normed.sem)

                summed = Count(sem("summed"))
                def rest_of_weights(c):
                    cs = slice(c * 512, (c + 1) * 512)
                    dve.wait_ge(w_hi, c + 1)
                    dve.tensor_tensor(wo[1][:, :, cs], W[:, :, cs], wo[0][:, :, cs].bitcast(F32), ALU.subtract).then_inc(w_lo, 1)

                rest_of_weights(0)
                merge_tile(0, 0, 0)
                rest(0, 0)
                rest_of_weights(1)
                merge_tile(1, 1, 0)
                before = steps[0]
                per_pair = before + 2 * LN_LINKS
                with dve.Fori(0, NT // 2 - 1) as i:
                    base[0], steps[0] = i * per_pair + before, 0
                    for par in range(2):
                        rest(2 * i + par + 1, par ^ 1)
                        merge_tile(2 * i + par + 2, par, i + 1)
                        norm_tile(2 * i + par, par, i)
                    assert steps[0] == per_pair, (steps[0], per_pair)
                base[0], steps[0] = (NT // 2 - 1) * per_pair + before, 0
                for n in range(NT - 2, NT + 1):
                    if n < NT:
                        rest(n + 1, (n + 1) % 2, P if n + 1 < NT else NS)
                    norm_tile(n, n % 2, n // 2, P if n < NT else NS)


NTOK = SEQ + NS
NPAD = (NT + 1) * P
TOK_CHUNKS = [(0, 384), (384, 384), (768, 320)]
FG = 256
NFG = FF // FG
FT = FG // P


@own_semaphores
def mlp(nc, env, name, cfg):
    cst = env["cst"]
    ident = cst("ident")
    NTT = NT + 1
    UP, DN = FT * len(TOK_CHUNKS), 2 * NTT
    up_v = cfg["w_up"].rearrange("(k p) (j n) -> j p k n", p=P, n=FG)
    dn_v = cfg["w_down"].rearrange("(j f p) n -> j p f n", p=P, f=FT)
    with ExitStack() as ctx:
        def sb(nm, shape, dt=F32):
            return ctx.enter_context(nc.sbuf_tensor(f"{name}_{nm}", shape, dt))

        def ps(nm):
            return ctx.enter_context(nc.psum_tensor(f"{name}_{nm}", [P, 512], F32))

        def sem(nm):
            return env["sems"].enter_context(nc.semaphore(f"{name}_{nm}"))

        up_raw, dn_raw = sb("up_raw", [P, KT, FG]), sb("dn_raw", [P, FT, D])
        up = [sb(f"up_{x}", [P, KT, FG], F32R) for x in ("hi", "lo")]
        dn = [sb(f"dn_{x}", [P, FT, D], F32R) for x in ("hi", "lo")]
        xT = [sb(f"xT_{x}", [P, KT, NTOK], F32R) for x in ("hi", "lo")]
        acc = sb("acc", [P, NTT, D])
        hT = [[sb(f"hT{i}_{x}", [P, FT, NPAD], F32R) for x in ("hi", "lo")] for i in range(2)]
        h = [sb(f"h{i}", [P, 384]) for i in range(3)]
        yn = [dn_raw[:, 0, :], dn_raw[:, 1, :], sb("yn2", [P, D])]
        gb, bb = up_raw[:, 0:4, :].rearrange("p k n -> p (k n)"), up_raw[:, 4:8, :].rearrange("p k n -> p (k n)")
        t = [ln_tiles(lambda nm, shape, i=i: sb(f"{nm}{i}", shape)) for i in range(2)]
        ps_u = [ps(f"ps_u{i}") for i in range(4)]
        ps_d = [ps(f"ps_d{i}") for i in range(4)]
        x_loaded = [sem(f"x_loaded{i}") for i in range(2)]
        stored = [sem(f"stored{i}") for i in range(3)]
        up_loaded, dn_loaded = sem("up_loaded"), sem("dn_loaded")
        gb_loaded, step, cleared = sem("gb_loaded"), sem("step"), sem("cleared")
        t_full, t_free, x_split, scaled = sem("t_full"), sem("t_free"), sem("x_split"), sem("scaled")
        up_hi, up_lo, dn_hi, dn_lo = (Count(sem(x)) for x in ("up_hi", "up_lo", "dn_hi", "dn_lo"))
        u_full, relu_done, squared = Count(sem("u_full"), UP), Count(sem("relu_done"), UP, credit=3), Count(sem("squared"), UP)
        h_hi, h_lo = Count(sem("h_hi"), UP), Count(sem("h_lo"), UP, credit=3)
        d_full, d_free = Count(sem("d_full"), DN), Count(sem("d_free"), DN, credit=4)
        ln_ready, log_done, rstd_ready, normed, gained, out_ready = (
            Count(sem(x)) for x in ("ln_ready", "log_done", "rstd_ready", "normed", "gained", "out_ready"))

        def rows_of(n):
            return P if n < NT else NS

        def as32(ap):
            return ap.bitcast(F32)

        with nc.Block() as block:
            @block.sync
            def _(sp):
                def load_up(n):
                    sp.dma_start(up_raw[:, :, :], up_v[n]).then_inc(up_loaded, 16)

                def load_dn(n):
                    sp.dma_start(dn_raw[:, :, :], dn_v[n]).then_inc(dn_loaded, 16)

                for n in range(NTT):
                    if n >= 2:
                        sp.wait_ge(t_full, 2 * n - 2)
                        sp.wait_ge(scaled, n - 1)
                    sp.dma_start(yn[n % 2][0:rows_of(n), :], cfg["x"][n * P:n * P + rows_of(n), :]).then_inc(x_loaded[n % 2], 16)
                    if n == 1:
                        load_up(0)
                sp.wait_ge(t_full, 2 * NTT)
                sp.wait_ge(scaled, NTT)
                load_dn(0)
                with sp.Fori(0, NFG - 1) as i:
                    sp.wait_ge(up_lo.sem, up_lo.done(i))
                    load_up(i + 1)
                    sp.wait_ge(dn_lo.sem, dn_lo.done(i))
                    load_dn(i + 1)
                sp.wait_ge(up_lo.sem, up_lo.done(NFG - 1))
                sp.dma_start(gb, cfg["g"].to_broadcast([P, D])).then_inc(gb_loaded, 16)
                sp.dma_start(bb, cfg["b"].to_broadcast([P, D])).then_inc(gb_loaded, 16)
                for n in range(NTT):
                    sp.wait_ge(out_ready.sem, out_ready.done(n))
                    sp.dma_start(cfg["out"](n), yn[n % 3][0:rows_of(n), :]).then_inc(stored[n % 3], 16)
                for slot in range(3):
                    sp.wait_ge(stored[slot], 16 * len(range(slot, NTT, 3)))

            @block.tensor
            def _(pe):
                for n in range(NTT):
                    rows = rows_of(n)
                    pe.wait_ge(x_loaded[n % 2], 16 * (n // 2 + 1))
                    for half in range(2):
                        if n >= 2:
                            pe.wait_ge(x_split, 2 * (n - 2) + half + 1)
                        for j in range(4):
                            c = (4 * half + j) * P
                            last = pe.transpose(ps_u[2 * (n % 2) + half][:, j * P:j * P + rows], yn[n % 2][0:rows, c:c + P], ident[0:rows, 0:rows])
                        last.then_inc(t_full, 1)
                pe.wait_ge(x_split, 2 * NTT)

                def hidden(n):
                    pe.wait_ge(up_lo.sem, up_lo.done(n))
                    for f in range(FT):
                        for c, (t0, w) in enumerate(TOK_CHUNKS):
                            b = f * len(TOK_CHUNKS) + c
                            bank = ps_u[b % 3]
                            pe.wait_ge(relu_done.sem, relu_done.done(n, b, back=3))
                            for k in range(KT):
                                for q, (wp, xp) in enumerate(split_passes((up[0], xT[0]), (up[1], xT[1]))):
                                    last = pe.matmul(bank[:, 0:w], wp[:, k, f * P:(f + 1) * P], xp[:, k, t0:t0 + w],
                                                     start=(k == 0 and q == 0), stop=(k == KT - 1 and q == 2))
                            last.then_inc(u_full.sem, 1)

                def down(n, par):
                    pe.wait_ge(dn_lo.sem, dn_lo.done(n))
                    pe.wait_ge(h_lo.sem, h_lo.done(n, UP - 1))
                    for m in range(NTT):
                        for c in range(2):
                            b = 2 * m + c
                            pe.wait_ge(d_free.sem, d_free.done(n, b, back=4))
                            for f in range(FT):
                                for q, (hp, wp) in enumerate(split_passes((hT[par][0], dn[0]), (hT[par][1], dn[1]))):
                                    last = pe.matmul(ps_d[(par * DN + b) % 4][:, :], hp[:, f, m * P:(m + 1) * P],
                                                     wp[:, f, c * 512:(c + 1) * 512], start=(f == 0 and q == 0),
                                                     stop=(f == FT - 1 and q == 2))
                            last.then_inc(d_full.sem, 1)

                hidden(0)
                pe.wait_ge(cleared, 1)
                with pe.Fori(0, NFG // 2 - 1) as i:
                    for par in range(2):
                        hidden(2 * i + par + 1)
                        down(2 * i + par, par)
                hidden(NFG - 1)
                down(NFG - 2, 0)
                down(NFG - 1, 1)

            @block.scalar
            def _(act):
                def split_weights(n, raw, hi, loaded, used, ready):
                    act.wait_ge(loaded, 16 * (n + 1))
                    if used is not None:
                        act.wait_ge(*used)
                    nc.scalar.copy(hi[:, :, :].rearrange("p k n -> p (k n)"), raw[:, :, :].rearrange("p k n -> p (k n)"))\
                        .then_inc(ready.sem, 1)

                for n in range(NTT):
                    rows = rows_of(n)
                    for half in range(2):
                        act.wait_ge(t_full, 2 * n + half + 1)
                        nc.scalar.copy(xT[0][:, 4 * half:4 * half + 4, n * P:n * P + rows],
                                       ps_u[2 * (n % 2) + half][:, :].rearrange("p (k t) -> p k t", t=P)[:, :, 0:rows]).then_inc(t_free, 1)
                    if n == 2:
                        split_weights(0, up_raw, up[0], up_loaded, None, up_hi)
                split_weights(0, dn_raw, dn[0], dn_loaded, None, dn_hi)

                def step_(n, par, last=False):
                    for b in range(UP + 1):
                        if b < UP:
                            f, (t0, w) = b // len(TOK_CHUNKS), TOK_CHUNKS[b % len(TOK_CHUNKS)]
                            act.wait_ge(u_full.sem, u_full.done(n, b))
                            act.wait_ge(h_lo.sem, h_lo.done(n, b, back=3))
                            nc.scalar.activation(h[(par * UP + b) % 3][:, 0:w], ps_u[b % 3][:, 0:w], ACT.Relu)\
                                .then_inc(relu_done.sem, 1)
                        if b >= 1:
                            f, (t0, w) = (b - 1) // len(TOK_CHUNKS), TOK_CHUNKS[(b - 1) % len(TOK_CHUNKS)]
                            act.wait_ge(squared.sem, squared.done(n, b - 1))
                            nc.scalar.copy(hT[par][0][:, f, t0:t0 + w], h[(par * UP + b - 1) % 3][:, 0:w]).then_inc(h_hi.sem, 1)
                    if not last:
                        split_weights(n + 1, up_raw, up[0], up_loaded, (u_full.sem, u_full.done(n, UP - 1)), up_hi)

                def next_down(n):
                    split_weights(n + 1, dn_raw, dn[0], dn_loaded, (d_full.sem, d_full.done(n, DN - 1)), dn_hi)

                step_(0, 0)
                with act.Fori(0, NFG // 2 - 1) as i:
                    for par in range(2):
                        step_(2 * i + par + 1, par ^ 1)
                        next_down(2 * i + par)
                step_(NFG - 1, 1, last=True)
                next_down(NFG - 2)
                for n in range(NTT):
                    root(nc, act, t[n % 2], rows_of(n), ln_ready, log_done, rstd_ready, n)

            @block.gpsimd
            def _(pool):
                pool.sem_inc(relu_done.sem, 3)
                pool.sem_inc(d_free.sem, 4)
                pool.sem_inc(h_lo.sem, 3)
                for par in range(2):
                    for part in range(2):
                        last = pool.memset(hT[par][part][:, :, NTOK:NPAD].bitcast(F32), 0.0)
                last.then_inc(cleared, 1)
                with pool.Fori(0, NFG // 2) as i:
                    for par in range(2):
                        n = 2 * i + par
                        for b in range(UP):
                            w = TOK_CHUNKS[b % len(TOK_CHUNKS)][1]
                            hs = h[(par * UP + b) % 3][:, 0:w]
                            pool.wait_ge(relu_done.sem, relu_done.done(n, b))
                            pool.tensor_tensor(hs, hs, hs, ALU.mult).then_inc(squared.sem, 1)
                pool.wait_ge(gb_loaded, 32)
                for n in range(NTT - 1):
                    o = yn[n % 3][0:rows_of(n), :]
                    pool.wait_ge(normed.sem, normed.done(n))
                    pool.tensor_tensor(o, o, gb[0:rows_of(n), :], ALU.mult).then_inc(gained.sem, 1)
                    pool.wait_ge(gained.sem, gained.done(n))
                    pool.tensor_tensor(o, o, bb[0:rows_of(n), :], ALU.add).then_inc(out_ready.sem, 1)

            @block.vector
            def _(dve):
                steps = [0]

                def link(ins):
                    steps[0] += 1
                    ins.then_inc(step, 1)
                    dve.wait_ge(step, steps[0])

                def rest(n, raw, parts, hi, lo):
                    dve.wait_ge(hi.sem, hi.done(n))
                    dve.tensor_tensor(parts[1][:, :, :], raw[:, :, :], as32(parts[0][:, :, :]), ALU.subtract).then_inc(lo.sem, 1)

                for n in range(NTT):
                    rows = rows_of(n)
                    dve.wait_ge(x_loaded[n % 2], 16 * (n // 2 + 1))
                    dve.tensor_scalar(acc[0:rows, n, :], yn[n % 2][0:rows, :], ALPHA, None, ALU.mult).then_inc(scaled, 1)
                    for half in range(2):
                        dve.wait_ge(t_free, 2 * n + half + 1)
                        dst = slice(4 * half, 4 * half + 4), slice(n * P, n * P + rows)
                        dve.tensor_tensor(xT[1][:, dst[0], dst[1]],
                                          ps_u[2 * (n % 2) + half][:, :].rearrange("p (k t) -> p k t", t=P)[:, :, 0:rows],
                                          as32(xT[0][:, dst[0], dst[1]]), ALU.subtract).then_inc(x_split, 1)
                    if n == 2:
                        rest(0, up_raw, up, up_hi, up_lo)
                rest(0, dn_raw, dn, dn_hi, dn_lo)
                dve.wait_ge(scaled, NTT)

                def hidden_rest(n, par, b):
                    f, (t0, w) = b // len(TOK_CHUNKS), TOK_CHUNKS[b % len(TOK_CHUNKS)]
                    dve.wait_ge(h_hi.sem, h_hi.done(n, b))
                    dve.tensor_tensor(hT[par][1][:, f, t0:t0 + w], h[(par * UP + b) % 3][:, 0:w],
                                      as32(hT[par][0][:, f, t0:t0 + w]), ALU.subtract).then_inc(h_lo.sem, 1)

                def add(n, par, m):
                    rows = rows_of(m)
                    for c in range(2):
                        b = 2 * m + c
                        dve.wait_ge(d_full.sem, d_full.done(n, b))
                        a = acc[0:rows, m, c * 512:(c + 1) * 512]
                        dve.tensor_tensor(a, a, ps_d[(par * DN + b) % 4][0:rows, :], ALU.add).then_inc(d_free.sem, 1)

                def hiddens(n, par, last=False):
                    for b in range(UP):
                        hidden_rest(n, par, b)
                    if not last:
                        rest(n + 1, up_raw, up, up_hi, up_lo)

                def adds(n, par):
                    dve.wait_ge(d_free.sem, d_free.done(n, 0, back=1))
                    for m in range(NTT):
                        add(n, par, m)

                def finish(m):
                    rows = rows_of(m)
                    if m >= 3:
                        dve.wait_ge(stored[m % 3], 16 * (m // 3))
                    normalise(dve, link, t[m % 2], rows, acc[0:rows, m, :], rstd_ready, m, yn[m % 3][0:rows, :], normed.sem)

                hiddens(0, 0)
                with dve.Fori(0, NFG // 2 - 1) as i:
                    for par in range(2):
                        hiddens(2 * i + par + 1, par ^ 1)
                        adds(2 * i + par, par)
                        rest(2 * i + par + 1, dn_raw, dn, dn_hi, dn_lo)
                hiddens(NFG - 1, 1, last=True)
                adds(NFG - 2, 0)
                rest(NFG - 1, dn_raw, dn, dn_hi, dn_lo)
                dve.wait_ge(d_free.sem, d_free.done(NFG - 1, 0, back=1))
                for m in range(NTT):
                    add(NFG - 1, 1, m)
                    dve.wait_ge(d_free.sem, d_free.done(NFG - 1, 2 * m + 1))
                    moments(dve, link, t[m % 2], rows_of(m), acc[0:rows_of(m), m, :], ln_ready)
                    if m >= 1:
                        finish(m - 1)
                finish(NTT - 1)
                o = yn[(NTT - 1) % 3][0:NS, :]
                dve.wait_ge(gb_loaded, 32)
                dve.wait_ge(normed.sem, normed.done(NTT - 1))
                link(dve.tensor_tensor(o, o, gb[0:NS, :], ALU.mult))
                dve.wait_ge(out_ready.sem, out_ready.done(NTT - 2))
                dve.tensor_tensor(o, o, bb[0:NS, :], ALU.add).then_inc(out_ready.sem, 1)


def program(nc, a, o):
    with ExitStack() as ctx:
        def dram(nm, shape):
            return nc.dram_tensor(nm, shape, F32, kind="Internal").ap()

        def sem(nm):
            return ctx.enter_context(nc.semaphore(nm))

        consts = ctx.enter_context(nc.sbuf_tensor("consts", [P, RESIDENT], F32))
        front = ctx.enter_context(ExitStack())
        w_group = front.enter_context(nc.sbuf_tensor("w_group", [P, KT, 2 * WB], F32))
        m_stack = front.enter_context(ExitStack())
        w_m = m_stack.enter_context(nc.sbuf_tensor("w_m", [P, KT, 4 * WA + 2 * HA], F32))

        def cst(nm, DRAM=False):
            c0, w = CONST_AT[nm]
            return (a["const"] if DRAM else consts)[:, c0:c0 + w]

        og = [dram(f"og{g}", (SEQ, SROW)) for g in range(NG)]
        zs = dram("zs", (NS, 3 * NG * WB))
        mix = dram("mix", (SEQ + NS, D))
        xp = a["x_prompt"][0]
        xs = a["x_sample"].rearrange("b t d -> (b t) d")
        w_in = a["w_in_ab"][0]
        const_loaded = sem("const_loaded")
        copied = sem("copied")
        env = {"cst": cst, "const": a["const"], "sems": ctx, "const_loaded": const_loaded}
        w_sems = {}

        def load_chunk(eng, dst, c, name, ranges, src):
            if name not in w_sems:
                w_sems[name] = [sem(f"w_{name}{i}") for i in range(len(ranges))]
            c0, width = ranges[c]
            eng.dma_start(dst, src.rearrange("(k p) n -> p k n", p=P)[:, :, c0:c0 + width]).then_inc(w_sems[name][c], 16)

        def load_staged(eng, slots, chunks, name, ranges, src):
            for c in chunks:
                load_chunk(eng, slots[:, :, c % 2 * 512:c % 2 * 512 + ranges[c][1]], c, name, ranges, src)

        def load_group(eng, g, chunks):
            load_staged(eng, w_group, chunks, f"g{g}", group_ranges(g), w_in)

        def load_m(eng, chunks):
            for c in chunks:
                load_chunk(eng, w_m[:, :, c * WA:c * WA + m_ranges[c][1]], c, "m", m_ranges, w_in)

        def group_ranges(g):
            return [(QB0 + j * NG * WB + g * WB, WB) for j in range(3)]

        m_ranges = [(j * WA, WA) for j in range(4)] + [(4 * WA, 2 * HA)]
        w_sems["m"] = [sem(f"w_m{c}") for c in range(len(m_ranges))]
        mlstm(nc, env, dict(
            x=xp, xs=xs, w=w_m, w_sems=w_sems["m"], bias=a["b_gate_ab"][0:1, :], out=mix,
            C_p=o[2][0, 0], C_s=o[3][0], n_p=o[4][0, 0], n_s=o[5][0], m_p=o[6][0, 0], m_s=o[7][0],
            C0=a["state_mlstm_C"][0], n0=a["state_mlstm_n"][0], m0=a["state_mlstm_m"][0],
            load_consts=lambda sp: sp.dma_start(consts[:, :], a["const"][:, 0:RESIDENT]).then_inc(const_loaded, 16),
            load_weights=load_m, prefetch=lambda sp: load_group(sp, 0, (0, 1))))
        m_stack.close()

        def dilated(g):
            cache_in, out_p, out_s = a[f"cache_dil{g + 1}_kv"][0], o[8 + 2 * g][0, 0], o[9 + 2 * g][0]
            keep, rate = KEEP_P[g], RATES[g]
            out_rows = out_p.rearrange("s two h d -> s two (h d)")

            def kv_rows(i, par, which):
                if rate == 1:
                    return [out_rows[:, which, :]]
                if rate == 4:
                    return [out_rows.rearrange("(p j) two c -> j two p c", j=4)[i, which]]
                v = out_rows.rearrange("(p j four) two c -> four j two p c", j=4, four=4)
                return [v[2 * par, i, which], v[2 * par + 1, i, which]]

            def spread(sp, i, par):
                old = CACHE[g]
                kept = KEEP_S[g] - TD
                src = cache_in.rearrange("(b two) s x h d -> two b s (x h d)", two=2)[par, i, old - kept:old, :]
                dst = out_s.rearrange("(b two) s x h d -> two b s (x h d)", two=2)[par, i, 0:kept, :]
                sp.dma_start(dst, src).then_inc(copied, 16)

            def store_sample(sp, z, s):
                sp.dma_start(zs.rearrange("t (j g c) -> t j g c", j=3, g=NG)[:, :, g, :],
                             z[0:NS, :].rearrange("t (j c) -> t j c", j=3)).then_inc(s, 16)

            def copy_sample(sp):
                src = zs.rearrange("(b t) (j g c) -> j g b t c", t=TD, j=3, g=NG)
                dst = out_s.rearrange("b s x h d -> x b s (h d)")
                for j in (1, 2):
                    sp.dma_start(dst[j - 1, :, KEEP_S[g] - TD:KEEP_S[g], :], src[j, g]).then_inc(copied, 16)

            def prefetch(sp):
                if g + 1 < NG:
                    load_group(sp, g + 1, (0, 1))

            attention(nc, env, f"g{g}", dict(
                heads=HB, widths=[WB] * 3, qw=WB, kw=WB, prev=rate < 16, rate=rate, sinks=None, x=xp, xs=xs,
                w=w_group, w_sems=w_sems[f"g{g}"], mask="m_pair" if rate == 16 else "m_dil",
                mask_even_after=rate == 1, rope=a["rope"][g], out=og[g], out_norm=False,
                kv_tiles=("last", "odd", "all")[g], kv_rows=kv_rows, spread=spread, store_sample=store_sample, copy_sample=copy_sample,
                load_chunks=lambda sp, chunks: load_group(sp, g, chunks), prefetch=prefetch))

        for g in range(NG):
            dilated(g)
        front.close()

        x_mid = [dram(f"x_mid{i}", (SEQ + NS, D)) for i in range(3)]
        zs_c = dram("zs_c", (NS, (HC + 2 * KVC) * DH))
        mix_c = dram("mix_c", (SEQ + NS, D))

        def after_mixing(layer, mixing, x_in, x_in_s, mix_in, og_in):
            with ExitStack() as inner:
                wo = inner.enter_context(nc.sbuf_tensor(f"wo{layer}", [P, KT, D], F32))
                wo_sem = sem(f"wo_loaded{layer}")
                w_o = a[("w_out_ab", "w_out_c")[layer]][0]

                def prefetch_wo(sp):
                    sp.dma_start(wo[:, :, :], w_o.rearrange("(k p) n -> p k n", p=P)).then_inc(wo_sem, 16)

                mixing(prefetch_wo)
                output_projection(nc, env, f"p{layer}", dict(
                    merge=layer == 0, w=wo, w_sem=wo_sem, x=x_in, xs=x_in_s, mix=mix_in, og=og_in, out=x_mid[2 * layer],
                    g=a["ln1_g"][layer:layer + 1, :], b=a["ln1_b"][layer:layer + 1, :]))
            if layer == 0:
                def out(n):
                    return x_mid[1][n * P:n * P + (P if n < NT else NS), :]
            else:
                def out(n):
                    return o[0][0, n * P:(n + 1) * P, :] if n < NT else o[1].rearrange("b t d -> (b t) d")
            mlp(nc, env, f"f{layer}", dict(x=x_mid[2 * layer], w_up=a["w_up"][layer], w_down=a["w_down"][layer], out=out,
                                          g=a["ln2_g"][layer:layer + 1, :], b=a["ln2_b"][layer:layer + 1, :]))

        def sample_dilated(prefetch_wo):
            sample_attention(nc, env, dict(
                caches=[a[f"cache_dil{g + 1}_kv"][0] for g in range(NG)], zs=zs, out=mix[SEQ:SEQ + NS, WA:D],
                prefetch=prefetch_wo))

        def windowed():
            out_p = o[14][0, 0].rearrange("s x h d -> s x (h d)")
            out_s = o[15][0].rearrange("b s x h d -> b s (x h d)")
            cache = a["cache_swa_kv"][0]
            def spread(sp, i, par):
                v = cache.rearrange("(b two) s x h d -> two b s (x h d)", two=2)
                sp.dma_start(out_s.rearrange("(b two) s c -> two b s c", two=2)[par, i, 0:P - TD, :], v[par, i, TD:P, :])\
                    .then_inc(copied, 16)

            def store_sample(sp, z, s):
                sp.dma_start(zs_c, z[0:NS, 0:(HC + 2 * KVC) * DH]).then_inc(s, 16)

            def copy_sample(sp):
                sp.dma_start(out_s[:, P - TD:P, :], zs_c.rearrange("(b t) c -> b t c", t=TD)[:, :, HC * DH:(HC + 2 * KVC) * DH])\
                    .then_inc(copied, 16)

            with nc.sbuf_tensor("w_c", [P, KT, 2 * 512], F32) as w_c:
                c_ranges = [(0, 512), (512, 512), (1024, 256)]
                w_sems["c"] = [sem(f"w_c{c}") for c in range(len(c_ranges))]
                attention(nc, env, "c", dict(
                    heads=HC, widths=[512, 512, 256], qw=HC * DH, kw=KVC * DH, prev=True, rate=1, sinks=a["sinks_c"][0:1, :],
                    x=x_mid[1][0:SEQ, :], xs=x_mid[1][SEQ:SEQ + NS, :], w=w_c, w_sems=w_sems["c"],
                    load_chunks=lambda sp, chunks: load_staged(sp, w_c, chunks, "c", c_ranges, a["w_in_c"][0]), mask="m_swa",
                    mask_even_after=True, rope=a["rope"][0], out=mix_c[0:SEQ, :], out_norm=True, kv_tiles="last",
                    kv_rows=lambda i, par, which: [out_p[:, which, :]], spread=spread, store_sample=store_sample, copy_sample=copy_sample,
                    prefetch=lambda sp: None))

        def sample_windowed(prefetch_wo):
            swa_sample(nc, env, dict(cache=a["cache_swa_kv"][0], zs=zs_c, out=mix_c[SEQ:SEQ + NS, :],
                                     sinks=a["sinks_c"][0:1, :], prefetch=prefetch_wo))

        after_mixing(0, sample_dilated, xp, xs, mix, og)
        windowed()
        after_mixing(1, sample_windowed, x_mid[1][0:SEQ, :], x_mid[1][SEQ:SEQ + NS, :], mix_c, None)

        with nc.Block() as block:
            @block.sync
            def _(sp):
                sp.wait_ge(copied, 16 * ((NG + 1) * BD + 2 * NG + 1))


OUTS = [(1, SEQ, D), (BD, TD, D), (1, 1, HA, DA, DA), (1, BD, HA, DA, DA), (1, 1, HA, DA), (1, BD, HA, DA), (1, 1, HA),
        (1, BD, HA)]
for _g in range(NG):
    OUTS += [(1, 1, KEEP_P[_g], 2, HB, DH), (1, BD, KEEP_S[_g], 2, HB, DH)]
OUTS += [(1, 1, P, 2, KVC, DH), (1, BD, P, 2, KVC, DH)]
INS = ["x_prompt", "x_sample", "state_mlstm_C", "state_mlstm_n", "state_mlstm_m", "cache_dil1_kv", "cache_dil2_kv",
       "cache_dil3_kv", "cache_swa_kv", "w_in_ab", "b_gate_ab", "w_out_ab", "w_in_c", "sinks_c", "w_out_c",
       "ln1_g", "ln1_b", "ln2_g", "ln2_b", "w_up", "w_down"]


def kernel(**inputs):
    import concourse.bacc as bacc
    from concourse.bass_utils import run_bass_kernel_spmd

    nc = bacc.Bacc("TRN2", target_bir_lowering=False, num_devices=1)
    arrays = {n: np.ascontiguousarray(inputs[n]) for n in INS}
    arrays["const"] = CONST
    arrays["rope"] = ROPE
    a = {n: nc.dram_tensor(f"in_{n}", v.shape, F32, kind="ExternalInput").ap() for n, v in arrays.items()}
    o = [nc.dram_tensor(f"out_{i}", s, F32, kind="ExternalOutput").ap() for i, s in enumerate(OUTS)]
    program(nc, a, o)
    r = run_bass_kernel_spmd(nc, [{f"in_{n}": v for n, v in arrays.items()}], core_ids=[0])
    return tuple(r.results[0][f"out_{i}"] for i in range(len(OUTS)))
```
